# Optimizing a Trainium2 kernel written in Bass

```python
import math, functools
import jax, jax.numpy as jnp
from jax import lax
import numpy as np

D_MODEL = 1024
BATCH = 1
SEQ = 1024
DEPTH = 1
DEC_BATCH = 8
DEC_SEQ = 1
PAST_LEN = 4096
PAGE_SIZE = 128

MEM_LEN = 256
CONV_CH = 512
CONV_WIDTH = 31
SWA_HEADS = 8
SWA_KV_HEADS = 2
SWA_GROUP = SWA_HEADS // SWA_KV_HEADS
SWA_HEAD_DIM = 64
WINDOW = 128
BLOCK = WINDOW
SWA_SCALE = SWA_HEAD_DIM ** -0.5
MEM_HEADS = 4
MEM_HEAD_DIM = 128
MEM_SCALE = MEM_HEAD_DIM ** -0.5
REL_BUCKETS = 32
REL_MAX_DIST = 128
PEER_HEADS = 8
PEER_N_KEYS = 128
PEER_N_EXPERTS = PEER_N_KEYS * PEER_N_KEYS
PEER_DK = 128
PEER_DK_HALF = PEER_DK // 2
PEER_TOPK = 16
PEER_BLOCK = 128
N_BRANCH = 3
EPS = 1e-6
NEG_INF = -1e30

W_GLU = 2 * CONV_CH
W_Q = SWA_HEADS * SWA_HEAD_DIM
W_KV = SWA_KV_HEADS * SWA_HEAD_DIM
W_QM = MEM_HEADS * MEM_HEAD_DIM
W_GATE = N_BRANCH * D_MODEL
IN_COLS = W_GLU + W_Q + 2 * W_KV + W_QM + W_GATE
IN_SPLITS = (W_GLU, W_GLU + W_Q, W_GLU + W_Q + W_KV, W_GLU + W_Q + 2 * W_KV, W_GLU + W_Q + 2 * W_KV + W_QM)

kernel_name = 'hybrid_conv_swa_mem_peer_decode_step'

def rmsnorm(x, g):
    xf = x.astype(jnp.float32)
    y = xf * lax.rsqrt(jnp.mean(xf * xf, axis=-1, keepdims=True) + EPS)
    return (y * g.astype(jnp.float32)).astype(x.dtype)

def layernorm(x, g, b):
    xf = x.astype(jnp.float32)
    mu = jnp.mean(xf, axis=-1, keepdims=True)
    var = jnp.mean(jnp.square(xf - mu), axis=-1, keepdims=True)
    y = (xf - mu) * lax.rsqrt(var + EPS)
    return (y * g.astype(jnp.float32) + b.astype(jnp.float32)).astype(x.dtype)

def rel_bucket(dist):
    n = jnp.maximum(dist, 0)
    max_exact = REL_BUCKETS // 2
    nf = jnp.maximum(n, 1).astype(jnp.float32)
    large = max_exact + (jnp.log(nf / max_exact) / math.log(REL_MAX_DIST / max_exact) * (REL_BUCKETS - max_exact)).astype(jnp.int32)
    large = jnp.minimum(large, REL_BUCKETS - 1)
    return jnp.where(n < max_exact, n, large)

def rel_bias(dist, table):
    b = jnp.moveaxis(table[rel_bucket(dist)], -1, 0).astype(jnp.float32)
    return b.reshape(SWA_KV_HEADS, SWA_GROUP, *dist.shape)

def sink_softmax(s, mask, sinks):
    sink = sinks.astype(jnp.float32).reshape(SWA_KV_HEADS, SWA_GROUP, 1, 1)
    s = jnp.where(mask, s, NEG_INF)
    m = jnp.maximum(jnp.max(s, axis=-1, keepdims=True), sink)
    p = jnp.exp(s - m)
    return p / (jnp.sum(p, axis=-1, keepdims=True) + jnp.exp(sink - m))

def conformer_conv(u, buf, dw_w, dw_b, ln_g, ln_b, w_pw):
    full = jnp.concatenate([buf.astype(u.dtype), u], axis=1)
    y = lax.conv_general_dilated(full, dw_w[:, None, :].astype(u.dtype), window_strides=(1,), padding='VALID',
                                 dimension_numbers=('NWC', 'WIO', 'NWC'), feature_group_count=CONV_CH) + dw_b
    y = jax.nn.silu(layernorm(y, ln_g, ln_b))
    return y @ w_pw, full[:, -(CONV_WIDTH - 1):]

def swa_prompt(q, k, v, sinks, table):
    n, s = q.shape[0], q.shape[1]
    nb = s // BLOCK
    qb = q.reshape(n, nb, BLOCK, SWA_KV_HEADS, SWA_GROUP, SWA_HEAD_DIM)
    kb = k.reshape(n, nb, BLOCK, SWA_KV_HEADS, SWA_HEAD_DIM)
    vb = v.reshape(n, nb, BLOCK, SWA_KV_HEADS, SWA_HEAD_DIM)
    pad = ((0, 0), (1, 0), (0, 0), (0, 0), (0, 0))
    kk = jnp.concatenate([jnp.pad(kb[:, :-1], pad), kb], axis=2)
    vv = jnp.concatenate([jnp.pad(vb[:, :-1], pad), vb], axis=2)
    qi = jnp.arange(BLOCK)[:, None]
    ki = jnp.arange(2 * BLOCK)[None, :]
    dist = BLOCK + qi - ki
    band = (dist >= 0) & (dist <= WINDOW)
    has_prev = (jnp.arange(nb) > 0)[:, None, None] | (ki >= BLOCK)[None]
    mask = (band[None] & has_prev)[None, :, None, None]
    sc = jnp.einsum('bnqhgd,bnkhd->bnhgqk', qb, kk, preferred_element_type=jnp.float32) * SWA_SCALE + rel_bias(dist, table)
    p = sink_softmax(sc, mask, sinks)
    o = jnp.einsum('bnhgqk,bnkhd->bnqhgd', p.astype(v.dtype), vv)
    return o.reshape(n, s, SWA_HEADS * SWA_HEAD_DIM), k[:, -WINDOW:], v[:, -WINDOW:]

def swa_sample(q, k, v, cache_k, cache_v, sinks, table):
    n, L = q.shape[0], q.shape[1]
    kk = jnp.concatenate([cache_k.astype(k.dtype), k], axis=1)
    vv = jnp.concatenate([cache_v.astype(v.dtype), v], axis=1)
    qpos = PAST_LEN + jnp.arange(L)
    kpos = PAST_LEN - WINDOW + jnp.arange(WINDOW + L)
    dist = qpos[:, None] - kpos[None, :]
    mask = (dist >= 0) & (dist <= WINDOW)
    qg = q.reshape(n, L, SWA_KV_HEADS, SWA_GROUP, SWA_HEAD_DIM)
    sc = jnp.einsum('bqhgd,bkhd->bhgqk', qg, kk, preferred_element_type=jnp.float32) * SWA_SCALE + rel_bias(dist, table)
    p = sink_softmax(sc, mask, sinks)
    o = jnp.einsum('bhgqk,bkhd->bqhgd', p.astype(v.dtype), vv)
    return o.reshape(n, L, SWA_HEADS * SWA_HEAD_DIM), kk[:, L:], vv[:, L:]

def mem_attend(q, mk, mv):
    s = jnp.einsum('blhd,bmhd->bhlm', q, mk.astype(q.dtype), preferred_element_type=jnp.float32) * MEM_SCALE
    w = jax.nn.softmax(s, axis=-1)
    o = jnp.einsum('bhlm,bmhd->blhd', w.astype(q.dtype), mv.astype(q.dtype))
    return o.reshape(q.shape[0], q.shape[1], MEM_HEADS * MEM_HEAD_DIM)

def peer_ffn(h, w_q, keys, w_down, w_up):
    shape = h.shape
    t = h.reshape(-1, D_MODEL)
    T = t.shape[0]
    nblk = -(-T // PEER_BLOCK)
    t = jnp.pad(t, ((0, nblk * PEER_BLOCK - T), (0, 0))).reshape(nblk, PEER_BLOCK, D_MODEL)

    def one_block(xb):
        q = (xb @ w_q).reshape(PEER_BLOCK, PEER_HEADS, 2, PEER_DK_HALF)
        s = jnp.einsum('thcd,hcnd->thcn', q, keys, preferred_element_type=jnp.float32)
        sv, si = lax.top_k(s, PEER_TOPK)
        cand = (sv[:, :, 0, :, None] + sv[:, :, 1, None, :]).reshape(PEER_BLOCK, PEER_HEADS, PEER_TOPK * PEER_TOPK)
        cv, ci = lax.top_k(cand, PEER_TOPK)
        i0 = jnp.take_along_axis(si[:, :, 0], ci // PEER_TOPK, axis=-1)
        i1 = jnp.take_along_axis(si[:, :, 1], ci % PEER_TOPK, axis=-1)
        eid = i0 * PEER_N_KEYS + i1
        gate = jax.nn.softmax(cv, axis=-1)
        u = w_down[eid]
        act = jax.nn.gelu(jnp.einsum('td,thkd->thk', xb, u, preferred_element_type=jnp.float32), approximate=False)
        return jnp.einsum('thk,thkd->td', (gate * act).astype(xb.dtype), w_up[eid])

    out = lax.map(one_block, t).reshape(-1, D_MODEL)[:T]
    return out.reshape(shape)

def decoder_layer(x, conv_buf, attn_fn, mem_k, mem_v, norm1_g, w_in, conv_dw_w, conv_dw_b, conv_ln_g, conv_ln_b,
                  w_conv_out, w_swa_out, w_mem_out, w_out, norm2_g, peer_w_q, peer_keys, peer_w_down, peer_w_up):
    n, L = x.shape[0], x.shape[1]
    h = rmsnorm(x, norm1_g)
    z_glu, q, k, v, qm, gate_logits = jnp.split(h @ w_in, IN_SPLITS, axis=-1)
    a, b = jnp.split(z_glu, 2, axis=-1)
    conv_y, new_conv = conformer_conv(a * jax.nn.sigmoid(b), conv_buf, conv_dw_w, conv_dw_b, conv_ln_g, conv_ln_b, w_conv_out)
    swa_o, new_k, new_v = attn_fn(q.reshape(n, L, SWA_HEADS, SWA_HEAD_DIM),
                                  k.reshape(n, L, SWA_KV_HEADS, SWA_HEAD_DIM),
                                  v.reshape(n, L, SWA_KV_HEADS, SWA_HEAD_DIM))
    mem_o = mem_attend(qm.reshape(n, L, MEM_HEADS, MEM_HEAD_DIM), mem_k, mem_v)
    g_conv, g_swa, g_mem = jnp.split(jax.nn.sigmoid(gate_logits), N_BRANCH, axis=-1)
    merged = g_conv * conv_y + g_swa * (swa_o @ w_swa_out) + g_mem * (mem_o @ w_mem_out)
    x = x + merged @ w_out
    x = x + peer_ffn(rmsnorm(x, norm2_g), peer_w_q, peer_keys, peer_w_down, peer_w_up)
    return x, new_conv, new_k, new_v

def setup_inputs(seed: int = 0) -> dict:
    key = jax.random.key(seed)
    ks = jax.random.split(key, 32)
    f32 = jnp.float32

    def nrm(k, shape, scale):
        return jax.random.normal(k, shape, f32) * scale

    def gain(k, shape):
        return 1.0 + 0.05 * jax.random.normal(k, shape, f32)

    return {
        'x_prompt': nrm(ks[0], (BATCH, SEQ, D_MODEL), 1.0),
        'x_sample': nrm(ks[1], (DEC_BATCH, DEC_SEQ, D_MODEL), 1.0),
        'cache_conv': nrm(ks[2], (DEPTH, DEC_BATCH, CONV_WIDTH - 1, CONV_CH), 0.5),
        'cache_swa_k': nrm(ks[3], (DEPTH, DEC_BATCH, WINDOW, SWA_KV_HEADS, SWA_HEAD_DIM), 1.0),
        'cache_swa_v': nrm(ks[4], (DEPTH, DEC_BATCH, WINDOW, SWA_KV_HEADS, SWA_HEAD_DIM), 1.0),
        'cache_mem_k': nrm(ks[5], (DEPTH, DEC_BATCH, MEM_LEN, MEM_HEADS, MEM_HEAD_DIM), 1.0),
        'cache_mem_v': nrm(ks[6], (DEPTH, DEC_BATCH, MEM_LEN, MEM_HEADS, MEM_HEAD_DIM), 1.0),
        'mem_prompt': nrm(ks[7], (BATCH, MEM_LEN, D_MODEL), 1.0),
        'rel_bias_table': nrm(ks[8], (REL_BUCKETS, SWA_HEADS), 0.5),
        'norm1_g': gain(ks[9], (DEPTH, D_MODEL)),
        'w_in': nrm(ks[10], (DEPTH, D_MODEL, IN_COLS), D_MODEL ** -0.5),
        'conv_dw_w': nrm(ks[11], (DEPTH, CONV_WIDTH, CONV_CH), CONV_WIDTH ** -0.5),
        'conv_dw_b': nrm(ks[12], (DEPTH, CONV_CH), 0.02),
        'conv_ln_g': gain(ks[13], (DEPTH, CONV_CH)),
        'conv_ln_b': nrm(ks[14], (DEPTH, CONV_CH), 0.02),
        'w_conv_out': nrm(ks[15], (DEPTH, CONV_CH, D_MODEL), CONV_CH ** -0.5),
        'swa_sinks': nrm(ks[16], (DEPTH, SWA_HEADS), 1.0),
        'w_swa_out': nrm(ks[17], (DEPTH, W_Q, D_MODEL), W_Q ** -0.5),
        'mem_norm_g': gain(ks[18], (DEPTH, D_MODEL)),
        'w_mem_kv': nrm(ks[19], (DEPTH, D_MODEL, 2 * W_QM), D_MODEL ** -0.5),
        'w_mem_out': nrm(ks[20], (DEPTH, W_QM, D_MODEL), W_QM ** -0.5),
        'w_out': nrm(ks[21], (DEPTH, D_MODEL, D_MODEL), D_MODEL ** -0.5),
        'norm2_g': gain(ks[22], (DEPTH, D_MODEL)),
        'peer_w_q': nrm(ks[23], (DEPTH, D_MODEL, PEER_HEADS * PEER_DK), D_MODEL ** -0.5),
        'peer_keys': nrm(ks[24], (DEPTH, PEER_HEADS, 2, PEER_N_KEYS, PEER_DK_HALF), PEER_DK_HALF ** -0.5),
        'peer_w_down': nrm(ks[25], (DEPTH, PEER_N_EXPERTS, D_MODEL), D_MODEL ** -0.5),
        'peer_w_up': nrm(ks[26], (DEPTH, PEER_N_EXPERTS, D_MODEL), PEER_HEADS ** -0.5),
        'final_norm_g': gain(ks[27], (D_MODEL,)),
    }

def reference(x_prompt, x_sample, cache_conv, cache_swa_k, cache_swa_v, cache_mem_k, cache_mem_v, mem_prompt,
              rel_bias_table, norm1_g, w_in, conv_dw_w, conv_dw_b, conv_ln_g, conv_ln_b, w_conv_out, swa_sinks,
              w_swa_out, mem_norm_g, w_mem_kv, w_mem_out, w_out, norm2_g, peer_w_q, peer_keys, peer_w_down,
              peer_w_up, final_norm_g):
    yp, ys = x_prompt, x_sample
    conv_p, kp, vp, mkp, mvp, conv_s, kss, vss = [], [], [], [], [], [], [], []
    for l in range(DEPTH):
        shared = (norm1_g[l], w_in[l], conv_dw_w[l], conv_dw_b[l], conv_ln_g[l], conv_ln_b[l], w_conv_out[l],
                  w_swa_out[l], w_mem_out[l], w_out[l], norm2_g[l], peer_w_q[l], peer_keys[l], peer_w_down[l], peer_w_up[l])
        mem_n = rmsnorm(mem_prompt, mem_norm_g[l])
        mkv = (mem_n @ w_mem_kv[l]).reshape(mem_prompt.shape[0], MEM_LEN, 2, MEM_HEADS, MEM_HEAD_DIM)
        mem_k, mem_v = mkv[:, :, 0], mkv[:, :, 1]
        conv0 = jnp.zeros((yp.shape[0], CONV_WIDTH - 1, CONV_CH), yp.dtype)
        attn_p = functools.partial(swa_prompt, sinks=swa_sinks[l], table=rel_bias_table)
        yp, c_p, k_p, v_p = decoder_layer(yp, conv0, attn_p, mem_k, mem_v, *shared)
        attn_s = functools.partial(swa_sample, cache_k=cache_swa_k[l], cache_v=cache_swa_v[l],
                                   sinks=swa_sinks[l], table=rel_bias_table)
        ys, c_s, k_s, v_s = decoder_layer(ys, cache_conv[l], attn_s, cache_mem_k[l], cache_mem_v[l], *shared)
        conv_p.append(c_p); kp.append(k_p); vp.append(v_p); mkp.append(mem_k); mvp.append(mem_v)
        conv_s.append(c_s); kss.append(k_s); vss.append(v_s)
    y_prompt = rmsnorm(yp, final_norm_g)
    y_sample = rmsnorm(ys, final_norm_g)
    return (y_prompt, y_sample, jnp.stack(conv_p), jnp.stack(kp), jnp.stack(vp), jnp.stack(mkp), jnp.stack(mvp),
            jnp.stack(conv_s), jnp.stack(kss), jnp.stack(vss))


_drawn_inputs = setup_inputs


def setup_inputs(seed=0):
    import zlib

    import numpy as np

    out = dict(_drawn_inputs(seed))
    spreads = {}
    factors = {'conv_ln_b': 3.056, 'swa_sinks': 6.844}
    for name, (base, spread) in spreads.items():
        noise = np.random.default_rng([zlib.crc32(name.encode()), seed]).standard_normal(out[name].shape)
        drawn = base * np.exp(spread * noise) if base else spread * noise
        out[name] = __import__('jax').numpy.asarray(drawn.astype(out[name].dtype))
    for name, factor in factors.items():
        out[name] = (out[name] * factor).astype(out[name].dtype)
    return out
```

```python
from contextlib import ExitStack

import concourse.bass as bass
from concourse import mybir
import math
import numpy as np

ALU = mybir.AluOpType
ACT = mybir.ActivationFunctionType
AX = mybir.AxisListType
F32 = mybir.dt.float32
U32 = mybir.dt.uint32

P = 128
D = 1024
SEQ = 1024
NB = 8
T = SEQ + NB
KD = D // P
NT = SEQ // P
GC = T // 3
MEM = 256
CH = 512
NC = CH // P
TAPS = 31
HALO = TAPS - 1
WIN = 128
HD = 64
SCALE = HD ** -0.5
MSCALE = 128 ** -0.5
NEG = -1e30
EPS = 1e-6
LINE = 384
HEADS = 8
TOPK = 16
SLOTS = HEADS * TOPK
NKEYS = 128
LOW = -3.0e38

CHUNKS = [("b", 0), ("a", 0), ("b", 1), ("a", 1), ("b", 2), ("a", 2), ("b", 3), ("a", 3), ("k", 0), ("v", 0)] + \
         [("q", c) for c in range(4)] + [("qm", c) for c in range(4)] + [("mem", c) for c in range(8)]
WRING = 6
DRING = 8
URING = 4
SEL_OPS = HEADS * 24 + 4


def build_kernel(nc, x_prompt, x_sample, xT, memT, w_chunks, w_gates, w_o, w_q, keysT, bias_tab, onehot, sinks_bc,
                 sinks_s, g1, gm, g2, gf, conv_w, conv_b, ln_g, ln_b, cacheT, cache_conv, cache_k, cache_v,
                 cache_kT, memkT, cache_mv, w_down, w_up,
                 y_prompt, y_sample, conv_p, k_p, v_p, mk_p, mv_p, conv_s, k_s, v_s):
    scratch_line = nc.dram_tensor("scratch_line", (HEADS, LINE), F32, kind="Internal").ap()
    scratch_vs = nc.dram_tensor("scratch_vs", (NB, P), F32, kind="Internal").ap()
    scratch_x1 = nc.dram_tensor("scratch_x1", (T, D), F32, kind="Internal").ap()
    scratch_xb = nc.dram_tensor("scratch_xb", (NB, D), F32, kind="Internal").ap()
    scratch_sc = nc.dram_tensor("scratch_sc", (NB * HEADS, 2 * NKEYS), F32, kind="Internal").ap()
    scratch_ids = nc.dram_tensor("scratch_ids", (NB, SLOTS), U32, kind="Internal").ap()
    scratch_gate = nc.dram_tensor("scratch_gate", (NB, SLOTS), F32, kind="Internal").ap()

    with ExitStack() as ctx:
        arena = ctx.enter_context(nc.sbuf_tensor("arena", [P, 52100], F32))
        consts = ctx.enter_context(nc.sbuf_tensor("constants", [P, 1000], F32))
        psum = ctx.enter_context(nc.psum_tensor("psum", [P, 8, 512], F32))

        def sem(name):
            return ctx.enter_context(nc.semaphore(name))

        def at(offset, *shape):
            n = math.prod(shape)
            v = arena[:, offset:offset + n]
            names = "abcde"[:len(shape)]
            if len(shape) > 1:
                v = v.rearrange(f"p ({' '.join(names)}) -> p {' '.join(names)}",
                                **{n: s for n, s in zip(names, shape)})
            return v

        ident = consts[:, 0:128]
        ones = consts[:, 128:256]
        eps = consts[:, 256:257]
        g1s, gms = consts[:, 257:265], consts[:, 265:273]
        cw = consts[:, 273:273 + NC * TAPS].rearrange("p (c t) -> p c t", c=NC)
        cb, lng, lnb = consts[:, 400:404], consts[:, 404:408], consts[:, 408:412]
        sink = consts[:, 412:420]
        sink_s = consts[:, 420:422]
        iota16 = consts[:, 432:448]
        small = consts[:, 448:1000]

        hT = at(0, KD, T)
        uT = at(8256, NC, HALO + T)
        yT = at(12504, NC, T)
        qT = at(16632, NC, T)
        kT = at(20760, P + T)
        vN = at(21920, NT + 2, P)
        qmT = at(23200, NC, T)
        memN = at(27328, 2, 8 * P)
        memKT = at(29376, NC, MEM)
        kN = at(30400, 2, P)
        lastu = at(30656, NC, P)
        us = at(31168, NC, NB, TAPS)
        MG = 32768
        mergedT = at(MG, KD, T)
        RG = MG + KD * T

        initialised = sem("initialised")
        loads = sem("loads")

        passed = sem("loop_waits_passed")

        def wait_loop(eng, sem, value):
            if isinstance(value, int) and value <= 0:
                return
            eng.wait_ge(sem, value)
            if not isinstance(value, int):
                eng.sem_inc(passed, 1)

        stores = sem("stores")
        n_stores = [0]

        def store(eng, dst, src):
            n_stores[0] += 16
            eng.dma_start(dst, src).then_inc(stores, 16)

        sq = at(MG, 2, T)
        sig = at(MG + 2 * T, 2, T)
        mT = at(MG + 4 * T, KD, MEM)
        std = at(RG + WRING * 1024, T)
        stdm = at(RG + WRING * 1024 + T, MEM)
        prod = at(RG + WRING * 1024 + T + MEM, NB, TAPS)
        wr = at(RG, WRING, KD, P)

        w_here = [sem(f"weights_here{i}") for i in range(WRING)]
        squared = sem("squared")
        summed = sem("summed")
        std_ready = sem("std_ready")
        h_ready = sem("h_ready")
        chunk_done = sem("chunk_done")
        set_free = [sem("psum_set0_free"), sem("psum_set1_free")]
        sig_ready = sem("sig_ready")
        dve1 = sem("dve1")
        cache_here = sem("conv_cache_here")
        padded = sem("padded")

        def groups(s):
            return psum[:, 3 * s:3 * s + 3, 0:GC]

        with nc.Block() as block:
            @block.sync
            def _(sp):
                for dst, src in ((mT, memT), (g1s, g1), (gms, gm), (cw, conv_w), (cb, conv_b), (lng, ln_g),
                                 (lnb, ln_b), (sink, sinks_bc), (sink_s[0:32, :], sinks_s)):
                    sp.dma_start(dst, src).then_inc(loads, 16)
                sp.dma_start(hT[:, 0:4, :], xT[:, 0:4, :]).then_inc(loads, 16)
                sp.dma_start(hT[:, 4:8, :], xT[:, 4:8, :]).then_inc(loads, 16)
                for i in range(len(CHUNKS)):
                    if i >= WRING:
                        sp.wait_ge(chunk_done, i - WRING + 1)
                    sp.dma_start(wr[:, i % WRING], w_chunks[i]).then_inc(w_here[i % WRING], 16)
                for c in range(NC):
                    sp.dma_start(us[:, c, :, 0:HALO], cacheT[:, c]).then_inc(cache_here, 16)
                store(sp, conv_s[:, 0:HALO - 1, :], cache_conv[:, 1:HALO, :])
                store(sp, k_s[:, 0:WIN - 1, :], cache_k[:, 1:WIN, :])
                store(sp, v_s[:, 0:WIN - 1, :], cache_v[:, 1:WIN, :])

            @block.gpsimd
            def _(pool):
                pool.memset(ident, 0.0).then_inc(initialised, 1)
                pool.memset(ones, 1.0).then_inc(initialised, 1)
                pool.memset(eps, EPS).then_inc(initialised, 1)
                pool.iota(iota16, [[1, TOPK]], base=0, channel_multiplier=0,
                          allow_small_or_imprecise_dtypes=True).then_inc(initialised, 1)
                pool.wait_ge(initialised, 4)
                pool.affine_select(out=ident, in_=ident, compare_op=ALU.not_equal, fill=1.0, base=0,
                                   pattern=[[-1, P]], channel_multiplier=1).then_inc(initialised, 1)
                pool.memset(uT[:, :, 0:HALO], 0.0).then_inc(padded, 1)
                pool.memset(kT[:, 0:P], 0.0).then_inc(padded, 1)
                pool.memset(vN[:, 0, :], 0.0).then_inc(padded, 1)

            @block.scalar
            def _(act):
                act.wait_ge(initialised, 5)
                act.wait_ge(loads, 16 * 11)
                for k in range(2 * KD):
                    if k >= 2:
                        act.wait_ge(summed, k - 1)
                    src = hT[:, k, :] if k < KD else mT[:, k - KD, :]
                    act.activation(sq[:, k % 2, 0:src.shape[1]], src, ACT.Square).then_inc(squared, 1)
                act.wait_ge(summed, 2 * KD)
                act.activation(std.rearrange("p (g n) -> p g n", g=3), groups(0), ACT.Sqrt, bias=eps,
                               scale=1.0 / D).then_inc(std_ready, 1)
                act.activation(stdm, psum[:, 3, 0:MEM], ACT.Sqrt, bias=eps, scale=1.0 / D).then_inc(std_ready, 1)
                for i, (kind, c) in enumerate(CHUNKS):
                    if kind == "a":
                        continue
                    act.wait_ge(chunk_done, i + 1)
                    src = groups(i % 2)
                    if kind == "b":
                        if c >= 2:
                            act.wait_ge(set_free[1], c - 1)
                        act.activation(sig[:, c % 2, :].rearrange("p (g n) -> p g n", g=3), src, ACT.Sigmoid)\
                           .then_inc(sig_ready, 1)
                        act.wait_ge(sig_ready, c + 1)
                        act.sem_inc(set_free[0], 1)
                        continue
                    if kind == "k":
                        act.activation(kN[:, 0, :], psum[:, 6, 0:P], ACT.Copy)
                        act.activation(kN[0:NB, 1, :], psum[0:NB, 6, P:2 * P], ACT.Copy)
                        dst = kT[:, P:P + T].rearrange("p (g n) -> p g n", g=3)
                    elif kind == "v":
                        for b in range(2):
                            act.activation(vN[:, 1 + 4 * b:5 + 4 * b, :],
                                           psum[:, 3 * (i % 2) + b, :].rearrange("p (t n) -> p t n", n=P), ACT.Copy)
                        dst, src = vN[0:NB, NT + 1, :], psum[0:NB, 3 * (i % 2) + 2, 0:P]
                    elif kind == "mem":
                        dst, src = memN[:, :, c * P:(c + 1) * P], psum[:, 3 * (i % 2):3 * (i % 2) + 2, 0:P]
                    else:
                        dst = (qT if kind == "q" else qmT)[:, c, :].rearrange("p (g n) -> p g n", g=3)
                    act.activation(dst, src, ACT.Copy).then_inc(set_free[i % 2], 1)

            @block.tensor
            def _(pe):
                pe.wait_ge(initialised, 5)
                for k in range(2 * KD):
                    pe.wait_ge(squared, k + 1)
                    if k < KD:
                        for g in range(3):
                            mm = pe.matmul(psum[:, g, 0:GC], ones, sq[:, k % 2, g * GC:(g + 1) * GC],
                                           start=(k == 0), stop=(k == KD - 1))
                    else:
                        mm = pe.matmul(psum[:, 3, 0:MEM], ones, sq[:, k % 2, 0:MEM],
                                       start=(k == KD), stop=(k == 2 * KD - 1))
                    mm.then_inc(summed, 1)
                for i, (kind, c) in enumerate(CHUNKS):
                    pe.wait_ge(w_here[i % WRING], 16 * (i // WRING + 1))
                    if i >= 2:
                        pe.wait_ge(set_free[i % 2], i // 2)
                    w = wr[:, i % WRING]
                    s = 3 * (i % 2)
                    for k in range(KD):
                        if i == 0:
                            pe.wait_ge(h_ready, k + 1)
                        first, last = k == 0, k == KD - 1
                        if kind in ("a", "b", "k", "q", "qm"):
                            for g in range(3):
                                mm = pe.matmul(psum[:, s + g, 0:GC], w[:, k, :], hT[:, k, g * GC:(g + 1) * GC],
                                               start=first, stop=last)
                    if kind == "k":
                        for k in range(KD):
                            pe.matmul(psum[:, 6, 0:P], hT[:, k, SEQ - P:SEQ], w[:, k, :],
                                      start=(k == 0), stop=(k == KD - 1))
                        for k in range(KD):
                            mm = pe.matmul(psum[0:NB, 6, P:2 * P], hT[:, k, SEQ:T], w[:, k, :],
                                           start=(k == 0), stop=(k == KD - 1))
                    if kind == "v":
                        for t in range(NT):
                            for k in range(KD):
                                pe.matmul(psum[:, s + t // 4, (t % 4) * P:(t % 4 + 1) * P],
                                          hT[:, k, t * P:(t + 1) * P], w[:, k, :],
                                          start=(k == 0), stop=(k == KD - 1))
                        for k in range(KD):
                            mm = pe.matmul(psum[0:NB, s + 2, 0:P], hT[:, k, SEQ:T], w[:, k, :],
                                           start=(k == 0), stop=(k == KD - 1))
                    if kind == "mem":
                        if c == 0:
                            pe.wait_ge(h_ready, 2 * KD)
                        for t in range(2):
                            for k in range(KD):
                                mm = pe.matmul(psum[:, s + t, 0:P], mT[:, k, t * P:(t + 1) * P], w[:, k, :],
                                               start=(k == 0), stop=(k == KD - 1))
                    mm.then_inc(chunk_done, 1)

            @block.vector
            def _(dve):
                n = [0]

                def link(ins):
                    n[0] += 1
                    ins.then_inc(dve1, 1)
                    dve.wait_ge(dve1, n[0])

                dve.wait_ge(std_ready, 2)
                link(dve.reciprocal(std, std))
                for k in range(KD):
                    dve.scalar_tensor_tensor(out=hT[:, k, :], in0=hT[:, k, :], scalar=g1s[:, k:k + 1], in1=std,
                                             op0=ALU.mult, op1=ALU.mult).then_inc(h_ready, 1)
                link(dve.reciprocal(stdm, stdm))
                for k in range(KD):
                    dve.scalar_tensor_tensor(out=mT[:, k, :], in0=mT[:, k, :], scalar=gms[:, k:k + 1], in1=stdm,
                                             op0=ALU.mult, op1=ALU.mult).then_inc(h_ready, 1)
                for c in range(NC):
                    dve.wait_ge(chunk_done, 2 * c + 2)
                    dve.wait_ge(sig_ready, c + 1)
                    dve.tensor_tensor(uT[:, c, HALO:HALO + T].rearrange("p (g n) -> p g n", g=3), groups(1),
                                      sig[:, c % 2, :].rearrange("p (g n) -> p g n", g=3), ALU.mult)\
                       .then_inc(set_free[1], 1)
                dve.wait_ge(padded, 3)
                dve.wait_ge(set_free[1], NC)
                dve.wait_ge(cache_here, 16 * NC)
                for c in range(NC):
                    acc = yT[:, c, 0:SEQ]
                    link(dve.tensor_scalar(acc, uT[:, c, 0:SEQ], cw[:, c, 0:1], cb[:, c:c + 1], ALU.mult, ALU.add))
                    for t in range(1, TAPS):
                        link(dve.scalar_tensor_tensor(out=acc, in0=uT[:, c, t:t + SEQ], scalar=cw[:, c, t:t + 1],
                                                      in1=acc, op0=ALU.mult, op1=ALU.add))
                    link(dve.tensor_copy(us[:, c, :, HALO], uT[:, c, HALO + SEQ:HALO + T]))
                    link(dve.tensor_tensor(prod, us[:, c], cw[:, c, :].unsqueeze(1).broadcast_to([P, NB, TAPS]),
                                           ALU.mult))
                    link(dve.tensor_reduce(yT[:, c, SEQ:T], prod, AX.X, ALU.add))
                    link(dve.tensor_scalar(yT[:, c, SEQ:T], yT[:, c, SEQ:T], cb[:, c:c + 1], None, ALU.add))

        lsum = sem("ln_summed")
        lcent = sem("ln_centred")
        lsq = sem("ln_squared")
        lvar = sem("ln_variance")
        lstd = sem("ln_std")
        lrec = sem("ln_reciprocal")
        lnorm = sem("ln_normed")
        lsilu = sem("ln_silu")
        turned_u = sem("conv_rows_turned")
        u_rows = sem("conv_rows_here")
        sq4 = at(MG, 3, NC, GC)
        lnstd = at(MG + 3 * NC * GC, 3, GC)
        lastsu = at(RG, NC, P)

        with nc.Block() as block:
            @block.tensor
            def _(pe):
                for g in range(3):
                    for c in range(NC):
                        mm = pe.matmul(psum[:, g, 0:GC], ones, yT[:, c, g * GC:(g + 1) * GC],
                                       start=(c == 0), stop=(c == NC - 1))
                    mm.then_inc(lsum, 1)
                for c in range(NC):
                    pe.transpose(psum[0:HALO, 6, c * P:(c + 1) * P], uT[:, c, SEQ:SEQ + HALO], ident)
                for c in range(NC):
                    mm = pe.transpose(psum[0:NB, 7, c * P:(c + 1) * P], uT[:, c, HALO + SEQ:HALO + T], ident)
                mm.then_inc(turned_u, 1)
                for g in range(3):
                    pe.wait_ge(lsq, NC * (g + 1))
                    for c in range(NC):
                        mm = pe.matmul(psum[:, 3 + g, 0:GC], ones, sq4[:, g, c, :],
                                       start=(c == 0), stop=(c == NC - 1))
                    mm.then_inc(lvar, 1)

            @block.vector
            def _(dve):
                for g in range(3):
                    dve.wait_ge(lsum, g + 1)
                    for c in range(NC):
                        y = yT[:, c, g * GC:(g + 1) * GC]
                        dve.scalar_tensor_tensor(out=y, in0=psum[:, g, 0:GC], scalar=-1.0 / CH, in1=y,
                                                 op0=ALU.mult, op1=ALU.add).then_inc(lcent, 1)
                dve.wait_ge(lcent, 3 * NC)
                for g in range(3):
                    dve.wait_ge(lstd, g + 1)
                    dve.reciprocal(lnstd[:, g, :], lnstd[:, g, :]).then_inc(lrec, 1)
                    dve.wait_ge(lrec, g + 1)
                    for c in range(NC):
                        y = yT[:, c, g * GC:(g + 1) * GC]
                        dve.tensor_tensor(y, y, lnstd[:, g, :], ALU.mult).then_inc(lnorm, 1)

            @block.scalar
            def _(act):
                for g in range(3):
                    for c in range(NC):
                        act.wait_ge(lcent, g * NC + c + 1)
                        act.activation(sq4[:, g, c, :], yT[:, c, g * GC:(g + 1) * GC], ACT.Square).then_inc(lsq, 1)
                act.wait_ge(turned_u, 1)
                act.activation(lastu[0:HALO], psum[0:HALO, 6, :].rearrange("p (c n) -> p c n", c=NC), ACT.Copy)\
                   .then_inc(u_rows, 1)
                act.activation(lastsu[0:NB], psum[0:NB, 7, :].rearrange("p (c n) -> p c n", c=NC), ACT.Copy)\
                   .then_inc(u_rows, 1)
                for g in range(3):
                    act.wait_ge(lvar, g + 1)
                    act.activation(lnstd[:, g, :], psum[:, 3 + g, 0:GC], ACT.Sqrt, bias=eps, scale=1.0 / CH)\
                       .then_inc(lstd, 1)
                for g in range(3):
                    for c in range(NC):
                        y = yT[:, c, g * GC:(g + 1) * GC]
                        act.wait_ge(lnorm, g * NC + c + 1)
                        act.activation(y, y, ACT.Silu, bias=lnb[:, c:c + 1], scale=lng[:, c:c + 1])\
                           .then_inc(lsilu, 1)

            @block.sync
            def _(sp):
                sp.wait_ge(u_rows, 2)
                store(sp, conv_p, lastu[0:HALO].rearrange("p c n -> p (c n)"))
                store(sp, conv_s[:, HALO - 1, :], lastsu[0:NB].rearrange("p c n -> p (c n)"))
                store(sp, k_p, kN[:, 0, :])
                store(sp, k_s[:, WIN - 1, :], kN[0:NB, 1, :])
                store(sp, v_p, vN[:, NT, :])
                store(sp, v_s[:, WIN - 1, :], vN[0:NB, NT + 1, :])
                for t in range(2):
                    store(sp, mk_p[t * P:(t + 1) * P, :], memN[:, t, 0:CH])
                    store(sp, mv_p[t * P:(t + 1) * P, :], memN[:, t, CH:2 * CH])
                sp.wait_ge(stores, n_stores[0])

        bias = at(MG, HEADS, 2 * P)
        bias0 = at(MG + 2048, HEADS, 2 * P)
        prob = at(MG + 4096, 2, 4, 2 * P)
        probT = at(MG + 6144, 2, 8, P)
        oh = at(RG, LINE)
        tab = at(RG + LINE, HEADS)
        line = at(RG + LINE + HEADS, LINE)
        Q0 = RG + 800
        kring = at(Q0, 2, NC, MEM)
        vring = at(Q0 + 2048, 2, 2, CH)
        ck = at(Q0 + 4096, NB, WIN + 1)
        cv = at(Q0 + 5128, NB, P)
        qmask = at(Q0 + 6152, NB, 32)
        qmmask = at(Q0 + 6408, 32, 32)
        ps_ = at(Q0 + 7432, 2, WIN + 1)
        psm = at(Q0 + 7690, MEM)
        pst = at(Q0 + 7946, 2, 32)
        pslast = at(Q0 + 8010, 2, 32)
        pmt = at(Q0 + 8074, 2, 32)
        vlast = at(Q0 + 8138, NB, P)
        bias_s = at(Q0 + 9162, 2, WIN + 1)
        flipped = at(MG + 4096, HEADS, 2 * P)
        flip = at(Q0 + 9420, P)
        stat = small[:, 0:320]
        units = [("swa", n, h) for n in range(NT) for h in range(2)] + [("mem", n, 0) for n in range(NT)]
        NU = len(units)
        mx, nm, rs, es, rd = (stat[:, 8 * i:8 * i + 8].rearrange("p (b h) -> p b h", b=2) for i in range(5))
        mxs, nms, rss, ess, rds = (stat[:, 40 + 2 * i:42 + 2 * i] for i in range(5))
        mxm, nmm, rsm, rdm = (stat[:, 50 + i:51 + i] for i in range(4))

        tab_here = sem("bias_table_here")
        tab_fill = sem("bias_table_filled")
        line_mm = sem("line_multiplied")
        line_ready = sem("line_ready")
        line_out = sem("line_out")
        bias_here = sem("flipped_bias_here")
        bias_s_here = sem("sample_bias_here")
        unflipped = sem("bias_unflipped")
        bias_ready = sem("bias_ready")
        s_done = sem("scores_done")
        pre_done = sem("maxima_done")
        exp_done = sem("exp_done")
        norm_done = sem("probs_normed")
        t_done = sem("probs_turned")
        tev_done = sem("turned_probs_copied")
        pv_done = sem("pv_done")
        o_done = sem("attention_copied")
        mk_turned = sem("mem_k_turned")
        mk_copied = sem("mem_k_copied")
        dve2 = sem("dve2")
        smp_in = sem("sample_swa_cache_here")
        vs_out = sem("vs_out")
        kr_here = [sem("mem_k0_here"), sem("mem_k1_here")]
        vr_here = [sem("mem_v0_here"), sem("mem_v1_here")]
        masked = sem("queries_masked")
        ss_done = sem("sample_scores_done")
        kr_used = sem("mem_k_used")
        vr_used = sem("mem_v_used")
        smax = sem("sample_maxima")
        sexp = sem("sample_exp")
        snorm = sem("sample_normed")
        sturn = sem("sample_turned")
        scopy = sem("sample_copied")
        spv = sem("sample_pv")
        so = sem("sample_attention_copied")

        with nc.Block() as block:
            @block.sync
            def _(sp):
                sp.dma_start(oh[0:33, 0:LINE - 1], onehot).then_inc(tab_here, 16)
                sp.dma_start(tab[0:32, :], bias_tab).then_inc(tab_here, 16)
                sp.dma_start(scratch_vs, vN[0:NB, NT + 1, :]).then_inc(vs_out, 16)
                sp.dma_start(ck[:, :, 0:WIN], cache_kT).then_inc(smp_in, 16)
                sp.dma_start(cv, cache_v.rearrange("b w d -> w b d")).then_inc(smp_in, 16)
                sp.wait_ge(line_ready, 1)
                sp.dma_start(scratch_line[:, 0:LINE - 1], line[0:HEADS, 0:LINE - 1]).then_inc(line_out, 16)
                sp.wait_ge(line_out, 16)
                skew = bass.AP(tensor=scratch_line.tensor, offset=0, ap=[[1, P], [LINE, HEADS], [1, 2 * P]])
                sp.dma_start(flipped, skew).then_inc(bias_here, 16)
                for c in range(4):
                    src = bass.AP(tensor=scratch_line.tensor, offset=((c // 2) * 4 + c % 2) * LINE + P - 1,
                                  ap=[[0, NB], [2 * LINE, 2], [1, WIN + 1]])
                    sp.dma_start(bias_s[c * NB:(c + 1) * NB], src).then_inc(bias_s_here, 16)
                sp.wait_ge(vs_out, 16)
                sp.dma_start(vlast[0:1], scratch_vs.rearrange("(o b) d -> o b d", o=1)).then_inc(smp_in, 16)
                for b in range(NB):
                    if b >= 2:
                        sp.wait_ge(kr_used, b - 1)
                    sp.dma_start(kring[:, b % 2], memkT[b]).then_inc(kr_here[b % 2], 16)
                for b in range(NB):
                    if b >= 2:
                        sp.wait_ge(vr_used, b - 1)
                    sp.dma_start(vring[:, b % 2], cache_mv[b].rearrange("(t p) n -> p t n", p=P))\
                      .then_inc(vr_here[b % 2], 16)

            @block.gpsimd
            def _(pool):
                pool.memset(tab[32:33, :], NEG).then_inc(tab_fill, 1)
                pool.wait_ge(tab_fill, 1)
                pool.memset(flip, 0.0).then_inc(tab_fill, 1)
                pool.wait_ge(tab_fill, 2)
                pool.affine_select(out=flip, in_=flip, compare_op=ALU.not_equal, fill=1.0, base=-(P - 1),
                                   pattern=[[1, P]], channel_multiplier=1).then_inc(tab_fill, 1)
                pool.memset(bias0[:, :, 0:P], NEG).then_inc(bias_ready, 1)
                pool.memset(qmask, 0.0).then_inc(masked, 1)
                pool.memset(qmmask, 0.0).then_inc(masked, 1)
                pool.wait_ge(masked, 2)
                for c in range(NC):
                    qm_d = bass.AP(tensor=arena.ap().tensor if callable(arena.ap) else arena, offset=Q0 + 6152 + c * NB,
                                   ap=[[52100, P], [33, NB]])
                    pool.tensor_copy(qm_d, qT[:, c, SEQ:T]).then_inc(masked, 1)
                    qmm_d = bass.AP(tensor=arena.ap().tensor if callable(arena.ap) else arena,
                                    offset=Q0 + 6408 + 33 * c * NB, ap=[[52100, P], [33, NB]])
                    pool.tensor_copy(qmm_d, qmT[:, c, SEQ:T]).then_inc(masked, 1)
                pool.wait_ge(smp_in, 48)
                pool.tensor_copy(ck[:, :, WIN], kT[:, P + SEQ:P + T]).then_inc(masked, 1)

            @block.tensor
            def _(pe):
                pe.wait_ge(tab_here, 32)
                pe.wait_ge(tab_fill, 1)
                pe.matmul(psum[0:HEADS, 7, 0:LINE - 1], tab[0:33, :], oh[0:33, 0:LINE - 1], start=True, stop=True)\
                  .then_inc(line_mm, 1)
                for t in range(2):
                    for h in range(NC):
                        mm = pe.transpose(psum[:, 4 + t, h * P:(h + 1) * P], memN[:, t, h * P:(h + 1) * P], ident)
                mm.then_inc(mk_turned, 1)
                pe.wait_ge(bias_here, 16)
                pe.wait_ge(tab_fill, 3)
                for h in range(HEADS):
                    mm = pe.matmul(psum[:, h // 2, (h % 2) * 256:(h % 2) * 256 + 256], flip, flipped[:, h, :],
                                   start=True, stop=True)
                mm.then_inc(unflipped, 1)
                pe.wait_ge(mk_copied, 2)
                pe.wait_ge(bias_ready, 3)
                for s in range(NU + 2):
                    if s < NU:
                        kind, n, hf = units[s]
                        if s >= 2:
                            pe.wait_ge(pre_done if kind == "swa" or units[s - 2][0] == "swa" else exp_done, s - 1)
                            if kind == "mem":
                                pe.wait_ge(exp_done, s - 1)
                        S = psum[:, 2 * (s % 2):2 * (s % 2) + 2, :].rearrange("p b (h k) -> p (b h) k", k=2 * P)
                        for i in range(4):
                            if kind == "swa":
                                j, c = i // 2, 2 * hf + i % 2
                                rows = slice(64 * j, 64 * j + 64)
                                mm = pe.matmul(S[:, i, :], qT[rows, c, n * P:(n + 1) * P],
                                               kT[rows, n * P:n * P + 2 * P], start=True, stop=True)
                            else:
                                mm = pe.matmul(S[:, i, :], qmT[:, i, n * P:(n + 1) * P], memKT[:, i, :],
                                               start=True, stop=True)
                        mm.then_inc(s_done, 1)
                    if 1 <= s <= NU:
                        u = s - 1
                        pe.wait_ge(norm_done, u + 1)
                        if u >= 1:
                            pe.wait_ge(tev_done, u)
                        for i in range(8):
                            mm = pe.transpose(psum[:, 4 + i // 4, (i % 4) * P:(i % 4 + 1) * P],
                                              prob[:, u % 2, i // 2, (i % 2) * P:(i % 2 + 1) * P], ident)
                        mm.then_inc(t_done, 1)
                    if s >= 2:
                        u = s - 2
                        kind, n, hf = units[u]
                        pe.wait_ge(tev_done, u + 1)
                        if u >= 1:
                            pe.wait_ge(o_done, u)
                        for i in range(4):
                            for kt in range(2):
                                pt = probT[:, u % 2, 2 * i + kt, :]
                                if kind == "swa":
                                    j, cc = i // 2, i % 2
                                    mm = pe.matmul(psum[64 * j:64 * j + 64, 6, cc * P:(cc + 1) * P],
                                                   vN[:, n + kt, 64 * j:64 * j + 64], pt, start=(kt == 0), stop=(kt == 1))
                                else:
                                    mm = pe.matmul(psum[:, 6, i * P:(i + 1) * P],
                                                   memN[:, kt, CH + i * P:CH + (i + 1) * P], pt,
                                                   start=(kt == 0), stop=(kt == 1))
                        mm.then_inc(pv_done, 1)
                pe.wait_ge(masked, 11)
                pe.wait_ge(norm_done, NU)
                for j in range(2):
                    rows = slice(64 * j, 64 * j + 64)
                    for b in range(NB):
                        mm = pe.matmul(psum[0:32, j, 0:WIN + 1], qmask[rows, b, :], ck[rows, b, :],
                                       start=(b == 0), stop=(b == NB - 1))
                mm.then_inc(ss_done, 1)
                for b in range(NB):
                    pe.wait_ge(kr_here[b % 2], 16 * (b // 2 + 1))
                    for h in range(NC):
                        mm = pe.matmul(psum[0:32, 2, 0:MEM], qmmask[:, h * NB + b, :], kring[:, b % 2, h, :],
                                       start=(b == 0 and h == 0), stop=(b == NB - 1 and h == NC - 1))
                    mm.then_inc(kr_used, 1)
                pe.wait_ge(snorm, 2)
                pe.wait_ge(tev_done, NU)
                for j in range(2):
                    pe.transpose(psum[:, 4, j * 32:(j + 1) * 32], ps_[0:32, j, 0:WIN], ident[0:32, 0:32])
                for j in range(2):
                    pe.transpose(psum[:, 4, 64 + j * 32:64 + (j + 1) * 32], psm[0:32, j * P:(j + 1) * P],
                                 ident[0:32, 0:32])
                for j in range(2):
                    mm = pe.transpose(psum[0:1, 5, j * 32:(j + 1) * 32], ps_[0:32, j, WIN:WIN + 1],
                                      ident[0:32, 0:32])
                mm.then_inc(sturn, 1)
                pe.wait_ge(scopy, 3)
                pe.wait_ge(smp_in, 48)
                pe.wait_ge(o_done, NU)
                for b in range(NB):
                    for j in range(2):
                        o = psum[64 * j:64 * j + 64, 6, 0:32].rearrange("p (c b) -> p c b", b=NB)[:, :, b]
                        w = pst[:, j, :].rearrange("p (c b) -> p c b", b=NB)[:, :, b]
                        wl = pslast[0:1, j, :].rearrange("p (c b) -> p c b", b=NB)[:, :, b]
                        pe.matmul(o, cv[:, b, 64 * j:64 * j + 64], w, start=True, stop=False)
                        mm = pe.matmul(o, vlast[0:1, b, 64 * j:64 * j + 64], wl, start=False, stop=True)
                mm.then_inc(spv, 1)
                for b in range(NB):
                    pe.wait_ge(vr_here[b % 2], 16 * (b // 2 + 1))
                    for h in range(NC):
                        r = h * NB + b
                        for t in range(2):
                            mm = pe.matmul(psum[:, 7, r:r + 1], vring[:, b % 2, t, h * P:(h + 1) * P],
                                           pmt[:, t, r:r + 1], start=(t == 0), stop=(t == 1))
                    mm.then_inc(vr_used, 1)

            @block.vector
            def _(dve):
                n_ = [0]

                def link(ins):
                    n_[0] += 1
                    ins.then_inc(dve2, 1)
                    dve.wait_ge(dve2, n_[0])

                dve.wait_ge(unflipped, 1)
                dve.wait_ge(bias_ready, 3)
                for s in range(NU + 1):
                    if s < NU:
                        kind, n, hf = units[s]
                        b = s % 2
                        S = psum[:, 2 * b:2 * b + 2, :].rearrange("p b (h k) -> p (b h) k", k=2 * P)
                        dve.wait_ge(s_done, s + 1)
                        if s >= 2:
                            dve.wait_ge(t_done, s - 1)
                        if kind == "swa":
                            bb = (bias if n else bias0)[:, 4 * hf:4 * hf + 4, :]
                            link(dve.scalar_tensor_tensor(out=prob[:, b], in0=S, scalar=SCALE, in1=bb,
                                                          op0=ALU.mult, op1=ALU.add))
                            link(dve.tensor_reduce(mx[:, b], prob[:, b], AX.X, ALU.max))
                            link(dve.tensor_tensor(mx[:, b], mx[:, b], sink[:, 4 * hf:4 * hf + 4], ALU.max))
                            link(dve.tensor_tensor(es[:, b], sink[:, 4 * hf:4 * hf + 4], mx[:, b], ALU.subtract))
                            dve.tensor_scalar(nm[:, b], mx[:, b], -1.0, None, ALU.mult).then_inc(pre_done, 1)
                        else:
                            link(dve.tensor_reduce(mx[:, b], S, AX.X, ALU.max))
                            dve.tensor_scalar(nm[:, b], mx[:, b], -MSCALE, None, ALU.mult).then_inc(pre_done, 1)
                    if s >= 1:
                        u = s - 1
                        b = u % 2
                        dve.wait_ge(exp_done, u + 1)
                        if units[u][0] == "swa":
                            link(dve.tensor_tensor(rs[:, b], rs[:, b], es[:, b], ALU.add))
                        link(dve.reciprocal(rd[:, b], rs[:, b]))
                        dve.tensor_tensor(prob[:, b], prob[:, b],
                                          rd[:, b].unsqueeze(2).broadcast_to([P, 4, 2 * P]), ALU.mult)\
                           .then_inc(norm_done, 1)
                dve.wait_ge(ss_done, 1)
                dve.wait_ge(bias_s_here, 16 * 4)
                sw = ps_[0:32]
                link(dve.scalar_tensor_tensor(out=sw, in0=psum[0:32, 0:2, 0:WIN + 1], scalar=SCALE,
                                              in1=bias_s[0:32], op0=ALU.mult, op1=ALU.add))
                link(dve.tensor_reduce(mxs[0:32], sw, AX.X, ALU.max))
                link(dve.tensor_tensor(mxs[0:32], mxs[0:32], sink_s[0:32], ALU.max))
                link(dve.tensor_tensor(ess[0:32], sink_s[0:32], mxs[0:32], ALU.subtract))
                dve.tensor_scalar(nms[0:32], mxs[0:32], -1.0, None, ALU.mult).then_inc(smax, 1)
                dve.wait_ge(kr_used, NB)
                link(dve.tensor_reduce(mxm[0:32], psum[0:32, 2, 0:MEM], AX.X, ALU.max))
                dve.tensor_scalar(nmm[0:32], mxm[0:32], -MSCALE, None, ALU.mult).then_inc(smax, 1)
                dve.wait_ge(sexp, 2)
                link(dve.tensor_tensor(rss[0:32], rss[0:32], ess[0:32], ALU.add))
                link(dve.reciprocal(rds[0:32], rss[0:32]))
                dve.tensor_tensor(sw, sw, rds[0:32].unsqueeze(2).broadcast_to([32, 2, WIN + 1]), ALU.mult)\
                   .then_inc(snorm, 1)
                link(dve.reciprocal(rdm[0:32], rsm[0:32]))
                dve.tensor_scalar(psm[0:32], psm[0:32], rdm[0:32], None, ALU.mult).then_inc(snorm, 1)

            @block.scalar
            def _(act):
                act.wait_ge(line_mm, 1)
                act.activation(line[0:HEADS, 0:LINE - 1], psum[0:HEADS, 7, 0:LINE - 1], ACT.Copy)\
                   .then_inc(line_ready, 1)
                act.wait_ge(mk_turned, 1)
                for t in range(2):
                    act.activation(memKT[:, :, t * P:(t + 1) * P],
                                   psum[:, 4 + t, :].rearrange("p (h n) -> p h n", h=NC), ACT.Copy)\
                       .then_inc(mk_copied, 1)
                act.wait_ge(unflipped, 1)
                turned_back = psum[:, 0:4, :].rearrange("p b (h k) -> p (b h) k", k=2 * P)
                act.activation(bias, turned_back, ACT.Copy).then_inc(bias_ready, 1)
                act.activation(bias0[:, :, P:2 * P], turned_back[:, :, P:2 * P], ACT.Copy).then_inc(bias_ready, 1)
                for s in range(NU + 2):
                    if s < NU:
                        kind, n, hf = units[s]
                        b = s % 2
                        S = psum[:, 2 * b:2 * b + 2, :].rearrange("p b (h k) -> p (b h) k", k=2 * P)
                        act.wait_ge(pre_done, s + 1)
                        if kind == "swa":
                            act.activation(es[:, b], es[:, b], ACT.Exp)
                        for i in range(4):
                            src = prob[:, b, i, :] if kind == "swa" else S[:, i, :]
                            ins = act.activation(prob[:, b, i, :], src, ACT.Exp, bias=nm[:, b, i:i + 1],
                                                 scale=1.0 if kind == "swa" else MSCALE,
                                                 accum_out=rs[:, b, i:i + 1])
                        ins.then_inc(exp_done, 1)
                    if 1 <= s <= NU:
                        u = s - 1
                        act.wait_ge(t_done, u + 1)
                        if u >= 2:
                            act.wait_ge(pv_done, u - 1)
                        act.activation(probT[:, u % 2],
                                       psum[:, 4:6, :].rearrange("p b (i n) -> p (b i) n", n=P), ACT.Copy)\
                           .then_inc(tev_done, 1)
                    if s >= 2:
                        u = s - 2
                        kind, n, hf = units[u]
                        act.wait_ge(pv_done, u + 1)
                        if kind == "swa":
                            dst = qT[:, 2 * hf:2 * hf + 2, n * P:(n + 1) * P]
                            src = psum[:, 6, 0:2 * P].rearrange("p (c n) -> p c n", c=2)
                        else:
                            dst = qmT[:, :, n * P:(n + 1) * P]
                            src = psum[:, 6, :].rearrange("p (c n) -> p c n", c=4)
                        act.activation(dst, src, ACT.Copy).then_inc(o_done, 1)
                act.wait_ge(smax, 1)
                act.activation(ess[0:32], ess[0:32], ACT.Exp)
                for j in range(2):
                    ins = act.activation(ps_[0:32, j, :], ps_[0:32, j, :], ACT.Exp, bias=nms[0:32, j:j + 1],
                                         accum_out=rss[0:32, j:j + 1])
                ins.then_inc(sexp, 1)
                act.wait_ge(smax, 2)
                act.activation(psm[0:32], psum[0:32, 2, 0:MEM], ACT.Exp, bias=nmm[0:32], scale=MSCALE,
                               accum_out=rsm[0:32]).then_inc(sexp, 1)
                act.wait_ge(sturn, 1)
                act.activation(pst, psum[:, 4, 0:64].rearrange("p (j r) -> p j r", j=2), ACT.Copy).then_inc(scopy, 1)
                act.activation(pmt, psum[:, 4, 64:128].rearrange("p (j r) -> p j r", j=2), ACT.Copy)\
                   .then_inc(scopy, 1)
                act.activation(pslast[0:1], psum[0:1, 5, 0:64].rearrange("p (j r) -> p j r", j=2), ACT.Copy)\
                   .then_inc(scopy, 1)
                act.wait_ge(spv, 1)
                act.wait_ge(masked, 10)
                act.activation(qT[:, :, SEQ:T], psum[:, 6, 0:32].rearrange("p (c b) -> p c b", b=NB), ACT.Copy)\
                   .then_inc(so, 1)
                act.wait_ge(vr_used, NB)
                act.activation(qmT[:, :, SEQ:T], psum[:, 7, 0:32].rearrange("p (c b) -> p c b", b=NB), ACT.Copy)\
                   .then_inc(so, 1)

        GRING = 5
        gw = at(RG, GRING, KD + NC, P)
        gsig = at(RG + GRING * 1536, 2, GC)
        gprod = at(RG + GRING * 1536 + 2 * GC, 2, GC)
        gw_here = [sem(f"gate_weights_here{i}") for i in range(GRING)]
        pair_done = sem("pair_done")
        gate_ready = sem("gate_ready")
        taken = sem("pair_taken")
        added = sem("added")
        branch = [yT, qT, qmT]
        pairs = [(m, br, g) for m in range(KD) for br in range(3) for g in range(3)]

        with nc.Block() as block:
            @block.sync
            def _(sp):
                for i in range(3 * KD):
                    if i >= GRING:
                        sp.wait_ge(pair_done, 3 * (i - GRING + 1))
                    sp.dma_start(gw[:, i % GRING], w_gates[i]).then_inc(gw_here[i % GRING], 16)

            @block.tensor
            def _(pe):
                for i, (m, br, g) in enumerate(pairs):
                    w = gw[:, (i // 3) % GRING]
                    if g == 0:
                        pe.wait_ge(gw_here[(i // 3) % GRING], 16 * (i // 3 // GRING + 1))
                    if i >= 4:
                        pe.wait_ge(taken, i - 3)
                    cols = slice(g * GC, (g + 1) * GC)
                    b = 2 * (i % 4)
                    for k in range(KD):
                        pe.matmul(psum[:, b, 0:GC], w[:, k, :], hT[:, k, cols], start=(k == 0), stop=(k == KD - 1))
                    for c in range(NC):
                        mm = pe.matmul(psum[:, b + 1, 0:GC], w[:, KD + c, :], branch[br][:, c, cols],
                                       start=(c == 0), stop=(c == NC - 1))
                    mm.then_inc(pair_done, 1)

            @block.scalar
            def _(act):
                for i in range(len(pairs)):
                    act.wait_ge(pair_done, i + 1)
                    if i >= 2:
                        act.wait_ge(taken, i - 1)
                    act.activation(gsig[:, i % 2, :], psum[:, 2 * (i % 4), 0:GC], ACT.Sigmoid)\
                       .then_inc(gate_ready, 1)

            @block.vector
            def _(dve):
                n_add = 0
                for i, (m, br, g) in enumerate(pairs):
                    dve.wait_ge(gate_ready, i + 1)
                    out = mergedT[:, m, g * GC:(g + 1) * GC]
                    dst = out if br == 0 else gprod[:, i % 2, :]
                    if n_add:
                        dve.wait_ge(added, n_add)
                    dve.tensor_tensor(dst, gsig[:, i % 2, :], psum[:, 2 * (i % 4) + 1, 0:GC], ALU.mult)\
                       .then_inc(taken, 1)
                    if br:
                        dve.wait_ge(taken, i + 1)
                        dve.tensor_tensor(out, out, dst, ALU.add).then_inc(added, 1)
                        n_add += 1

        xb = at(0, NT, D)
        wo = at(16384, KD, D)
        xin = at(RG, 2, D)
        g2b = at(RG + 2048, D)
        xbs = at(RG + 3072, D)
        x1s = at(RG + 4096, D)
        junk = at(RG + 5120, D)
        x1_out = [sem("x1_out0"), sem("x1_out1")]
        x_here = [sem("x_here0"), sem("x_here1")]
        wo_here = sem("w_out_here")
        o_mm = sem("out_product")
        x1_done = sem("x1_done")
        x1_sq = sem("x1_squared")
        x1_std = sem("x1_std")
        x1_rec = sem("x1_reciprocal")
        xb_done = sem("xb_done")
        st2 = small[:, 320:352]

        def tile_rows(n):
            return P if n < NT else NB

        with nc.Block() as block:
            @block.sync
            def _(sp):
                sp.dma_start(wo, w_o).then_inc(wo_here, 16)
                sp.dma_start(g2b, bass.AP(tensor=g2.tensor, offset=g2.offset, ap=[[0, P], [1, D]])).then_inc(wo_here, 16)
                for n in range(NT + 1):
                    if n >= 2 and n < NT:
                        sp.wait_ge(x1_out[n % 2], 16 * (n // 2))
                        sp.wait_ge(xb_done, n - 1)
                    if n < NT:
                        sp.dma_start(xin[:, n % 2, :], x_prompt[n * P:(n + 1) * P, :]).then_inc(x_here[n % 2], 16)
                    else:
                        sp.dma_start(x1s[0:NB, :], x_sample).then_inc(x_here[0], 16)
                    if 1 <= n:
                        sp.wait_ge(x1_done, n)
                        sp.dma_start(scratch_x1[(n - 1) * P:n * P, :], xin[:, (n - 1) % 2, :])\
                          .then_inc(x1_out[(n - 1) % 2], 16)
                sp.wait_ge(x1_done, NT + 1)
                sp.dma_start(scratch_x1[SEQ:T, :], x1s[0:NB, :]).then_inc(x1_out[0], 16)
                sp.wait_ge(x1_out[0], 16 * 5)
                sp.wait_ge(x1_out[1], 16 * 4)

            @block.tensor
            def _(pe):
                pe.wait_ge(wo_here, 32)
                for n in range(NT + 1):
                    r = tile_rows(n)
                    if n >= 2:
                        pe.wait_ge(x1_done, n - 1)
                    for k in range(KD):
                        for h in range(2):
                            mm = pe.matmul(psum[0:r, 2 * (n % 2) + h, :], mergedT[:, k, n * P:n * P + r],
                                           wo[:, k, h * 512:(h + 1) * 512], start=(k == 0), stop=(k == KD - 1))
                    mm.then_inc(o_mm, 1)

            @block.vector
            def _(dve):
                for n in range(NT + 1):
                    r = tile_rows(n)
                    x1 = xin[:, n % 2, :] if n < NT else x1s[0:NB, :]
                    dst = xb[:, n, :] if n < NT else xbs[0:NB, :]
                    dve.wait_ge(o_mm, n + 1)
                    dve.wait_ge(x_here[n % 2], 16 * (n // 2 + 1))
                    dve.tensor_tensor(x1.rearrange("p (h n) -> p h n", h=2), x1.rearrange("p (h n) -> p h n", h=2),
                                      psum[0:r, 2 * (n % 2):2 * (n % 2) + 2, :], ALU.add).then_inc(x1_done, 1)
                    dve.wait_ge(x1_std, n + 1)
                    dve.reciprocal(st2[0:r, n:n + 1], st2[0:r, n:n + 1]).then_inc(x1_rec, 1)
                    dve.wait_ge(x1_rec, n + 1)
                    dve.scalar_tensor_tensor(out=dst, in0=x1, scalar=st2[0:r, n:n + 1], in1=g2b[0:r, :],
                                             op0=ALU.mult, op1=ALU.mult).then_inc(xb_done, 1)

            @block.scalar
            def _(act):
                for n in range(NT + 1):
                    r = tile_rows(n)
                    x1 = xin[:, n % 2, :] if n < NT else x1s[0:NB, :]
                    s_ = st2[0:r, n:n + 1]
                    act.wait_ge(x1_done, n + 1)
                    act.wait_ge(initialised, 5)
                    if n:
                        act.wait_ge(x1_sq, n)
                    act.activation(junk[0:r, :], x1, ACT.Square, accum_out=s_).then_inc(x1_sq, 1)
                    act.wait_ge(x1_sq, n + 1)
                    act.activation(s_, s_, ACT.Sqrt, bias=eps[0:r], scale=1.0 / D).then_inc(x1_std, 1)

        scores = at(16384, NT, HEADS, 2 * NKEYS)
        wq = at(MG, KD, D)
        keys = at(RG, HEADS, 2 * NKEYS)
        xbT = at(RG + 2048 + 1024 * 3, 2, KD, P)
        pqT = at(8192, 2, HEADS, P)
        scs = at(8192 + 2048, HEADS, 2 * NKEYS)
        wq_here = sem("peer_w_q_here")
        key_zero = sem("key_zero")
        xT_done = sem("xb_turned")
        xT_copied = sem("xb_turned_copied")
        pq_done = sem("peer_q_done")
        pq_copied = sem("peer_q_copied")
        sc_done = sem("peer_scores_done")
        sc_copied = sem("peer_scores_copied")
        smp_out = sem("sample_rows_out")

        with nc.Block() as block:
            @block.sync
            def _(sp):
                sp.dma_start(wq, w_q).then_inc(wq_here, 16)
                sp.wait_ge(key_zero, 1)
                sp.dma_start(keys[0:64, :, 0:NKEYS], keysT[0:64]).then_inc(wq_here, 16)
                sp.dma_start(keys[64:128, :, NKEYS:2 * NKEYS], keysT[64:128]).then_inc(wq_here, 16)
                sp.dma_start(scratch_xb, xbs[0:NB, :]).then_inc(smp_out, 16)
                sp.wait_ge(sc_copied, NT + 1)
                sp.dma_start(scratch_sc.rearrange("(b h) n -> b (h n)", h=HEADS),
                             scs[0:NB].rearrange("p h n -> p (h n)")).then_inc(smp_out, 16)
                sp.wait_ge(smp_out, 32)

            @block.gpsimd
            def _(pool):
                pool.memset(keys, 0.0).then_inc(key_zero, 1)

            @block.tensor
            def _(pe):
                for s in range(NT + 3):
                    if s <= NT:
                        n = s
                        r = tile_rows(n)
                        src = xb[:, n, :] if n < NT else xbs[0:NB, :]
                        if n >= 1:
                            pe.wait_ge(xT_copied, n)
                        for k in range(KD):
                            mm = pe.transpose(psum[:, k // 4, (k % 4) * P:(k % 4) * P + r],
                                              src[:, k * P:(k + 1) * P], ident[0:r, 0:r])
                        mm.then_inc(xT_done, 1)
                    if 1 <= s <= NT + 1:
                        n = s - 1
                        r = tile_rows(n)
                        pe.wait_ge(xT_copied, n + 1)
                        pe.wait_ge(wq_here, 48)
                        if n >= 1:
                            pe.wait_ge(pq_copied, n)
                        for h in range(HEADS):
                            for k in range(KD):
                                mm = pe.matmul(psum[:, 2 + h // 4, (h % 4) * P:(h % 4) * P + r],
                                               wq[:, k, h * P:(h + 1) * P], xbT[:, n % 2, k, 0:r],
                                               start=(k == 0), stop=(k == KD - 1))
                        mm.then_inc(pq_done, 1)
                    if s >= 2:
                        n = s - 2
                        r = tile_rows(n)
                        pe.wait_ge(pq_copied, n + 1)
                        if n >= 1:
                            pe.wait_ge(sc_copied, n)
                        for h in range(HEADS):
                            mm = pe.matmul(psum[0:r, 4 + h // 2, (h % 2) * 256:(h % 2) * 256 + 256],
                                           pqT[:, n % 2, h, 0:r], keys[:, h, :], start=True, stop=True)
                        mm.then_inc(sc_done, 1)

            @block.scalar
            def _(act):
                for n in range(NT + 1):
                    r = tile_rows(n)
                    act.wait_ge(xT_done, n + 1)
                    if n >= 2:
                        act.wait_ge(pq_done, n - 1)
                    act.activation(xbT[:, n % 2, :, 0:r],
                                   psum[:, 0:2, :].rearrange("p b (k n) -> p (b k) n", n=P)[:, :, 0:r], ACT.Copy)\
                       .then_inc(xT_copied, 1)
                    act.wait_ge(pq_done, n + 1)
                    if n >= 2:
                        act.wait_ge(sc_done, n - 1)
                    act.activation(pqT[:, n % 2, :, 0:r],
                                   psum[:, 2:4, :].rearrange("p b (k n) -> p (b k) n", n=P)[:, :, 0:r], ACT.Copy)\
                       .then_inc(pq_copied, 1)

            @block.vector
            def _(dve):
                for n in range(NT + 1):
                    r = tile_rows(n)
                    dve.wait_ge(sc_done, n + 1)
                    dst = scores[:, n] if n < NT else scs[0:NB]
                    dve.tensor_copy(dst.rearrange("p (b h) n -> p b (h n)", b=4), psum[0:r, 4:8, :])\
                       .then_inc(sc_copied, 1)

        rowD = at(MG, DRING, D)
        rowU = at(MG + DRING * D, URING, D)
        E0 = 8192
        scur = at(E0, HEADS, 2, NKEYS)
        xcur = at(E0 + 2048, D)
        x1cur = at(E0 + 3072, D)
        gfb = at(E0 + 4096, D)
        ybuf = at(E0 + 5120, D)
        oneh = at(E0 + 6144, 2, TOPK, TOPK)
        oneh2 = at(E0 + 6656, 2, TOPK, TOPK)
        cand = at(E0 + 7168, TOPK, TOPK)
        cand2 = at(E0 + 7424, TOPK, TOPK)
        stmp = at(E0 + 7680, 2, NKEYS)
        E1 = MG + (DRING + URING) * D
        sv = at(E1, HEADS, 2, TOPK)
        si = at(E1 + 256, HEADS, 2, TOPK).bitcast(U32)
        sif = at(E1 + 512, HEADS, 2, TOPK)
        best = at(E1 + 768, HEADS, TOPK)
        ci = at(E1 + 896, HEADS, TOPK).bitcast(U32)
        ij = at(E1 + 1024, HEADS, 2, TOPK).bitcast(U32)
        ijf = at(E1 + 1280, HEADS, 2, TOPK)
        pick = at(E1 + 1536, HEADS, 2, TOPK)
        idN = at(E1 + 1792, SLOTS).bitcast(U32)
        idD = at(E1 + 1920, SLOTS).bitcast(U32)
        idU = at(E1 + 2048, SLOTS).bitcast(U32)
        gateN = at(E1 + 2176, HEADS, TOPK)
        gateD = at(E1 + 2304, SLOTS)
        dots = at(E1 + 2432, SLOTS)
        coef = at(E1 + 2560, SLOTS)
        gel = at(E1 + 2688, SLOTS)
        diag = at(E1 + 2816, 4, P)
        st3 = small[:, 352:400]
        hsum, hrec = st3[:, 0:8], st3[:, 8:16]
        msq, mrec = st3[:, 16:17], st3[:, 17:18]

        sel = sem("select_step")
        sel_exp = sem("select_exp")
        scur_here = sem("block_scores_copied")
        xcur_here = sem("block_x_copied")
        ids_ready = sem("expert_lists_ready")
        idu_ready = sem("up_lists_ready")
        gD = [sem(f"down_rows_here{i}") for i in range(DRING)]
        gU = [sem(f"up_rows_here{i}") for i in range(URING)]
        dot_done = sem("dots_done")
        gelu_done = sem("gelu_done")
        coef_ready = sem("coefficients_ready")
        gates_moved = sem("gates_moved")
        diag_ready = sem("diagonal_ready")
        up_done = sem("up_products_done")
        x1_here = sem("x1_here")
        y_sum = sem("y_summed")
        y_sq = sem("y_squared")
        y_std = sem("y_std")
        y_rec = sem("y_reciprocal")
        y_ready = sem("y_ready")
        y_out = sem("y_out")
        gf_here = sem("final_gain_here")

        def select_head_keys(dve, link, p, s2, svh, sih):
            for c in range(2):
                link(dve.max(svh[:, c, 0:8], s2[:, c, :]))
                link(dve.max_index(sih[:, c, 0:8], svh[:, c, 0:8], s2[:, c, :]))
                link(dve.match_replace(stmp[0:p, c, :], svh[:, c, 0:8], s2[:, c, :], LOW))
                link(dve.max(svh[:, c, 8:16], stmp[0:p, c, :]))
                link(dve.max_index(sih[:, c, 8:16], svh[:, c, 8:16], stmp[0:p, c, :]))

        def select_head_pairs(dve, link, p, svh, bh, cih):
            cd, c2 = cand[0:p], cand2[0:p]
            link(dve.tensor_tensor(cd, svh[:, 0, :].unsqueeze(2).broadcast_to([p, TOPK, TOPK]),
                                   svh[:, 1, :].unsqueeze(1).broadcast_to([p, TOPK, TOPK]), ALU.add))
            cf, cf2 = cd.rearrange("p i j -> p (i j)"), c2.rearrange("p i j -> p (i j)")
            link(dve.max(bh[:, 0:8], cf))
            link(dve.max_index(cih[:, 0:8], bh[:, 0:8], cf))
            link(dve.match_replace(cf2, bh[:, 0:8], cf, LOW))
            link(dve.max(bh[:, 8:16], cf2))
            link(dve.max_index(cih[:, 8:16], bh[:, 8:16], cf2))

        def select_head_ids(dve, link, p, sih, sfh, cih, ijh, ijfh, pk, idh):
            link(dve.tensor_scalar(ijh[:, 0, :], cih, 4, None, ALU.logical_shift_right))
            link(dve.tensor_scalar(ijh[:, 1, :], cih, 15, None, ALU.bitwise_and))
            link(dve.tensor_copy(ijfh, ijh))
            link(dve.tensor_copy(sfh, sih))
            o1, o2 = oneh[0:p], oneh2[0:p]
            full = [p, 2, TOPK, TOPK]
            link(dve.tensor_tensor(o1, iota16[0:p].unsqueeze(1).unsqueeze(1).broadcast_to(full),
                                   ijfh.unsqueeze(3).broadcast_to(full), ALU.is_equal))
            link(dve.tensor_tensor(o2, o1, sfh.unsqueeze(2).broadcast_to(full), ALU.mult))
            link(dve.tensor_reduce(pk, o2, AX.X, ALU.add))
            link(dve.scalar_tensor_tensor(out=idh, in0=pk[:, 0, :], scalar=float(NKEYS), in1=pk[:, 1, :],
                                          op0=ALU.mult, op1=ALU.add))

        with nc.Block() as block:
            def peel(body, eng):
                body(0, True, False, True)
                body(1, True, True, True)
                with eng.Fori(2, NT - 1) as it:
                    body(it, True, True, True)
                body(NT - 1, True, True, False)
                body(NT, False, True, False)

            @block.gpsimd
            def _(pool):
                def step(it, down, up, select):
                    wait_loop(pool, ids_ready, it * 2 + 1)
                    for j in range(SLOTS):
                        if up:
                            wait_loop(pool, up_done, (it - 1) * SLOTS + max(j - URING + 1, 0))
                            pool.indirect_dma_start(rowU[:, j % URING, :], None, w_up,
                                                    bass.IndirectOffsetOnAxis(ap=idU[:, j:j + 1], axis=0))\
                                .then_inc(gU[j % URING], 16)
                        if down:
                            if not (isinstance(it, int) and it == 0 and j < DRING):
                                wait_loop(pool, dot_done, it * SLOTS + (j - DRING + 1))
                            pool.indirect_dma_start(rowD[:, j % DRING, :], None, w_down,
                                                    bass.IndirectOffsetOnAxis(ap=idD[:, j:j + 1], axis=0))\
                                .then_inc(gD[j % DRING], 16)
                    if down:
                        wait_loop(pool, dot_done, (it + 1) * SLOTS)
                        if up:
                            wait_loop(pool, up_done, it * SLOTS)
                        pool.tensor_copy(idU, idD).then_inc(ids_ready, 1)
                        wait_loop(pool, ids_ready, it * 2 + 2)
                        if select:
                            wait_loop(pool, sel, (it + 2) * SEL_OPS)
                        pool.tensor_copy(idD, idN).then_inc(ids_ready, 1)
                        wait_loop(pool, ids_ready, it * 2 + 3)

                pool.wait_ge(sel, SEL_OPS)
                pool.tensor_copy(idD, idN).then_inc(ids_ready, 1)
                pool.wait_ge(ids_ready, 1)
                peel(step, pool)

            @block.vector
            def _(dve):
                def selection(sb):
                    k = [0]

                    def link(ins):
                        k[0] += 1
                        ins.then_inc(sel, 1)
                        wait_loop(dve, sel, sb * SEL_OPS + k[0])

                    pieces = []

                    def gates():
                        full = [P, HEADS, TOPK]
                        wait_loop(dve, gates_moved, sb)
                        link(dve.tensor_tensor(gateN, best, best[:, :, 0:1].broadcast_to(full), ALU.subtract))
                        wait_loop(dve, sel_exp, sb + 1)
                        link(dve.tensor_reduce(hsum, gateN, AX.X, ALU.add))
                        link(dve.reciprocal(hrec, hsum))
                        link(dve.tensor_tensor(gateN, gateN, hrec.unsqueeze(2).broadcast_to(full), ALU.mult))

                    def keys_of(h):
                        if h == 0:
                            wait_loop(dve, scur_here, sb + 1)
                        select_head_keys(dve, link, P, scur[:, h], sv[:, h], si[:, h])

                    def ids_of(h):
                        select_head_pairs(dve, link, P, sv[:, h], best[:, h], ci[:, h])
                        select_head_ids(dve, link, P, si[:, h], sif[:, h], ci[:, h], ij[:, h], ijf[:, h], pick[:, h],
                                        idN[:, h * TOPK:(h + 1) * TOPK])

                    return keys_of, ids_of, gates

                def step(it, down, up, select):
                    if select:
                        keys_of, ids_of, gates = selection(it + 1)
                    if down:
                        for j in range(SLOTS):
                            if select and j % 8 == 4:
                                if j % 16 == 4:
                                    if j == 4:
                                        wait_loop(dve, ids_ready, it * 2 + 1)
                                    keys_of(j // 16)
                                else:
                                    ids_of(j // 16)
                            if j == 0:
                                wait_loop(dve, xcur_here, it + 1)
                                wait_loop(dve, gelu_done, it)
                            wait_loop(dve, gD[j % DRING], (it * (SLOTS // DRING) + j // DRING + 1) * 16)
                            dve.tensor_tensor_reduce(rowD[:, j % DRING, :], rowD[:, j % DRING, :], xcur, 1.0, 0.0,
                                                     ALU.mult, ALU.add, dots[:, j:j + 1]).then_inc(dot_done, 1)
                        if select:
                            gates()
                        wait_loop(dve, gelu_done, it + 1)
                        dve.tensor_tensor(coef, gel, gateD, ALU.mult).then_inc(coef_ready, 1)
                        wait_loop(dve, coef_ready, it + 1)
                        if select:
                            dve.tensor_copy(gateD, gateN.rearrange("p h k -> p (h k)")).then_inc(gates_moved, 1)
                            wait_loop(dve, gates_moved, it + 2)
                    if up:
                        wait_loop(dve, up_done, it * SLOTS)
                        wait_loop(dve, x1_here, it * 16)
                        wait_loop(dve, y_out, (it - 1) * 16)
                        dve.tensor_tensor(ybuf.rearrange("p (h n) -> p h n", h=2),
                                          x1cur.rearrange("p (h n) -> p h n", h=2), psum[:, 0:2, :], ALU.add)\
                           .then_inc(y_sum, 1)
                        wait_loop(dve, y_std, it)
                        dve.reciprocal(mrec, msq).then_inc(y_rec, 1)
                        wait_loop(dve, y_rec, it)
                        dve.scalar_tensor_tensor(out=ybuf, in0=ybuf, scalar=mrec, in1=gfb, op0=ALU.mult,
                                                 op1=ALU.mult).then_inc(y_ready, 1)

                dve.wait_ge(gf_here, 16)
                keys_of, ids_of, gates = selection(0)
                for h in range(HEADS):
                    keys_of(h)
                    ids_of(h)
                gates()
                dve.tensor_copy(gateD, gateN.rearrange("p h k -> p (h k)")).then_inc(gates_moved, 1)
                dve.wait_ge(gates_moved, 1)
                peel(step, dve)

            @block.scalar
            def _(act):
                def step(it, down, up, select):
                    if up:
                        wait_loop(act, coef_ready, it)
                        for j in range(SLOTS):
                            wait_loop(act, up_done, (it - 1) * SLOTS + max(j - 3, 0))
                            act.activation(diag[:, j % 4, :], ident, ACT.Copy, scale=coef[:, j:j + 1])\
                               .then_inc(diag_ready, 1)
                    if select:
                        wait_loop(act, sel, (it + 1) * SEL_OPS + SEL_OPS - 3)
                        act.activation(gateN, gateN, ACT.Exp).then_inc(sel_exp, 1)
                    if down:
                        wait_loop(act, dot_done, (it + 1) * SLOTS)
                        wait_loop(act, coef_ready, it)
                        act.activation(gel, dots, ACT.Gelu).then_inc(gelu_done, 1)
                        if select:
                            act.activation(xcur, xb[:, bass.ds(it + 1, 1), :].rearrange("p a d -> p (a d)"),
                                           ACT.Copy).then_inc(xcur_here, 1)
                            if not isinstance(it, int) or it + 2 < NT:
                                act.activation(scur.rearrange("p h c n -> p (h c n)"),
                                               scores_pad[:, bass.ds(it + 2, 1), :].rearrange("p a d -> p (a d)"),
                                               ACT.Copy).then_inc(scur_here, 1)
                    if up:
                        wait_loop(act, y_sum, it)
                        act.activation(x1cur, ybuf, ACT.Square, accum_out=msq).then_inc(y_sq, 1)
                        wait_loop(act, y_sq, it)
                        act.activation(msq, msq, ACT.Sqrt, bias=eps, scale=1.0 / D).then_inc(y_std, 1)

                scores_pad = at(16384, NT, HEADS * 2 * NKEYS)
                act.activation(scur.rearrange("p h c n -> p (h c n)"), scores_pad[:, 0, :], ACT.Copy)\
                   .then_inc(scur_here, 1)
                act.activation(xcur, xb[:, 0, :], ACT.Copy).then_inc(xcur_here, 1)
                act.wait_ge(sel, SEL_OPS - 3)
                act.activation(gateN, gateN, ACT.Exp).then_inc(sel_exp, 1)
                act.activation(scur.rearrange("p h c n -> p (h c n)"), scores_pad[:, 1, :], ACT.Copy)\
                   .then_inc(scur_here, 1)
                step(0, True, False, True)
                step(1, True, True, True)
                with act.Fori(2, NT - 2) as it:
                    step(it, True, True, True)
                step(NT - 2, True, True, True)
                step(NT - 1, True, True, False)
                step(NT, False, True, False)

            @block.tensor
            def _(pe):
                def step(it, down, up, select):
                    if not up:
                        return
                    if not isinstance(it, int) or it >= 2:
                        wait_loop(pe, y_sum, it - 1)
                    for j in range(SLOTS):
                        wait_loop(pe, gU[j % URING], ((it - 1) * (SLOTS // URING) + j // URING + 1) * 16)
                        wait_loop(pe, diag_ready, (it - 1) * SLOTS + j + 1)
                        for h in range(2):
                            mm = pe.matmul(psum[:, h, :], diag[:, j % 4, :], rowU[:, j % URING, h * 512:(h + 1) * 512],
                                           start=(j == 0), stop=(j == SLOTS - 1))
                        mm.then_inc(up_done, 1)
                peel(step, pe)

            @block.sync
            def _(sp):
                def step(it, down, up, select):
                    if not up:
                        return
                    first = isinstance(it, int) and it == 1
                    if not first:
                        wait_loop(sp, y_std, it - 1)
                    sp.dma_start(x1cur, scratch_x1[bass.ds((it - 1) * P, P), :]).then_inc(x1_here, 16)
                    wait_loop(sp, y_ready, it)
                    sp.dma_start(y_prompt[bass.ds((it - 1) * P, P), :], ybuf).then_inc(y_out, 16)

                sp.dma_start(gfb, bass.AP(tensor=gf.tensor, offset=gf.offset, ap=[[0, P], [1, D]])).then_inc(gf_here, 16)
                peel(step, sp)
                sp.wait_ge(y_out, 16 * NT)

        xbc = at(0, NB, D)
        ssc = at(16384, 2, NKEYS)
        idcols = at(16384 + 512, NB).bitcast(U32)
        gatecols = at(16384 + 528, NB)
        dcols = at(16384 + 544, NB)
        ccols = at(16384 + 560, NB)
        cmask = at(16384 + 576, NB, NB)
        ys = at(16384 + 1024, D)
        ysq = at(16384 + 2048, D)
        x1keep = at(16384 + 3072, D)
        ss_here = sem("sample_scores_here")
        sel2 = sem("sample_select_step")
        sx = sem("sample_select_exp")
        lists_out = sem("sample_lists_out")
        lists_in = sem("sample_lists_in")
        gS = [sem(f"sample_down_rows_here{i}") for i in range(NB)]
        gT = [sem(f"sample_up_rows_here{i}") for i in range(NB)]
        sdot = sem("sample_dots")
        sgel = sem("sample_gelu")
        smask = sem("sample_mask")
        sup = sem("sample_up")
        sy = sem("sample_y")
        sysq = sem("sample_y_squared")
        systd = sem("sample_y_std")
        R2 = NB * HEADS
        NSEL2 = 24 + 4

        with nc.Block() as block:
            @block.sync
            def _(sp):
                sp.dma_start(ssc[0:R2], scratch_sc.rearrange("r (c n) -> r c n", c=2)).then_inc(ss_here, 16)
                for b in range(NB):
                    sp.dma_start(xbc[:, b, :], bass.AP(tensor=scratch_xb.tensor, offset=b * D, ap=[[0, P], [1, D]]))\
                      .then_inc(ss_here, 16)
                sp.dma_start(x1keep[0:NB], scratch_x1[SEQ:T, :]).then_inc(ss_here, 16)
                sp.wait_ge(sel2, NSEL2)
                sp.dma_start(scratch_ids.rearrange("b (h k) -> (b h) k", h=HEADS), idN[0:R2, 0:TOPK])\
                  .then_inc(lists_out, 16)
                sp.dma_start(scratch_gate.rearrange("b (h k) -> (b h) k", h=HEADS), gateN[0:R2, 0, :])\
                  .then_inc(lists_out, 16)
                sp.wait_ge(lists_out, 32)
                with nc.allow_non_contiguous_dma("a list of 1024 words, turned"):
                    sp.dma_start(idcols, scratch_ids.rearrange("b s -> s b")).then_inc(lists_in, 16)
                    sp.dma_start(gatecols, scratch_gate.rearrange("b s -> s b")).then_inc(lists_in, 16)
                sp.wait_ge(sy, 5)
                store(sp, y_sample, ys[0:NB, :])

            @block.gpsimd
            def _(pool):
                pool.memset(cmask, 0.0).then_inc(smask, 1)
                pool.wait_ge(lists_in, 32)
                for b in range(NB):
                    pool.indirect_dma_start(rowD[:, b, :], None, w_down,
                                            bass.IndirectOffsetOnAxis(ap=idcols[:, b:b + 1], axis=0))\
                        .then_inc(gS[b], 16)
                for b in range(NB):
                    dst = rowU[:, b, :] if b < URING else rowD[:, b - URING, :]
                    if b >= URING:
                        pool.wait_ge(sdot, b - URING + 1)
                    pool.indirect_dma_start(dst, None, w_up,
                                            bass.IndirectOffsetOnAxis(ap=idcols[:, b:b + 1], axis=0))\
                        .then_inc(gT[b], 16)

            @block.vector
            def _(dve):
                k = [0]

                def link(ins):
                    k[0] += 1
                    ins.then_inc(sel2, 1)
                    dve.wait_ge(sel2, k[0])

                dve.wait_ge(ss_here, 16 * (NB + 2))
                select_head_keys(dve, link, R2, ssc[0:R2], sv[0:R2, 0], si[0:R2, 0])
                select_head_pairs(dve, link, R2, sv[0:R2, 0], best[0:R2, 0], ci[0:R2, 0])
                select_head_ids(dve, link, R2, si[0:R2, 0], sif[0:R2, 0], ci[0:R2, 0], ij[0:R2, 0], ijf[0:R2, 0],
                                pick[0:R2, 0], idN[0:R2, 0:TOPK])
                gg = gateN[0:R2, 0, :]
                link(dve.tensor_scalar(gg, best[0:R2, 0, :], best[0:R2, 0, 0:1], None, ALU.subtract))
                dve.wait_ge(sx, 1)
                link(dve.tensor_reduce(hsum[0:R2, 0:1], gg, AX.X, ALU.add))
                link(dve.reciprocal(hrec[0:R2, 0:1], hsum[0:R2, 0:1]))
                link(dve.tensor_scalar(gg, gg, hrec[0:R2, 0:1], None, ALU.mult))
                for b in range(NB):
                    dve.wait_ge(gS[b], 16)
                    dve.tensor_tensor_reduce(rowD[:, b, :], rowD[:, b, :], xbc[:, b, :], 1.0, 0.0, ALU.mult,
                                             ALU.add, dcols[:, b:b + 1]).then_inc(sdot, 1)
                dve.wait_ge(sgel, 1)
                dve.wait_ge(lists_in, 32)
                dve.tensor_tensor(ccols, ccols, gatecols, ALU.mult).then_inc(sgel, 1)
                dve.wait_ge(sgel, 2)
                dve.wait_ge(smask, 1)
                for b in range(NB):
                    dve.tensor_copy(cmask[:, b, b:b + 1], ccols[:, b:b + 1]).then_inc(smask, 1)
                dve.wait_ge(sup, NB)
                dve.tensor_tensor(ys[0:NB].rearrange("p (h n) -> p h n", h=2),
                                  x1keep[0:NB].rearrange("p (h n) -> p h n", h=2), psum[0:NB, 0:2, :], ALU.add)\
                   .then_inc(sy, 1)
                dve.wait_ge(systd, 1)
                dve.reciprocal(mrec[0:NB], msq[0:NB]).then_inc(sy, 1)
                dve.wait_ge(sy, 2)
                dve.scalar_tensor_tensor(out=ys[0:NB], in0=ys[0:NB], scalar=mrec[0:NB], in1=gfb[0:NB], op0=ALU.mult,
                                         op1=ALU.mult).then_inc(sy, 3)

            @block.scalar
            def _(act):
                act.wait_ge(sel2, 25)
                act.activation(gateN[0:R2, 0, :], gateN[0:R2, 0, :], ACT.Exp).then_inc(sx, 1)
                act.wait_ge(sdot, NB)
                act.activation(ccols, dcols, ACT.Gelu).then_inc(sgel, 1)
                act.wait_ge(sy, 1)
                act.activation(ysq[0:NB], ys[0:NB], ACT.Square, accum_out=msq[0:NB]).then_inc(sysq, 1)
                act.wait_ge(sysq, 1)
                act.activation(msq[0:NB], msq[0:NB], ACT.Sqrt, bias=eps[0:NB], scale=1.0 / D).then_inc(systd, 1)

            @block.tensor
            def _(pe):
                pe.wait_ge(smask, NB + 1)
                for b in range(NB):
                    src = rowU[:, b, :] if b < URING else rowD[:, b - URING, :]
                    pe.wait_ge(gT[b], 16)
                    for h in range(2):
                        mm = pe.matmul(psum[0:NB, h, :], cmask[:, b, :], src[:, h * 512:(h + 1) * 512],
                                       start=(b == 0), stop=(b == NB - 1))
                    mm.then_inc(sup, 1)

        with nc.Block() as block:
            @block.sync
            def _(sp):
                sp.wait_ge(stores, n_stores[0])


_NAMES = ["x_prompt", "x_sample", "xT", "memT", "w_chunks", "w_gates", "w_o", "w_q", "keysT", "bias_tab", "onehot",
          "sinks_bc", "sinks_s", "g1", "gm", "g2", "gf", "conv_w", "conv_b", "ln_g", "ln_b", "cacheT", "cache_conv",
          "cache_k", "cache_v", "cache_kT", "memkT", "cache_mv", "w_down", "w_up"]
_OUTS = [((SEQ, D), (1, SEQ, D)), ((NB, D), (NB, 1, D)), ((HALO, CH), (1, 1, HALO, CH)),
         ((WIN, P), (1, 1, WIN, 2, HD)), ((WIN, P), (1, 1, WIN, 2, HD)),
         ((MEM, CH), (1, 1, MEM, 4, P)), ((MEM, CH), (1, 1, MEM, 4, P)),
         ((NB, HALO, CH), (1, NB, HALO, CH)), ((NB, WIN, P), (1, NB, WIN, 2, HD)), ((NB, WIN, P), (1, NB, WIN, 2, HD))]


def bucket_rows():
    oh = np.zeros((33, LINE - 1), np.float32)
    for r in range(LINE - 1):
        dist = 2 * P - 1 - r
        if dist < 0 or dist > WIN:
            oh[32, r] = 1
        elif dist < 16:
            oh[dist, r] = 1
        else:
            oh[min(31, 16 + int(math.log(dist / 16) / math.log(128 / 16) * 16)), r] = 1
    return oh


def lay_out(x_prompt, x_sample, cache_conv, cache_swa_k, cache_swa_v, cache_mem_k, cache_mem_v, mem_prompt,
            rel_bias_table, norm1_g, w_in, conv_dw_w, conv_dw_b, conv_ln_g, conv_ln_b, w_conv_out, swa_sinks,
            w_swa_out, mem_norm_g, w_mem_kv, w_mem_out, w_out, norm2_g, peer_w_q, peer_keys, peer_w_down,
            peer_w_up, final_norm_g):
    xp, xs = x_prompt[0], x_sample[:, 0]

    def slices(w):
        return w.reshape(-1, P, w.shape[1]).transpose(1, 0, 2)

    w = w_in[0]
    q_cols = [np.r_[c * HD:(c + 1) * HD, (c + 4) * HD:(c + 5) * HD] for c in range(4)]
    q0, k0 = 2 * CH, 2 * CH + 512
    v0, m0, gate0 = k0 + P, k0 + 2 * P, k0 + 2 * P + 512
    start = {"a": 0, "b": CH, "k": k0, "v": v0, "qm": m0}
    chunks = []
    for kind, c in CHUNKS:
        if kind == "q":
            part = w[:, q0 + q_cols[c]]
        elif kind == "mem":
            part = w_mem_kv[0][:, c * P:(c + 1) * P]
        else:
            part = w[:, start[kind] + c * P:start[kind] + (c + 1) * P]
        chunks.append(slices(part))
    outs = [w_conv_out[0], w_swa_out[0][np.concatenate(q_cols)], w_mem_out[0]]
    gates = []
    for m in range(KD):
        for br in range(3):
            g = slices(w[:, gate0 + br * D + m * P:gate0 + br * D + (m + 1) * P])
            gates.append(np.concatenate([g, slices(outs[br][:, m * P:(m + 1) * P])], axis=1))
    order = [2 * hf + cc + 4 * j for hf in range(2) for j in range(2) for cc in range(2)]
    sinks = swa_sinks[0]
    return {
        "x_prompt": xp, "x_sample": xs,
        "xT": slices(np.concatenate([xp, xs]).T), "memT": slices(mem_prompt[0].T),
        "w_chunks": np.stack(chunks), "w_gates": np.stack(gates),
        "w_o": slices(w_out[0]), "w_q": slices(peer_w_q[0]),
        "keysT": peer_keys[0].transpose(1, 3, 0, 2).reshape(P, HEADS, NKEYS),
        "bias_tab": rel_bias_table[:, order], "onehot": bucket_rows(),
        "sinks_bc": np.broadcast_to(sinks[order], (P, 8)),
        "sinks_s": np.repeat(sinks.reshape(2, 4).T, NB, axis=0),
        "g1": norm1_g[0].reshape(KD, P).T, "gm": mem_norm_g[0].reshape(KD, P).T,
        "g2": norm2_g[0], "gf": final_norm_g,
        "conv_w": conv_dw_w[0].reshape(TAPS, NC, P).transpose(2, 1, 0),
        "conv_b": conv_dw_b[0].reshape(NC, P).T, "ln_g": conv_ln_g[0].reshape(NC, P).T,
        "ln_b": conv_ln_b[0].reshape(NC, P).T,
        "cacheT": cache_conv[0].transpose(2, 0, 1).reshape(NC, P, NB, HALO).transpose(1, 0, 2, 3),
        "cache_conv": cache_conv[0], "cache_k": cache_swa_k[0].reshape(NB, WIN, P),
        "cache_v": cache_swa_v[0].reshape(NB, WIN, P),
        "cache_kT": cache_swa_k[0].reshape(NB, WIN, P).transpose(2, 0, 1),
        "memkT": cache_mem_k[0].transpose(0, 3, 2, 1), "cache_mv": cache_mem_v[0].reshape(NB, MEM, CH),
        "w_down": peer_w_down[0], "w_up": peer_w_up[0],
    }


def kernel(**inputs):
    import concourse.bacc as bacc
    from concourse.bass_utils import run_bass_kernel_spmd

    laid = lay_out(**{k: np.asarray(v) for k, v in inputs.items()})
    nc = bacc.Bacc("TRN2", target_bir_lowering=False, num_devices=1)
    arrays, args = {}, []
    for name in _NAMES:
        a = np.ascontiguousarray(laid[name])
        arrays[f"in_{name}"] = a
        args.append(nc.dram_tensor(f"in_{name}", a.shape, mybir.dt.from_np(a.dtype), kind="ExternalInput").ap())
    for i, (shape, _) in enumerate(_OUTS):
        args.append(nc.dram_tensor(f"out_{i}", shape, F32, kind="ExternalOutput").ap())
    build_kernel(nc, *args)
    r = run_bass_kernel_spmd(nc, [arrays], core_ids=[0])
    return tuple(r.results[0][f"out_{i}"].reshape(full) for i, (_, full) in enumerate(_OUTS))
```

```python
from contextlib import ExitStack

import concourse.bass as bass
from concourse import mybir
import math
import numpy as np

ALU = mybir.AluOpType
ACT = mybir.ActivationFunctionType
AX = mybir.AxisListType
F32 = mybir.dt.float32
U32 = mybir.dt.uint32

P = 128
D = 1024
SEQ = 1024
NB = 8
T = SEQ + NB
KD = D // P
NT = SEQ // P
GC = T // 3
MEM = 256
CH = 512
NC = CH // P
TAPS = 31
HALO = TAPS - 1
WIN = 128
HD = 64
SCALE = HD ** -0.5
MSCALE = 128 ** -0.5
NEG = -1e30
EPS = 1e-6
LINE = 384
HEADS = 8
TOPK = 16
SLOTS = HEADS * TOPK
NKEYS = 128
LOW = -3.0e38

CHUNKS = [("b", 0), ("a", 0), ("b", 1), ("a", 1), ("b", 2), ("a", 2), ("b", 3), ("a", 3), ("k", 0), ("v", 0)] + \
         [("q", c) for c in range(4)] + [("qm", c) for c in range(4)] + [("mem", c) for c in range(8)]
WRING = 6
DRING = 8
URING = 4
SEL_OPS = HEADS * 24 + 4


def build_kernel(nc, x_prompt, x_sample, xT, memT, w_chunks, w_gates, w_o, w_q, keysT, bias_tab, onehot, sinks_bc,
                 sinks_s, g1, gm, g2, gf, conv_w, conv_b, ln_g, ln_b, cacheT, cache_conv, cache_k, cache_v,
                 cache_kT, memkT, cache_mv, w_down, w_up,
                 y_prompt, y_sample, conv_p, k_p, v_p, mk_p, mv_p, conv_s, k_s, v_s):
    scratch_line = nc.dram_tensor("scratch_line", (HEADS, LINE), F32, kind="Internal").ap()
    scratch_vs = nc.dram_tensor("scratch_vs", (NB, P), F32, kind="Internal").ap()
    scratch_x1 = nc.dram_tensor("scratch_x1", (T, D), F32, kind="Internal").ap()
    scratch_xb = nc.dram_tensor("scratch_xb", (NB, D), F32, kind="Internal").ap()
    scratch_sc = nc.dram_tensor("scratch_sc", (NB * HEADS, 2 * NKEYS), F32, kind="Internal").ap()
    scratch_ids = nc.dram_tensor("scratch_ids", (NB, SLOTS), U32, kind="Internal").ap()
    scratch_gate = nc.dram_tensor("scratch_gate", (NB, SLOTS), F32, kind="Internal").ap()

    with ExitStack() as ctx:
        arena = ctx.enter_context(nc.sbuf_tensor("arena", [P, 52100], F32))
        consts = ctx.enter_context(nc.sbuf_tensor("constants", [P, 1000], F32))
        psum = ctx.enter_context(nc.psum_tensor("psum", [P, 8, 512], F32))

        def sem(name):
            return ctx.enter_context(nc.semaphore(name))

        def at(offset, *shape):
            n = math.prod(shape)
            v = arena[:, offset:offset + n]
            names = "abcde"[:len(shape)]
            if len(shape) > 1:
                v = v.rearrange(f"p ({' '.join(names)}) -> p {' '.join(names)}",
                                **{n: s for n, s in zip(names, shape)})
            return v

        ident = consts[:, 0:128]
        ones = consts[:, 128:256]
        eps = consts[:, 256:257]
        g1s, gms = consts[:, 257:265], consts[:, 265:273]
        cw = consts[:, 273:273 + NC * TAPS].rearrange("p (c t) -> p c t", c=NC)
        cb, lng, lnb = consts[:, 400:404], consts[:, 404:408], consts[:, 408:412]
        sink = consts[:, 412:420]
        sink_s = consts[:, 420:422]
        iota16 = consts[:, 432:448]
        small = consts[:, 448:1000]

        hT = at(0, KD, T)
        uT = at(8256, NC, HALO + T)
        yT = at(12504, NC, T)
        qT = at(16632, NC, T)
        kT = at(20760, P + T)
        vN = at(21920, NT + 2, P)
        qmT = at(23200, NC, T)
        memN = at(27328, 2, 8 * P)
        memKT = at(29376, NC, MEM)
        kN = at(30400, 2, P)
        lastu = at(30656, NC, P)
        us = at(31168, NC, NB, TAPS)
        MG = 32768
        mergedT = at(MG, KD, T)
        RG = MG + KD * T

        initialised = sem("initialised")
        loads = sem("loads")

        passed = sem("loop_waits_passed")

        def wait_loop(eng, sem, value):
            if isinstance(value, int) and value <= 0:
                return
            eng.wait_ge(sem, value)
            if not isinstance(value, int):
                eng.sem_inc(passed, 1)

        stores = sem("stores")
        n_stores = [0]

        def store(eng, dst, src):
            n_stores[0] += 16
            eng.dma_start(dst, src).then_inc(stores, 16)

        sq = at(MG, 2, T)
        sig = at(MG + 2 * T, 2, T)
        mT = at(MG + 4 * T, KD, MEM)
        std = at(RG + WRING * 1024, T)
        stdm = at(RG + WRING * 1024 + T, MEM)
        prod = at(RG + WRING * 1024 + T + MEM, NB, TAPS)
        wr = at(RG, WRING, KD, P)

        w_here = [sem(f"weights_here{i}") for i in range(WRING)]
        squared = sem("squared")
        summed = sem("summed")
        std_ready = sem("std_ready")
        h_ready = sem("h_ready")
        chunk_done = sem("chunk_done")
        set_free = [sem("psum_set0_free"), sem("psum_set1_free")]
        sig_ready = sem("sig_ready")
        dve1 = sem("dve1")
        cache_here = sem("conv_cache_here")
        padded = sem("padded")

        def groups(s):
            return psum[:, 3 * s:3 * s + 3, 0:GC]

        with nc.Block() as block:
            @block.sync
            def _(sp):
                for dst, src in ((mT, memT), (g1s, g1), (gms, gm), (cw, conv_w), (cb, conv_b), (lng, ln_g),
                                 (lnb, ln_b), (sink, sinks_bc), (sink_s[0:32, :], sinks_s)):
                    sp.dma_start(dst, src).then_inc(loads, 16)
                sp.dma_start(hT[:, 0:4, :], xT[:, 0:4, :]).then_inc(loads, 16)
                sp.dma_start(hT[:, 4:8, :], xT[:, 4:8, :]).then_inc(loads, 16)
                for i in range(len(CHUNKS)):
                    if i == WRING:
                        for c in range(NC):
                            sp.dma_start(us[:, c, :, 0:HALO], cacheT[:, c]).then_inc(cache_here, 16)
                    if i >= WRING:
                        sp.wait_ge(chunk_done, i - WRING + 1)
                    sp.dma_start(wr[:, i % WRING], w_chunks[i]).then_inc(w_here[i % WRING], 16)
                store(sp, conv_s[:, 0:HALO - 1, :], cache_conv[:, 1:HALO, :])
                store(sp, k_s[:, 0:WIN - 1, :], cache_k[:, 1:WIN, :])
                store(sp, v_s[:, 0:WIN - 1, :], cache_v[:, 1:WIN, :])

            @block.gpsimd
            def _(pool):
                pool.memset(ident, 0.0).then_inc(initialised, 1)
                pool.memset(ones, 1.0).then_inc(initialised, 1)
                pool.memset(eps, EPS).then_inc(initialised, 1)
                pool.iota(iota16, [[1, TOPK]], base=0, channel_multiplier=0,
                          allow_small_or_imprecise_dtypes=True).then_inc(initialised, 1)
                pool.wait_ge(initialised, 4)
                pool.affine_select(out=ident, in_=ident, compare_op=ALU.not_equal, fill=1.0, base=0,
                                   pattern=[[-1, P]], channel_multiplier=1).then_inc(initialised, 1)
                pool.memset(uT[:, :, 0:HALO], 0.0).then_inc(padded, 1)
                pool.memset(kT[:, 0:P], 0.0).then_inc(padded, 1)
                pool.memset(vN[:, 0, :], 0.0).then_inc(padded, 1)

            @block.scalar
            def _(act):
                act.wait_ge(initialised, 5)
                act.wait_ge(loads, 16 * 11)
                for k in range(2 * KD):
                    if k >= 2:
                        act.wait_ge(summed, k - 1)
                    src = hT[:, k, :] if k < KD else mT[:, k - KD, :]
                    act.activation(sq[:, k % 2, 0:src.shape[1]], src, ACT.Square).then_inc(squared, 1)
                act.wait_ge(summed, 2 * KD)
                act.activation(std.rearrange("p (g n) -> p g n", g=3), groups(0), ACT.Sqrt, bias=eps,
                               scale=1.0 / D).then_inc(std_ready, 1)
                act.activation(stdm, psum[:, 3, 0:MEM], ACT.Sqrt, bias=eps, scale=1.0 / D).then_inc(std_ready, 1)
                for i, (kind, c) in enumerate(CHUNKS):
                    if kind == "a":
                        continue
                    act.wait_ge(chunk_done, i + 1)
                    src = groups(i % 2)
                    if kind == "b":
                        if c >= 2:
                            act.wait_ge(set_free[1], c - 1)
                        act.activation(sig[:, c % 2, :].rearrange("p (g n) -> p g n", g=3), src, ACT.Sigmoid)\
                           .then_inc(sig_ready, 1)
                        act.wait_ge(sig_ready, c + 1)
                        act.sem_inc(set_free[0], 1)
                        continue
                    if kind == "k":
                        act.activation(kN[:, 0, :], psum[:, 6, 0:P], ACT.Copy)
                        act.activation(kN[0:NB, 1, :], psum[0:NB, 6, P:2 * P], ACT.Copy)
                        dst = kT[:, P:P + T].rearrange("p (g n) -> p g n", g=3)
                    elif kind == "v":
                        for b in range(2):
                            act.activation(vN[:, 1 + 4 * b:5 + 4 * b, :],
                                           psum[:, 3 * (i % 2) + b, :].rearrange("p (t n) -> p t n", n=P), ACT.Copy)
                        dst, src = vN[0:NB, NT + 1, :], psum[0:NB, 3 * (i % 2) + 2, 0:P]
                    elif kind == "mem":
                        dst, src = memN[:, :, c * P:(c + 1) * P], psum[:, 3 * (i % 2):3 * (i % 2) + 2, 0:P]
                    else:
                        dst = (qT if kind == "q" else qmT)[:, c, :].rearrange("p (g n) -> p g n", g=3)
                    act.activation(dst, src, ACT.Copy).then_inc(set_free[i % 2], 1)

            @block.tensor
            def _(pe):
                pe.wait_ge(initialised, 5)
                for k in range(2 * KD):
                    pe.wait_ge(squared, k + 1)
                    if k < KD:
                        for g in range(3):
                            mm = pe.matmul(psum[:, g, 0:GC], ones, sq[:, k % 2, g * GC:(g + 1) * GC],
                                           start=(k == 0), stop=(k == KD - 1))
                    else:
                        mm = pe.matmul(psum[:, 3, 0:MEM], ones, sq[:, k % 2, 0:MEM],
                                       start=(k == KD), stop=(k == 2 * KD - 1))
                    mm.then_inc(summed, 1)
                for i, (kind, c) in enumerate(CHUNKS):
                    pe.wait_ge(w_here[i % WRING], 16 * (i // WRING + 1))
                    if i >= 2:
                        pe.wait_ge(set_free[i % 2], i // 2)
                    w = wr[:, i % WRING]
                    s = 3 * (i % 2)
                    for k in range(KD):
                        if i == 0:
                            pe.wait_ge(h_ready, k + 1)
                        first, last = k == 0, k == KD - 1
                        if kind in ("a", "b", "k", "q", "qm"):
                            for g in range(3):
                                mm = pe.matmul(psum[:, s + g, 0:GC], w[:, k, :], hT[:, k, g * GC:(g + 1) * GC],
                                               start=first, stop=last)
                    if kind == "k":
                        for k in range(KD):
                            pe.matmul(psum[:, 6, 0:P], hT[:, k, SEQ - P:SEQ], w[:, k, :],
                                      start=(k == 0), stop=(k == KD - 1))
                        for k in range(KD):
                            mm = pe.matmul(psum[0:NB, 6, P:2 * P], hT[:, k, SEQ:T], w[:, k, :],
                                           start=(k == 0), stop=(k == KD - 1))
                    if kind == "v":
                        for t in range(NT):
                            for k in range(KD):
                                pe.matmul(psum[:, s + t // 4, (t % 4) * P:(t % 4 + 1) * P],
                                          hT[:, k, t * P:(t + 1) * P], w[:, k, :],
                                          start=(k == 0), stop=(k == KD - 1))
                        for k in range(KD):
                            mm = pe.matmul(psum[0:NB, s + 2, 0:P], hT[:, k, SEQ:T], w[:, k, :],
                                           start=(k == 0), stop=(k == KD - 1))
                    if kind == "mem":
                        if c == 0:
                            pe.wait_ge(h_ready, 2 * KD)
                        for t in range(2):
                            for k in range(KD):
                                mm = pe.matmul(psum[:, s + t, 0:P], mT[:, k, t * P:(t + 1) * P], w[:, k, :],
                                               start=(k == 0), stop=(k == KD - 1))
                    mm.then_inc(chunk_done, 1)

            @block.vector
            def _(dve):
                n = [0]

                def link(ins):
                    n[0] += 1
                    ins.then_inc(dve1, 1)
                    dve.wait_ge(dve1, n[0])

                dve.wait_ge(std_ready, 2)
                link(dve.reciprocal(std, std))
                for k in range(KD):
                    dve.scalar_tensor_tensor(out=hT[:, k, :], in0=hT[:, k, :], scalar=g1s[:, k:k + 1], in1=std,
                                             op0=ALU.mult, op1=ALU.mult).then_inc(h_ready, 1)
                link(dve.reciprocal(stdm, stdm))
                for k in range(KD):
                    dve.scalar_tensor_tensor(out=mT[:, k, :], in0=mT[:, k, :], scalar=gms[:, k:k + 1], in1=stdm,
                                             op0=ALU.mult, op1=ALU.mult).then_inc(h_ready, 1)
                for c in range(NC):
                    dve.wait_ge(chunk_done, 2 * c + 2)
                    dve.wait_ge(sig_ready, c + 1)
                    dve.tensor_tensor(uT[:, c, HALO:HALO + T].rearrange("p (g n) -> p g n", g=3), groups(1),
                                      sig[:, c % 2, :].rearrange("p (g n) -> p g n", g=3), ALU.mult)\
                       .then_inc(set_free[1], 1)
                dve.wait_ge(padded, 3)
                dve.wait_ge(set_free[1], NC)
                dve.wait_ge(cache_here, 16 * NC)
                for c in range(NC):
                    acc = yT[:, c, 0:SEQ]
                    link(dve.tensor_scalar(acc, uT[:, c, 0:SEQ], cw[:, c, 0:1], cb[:, c:c + 1], ALU.mult, ALU.add))
                    for t in range(1, TAPS):
                        link(dve.scalar_tensor_tensor(out=acc, in0=uT[:, c, t:t + SEQ], scalar=cw[:, c, t:t + 1],
                                                      in1=acc, op0=ALU.mult, op1=ALU.add))
                    link(dve.tensor_copy(us[:, c, :, HALO], uT[:, c, HALO + SEQ:HALO + T]))
                    link(dve.tensor_tensor(prod, us[:, c], cw[:, c, :].unsqueeze(1).broadcast_to([P, NB, TAPS]),
                                           ALU.mult))
                    link(dve.tensor_reduce(yT[:, c, SEQ:T], prod, AX.X, ALU.add))
                    link(dve.tensor_scalar(yT[:, c, SEQ:T], yT[:, c, SEQ:T], cb[:, c:c + 1], None, ALU.add))

        lsum = sem("ln_summed")
        lcent = sem("ln_centred")
        lsq = sem("ln_squared")
        lvar = sem("ln_variance")
        lstd = sem("ln_std")
        lrec = sem("ln_reciprocal")
        lnorm = sem("ln_normed")
        lsilu = sem("ln_silu")
        turned_u = sem("conv_rows_turned")
        u_rows = sem("conv_rows_here")
        sq4 = at(MG, 3, NC, GC)
        lnstd = at(MG + 3 * NC * GC, 3, GC)
        lastsu = at(RG, NC, P)

        with nc.Block() as block:
            @block.tensor
            def _(pe):
                for g in range(3):
                    for c in range(NC):
                        mm = pe.matmul(psum[:, g, 0:GC], ones, yT[:, c, g * GC:(g + 1) * GC],
                                       start=(c == 0), stop=(c == NC - 1))
                    mm.then_inc(lsum, 1)
                for c in range(NC):
                    pe.transpose(psum[0:HALO, 6, c * P:(c + 1) * P], uT[:, c, SEQ:SEQ + HALO], ident)
                for c in range(NC):
                    mm = pe.transpose(psum[0:NB, 7, c * P:(c + 1) * P], uT[:, c, HALO + SEQ:HALO + T], ident)
                mm.then_inc(turned_u, 1)
                for g in range(3):
                    pe.wait_ge(lsq, NC * (g + 1))
                    for c in range(NC):
                        mm = pe.matmul(psum[:, 3 + g, 0:GC], ones, sq4[:, g, c, :],
                                       start=(c == 0), stop=(c == NC - 1))
                    mm.then_inc(lvar, 1)

            @block.vector
            def _(dve):
                for g in range(3):
                    dve.wait_ge(lsum, g + 1)
                    for c in range(NC):
                        y = yT[:, c, g * GC:(g + 1) * GC]
                        dve.scalar_tensor_tensor(out=y, in0=psum[:, g, 0:GC], scalar=-1.0 / CH, in1=y,
                                                 op0=ALU.mult, op1=ALU.add).then_inc(lcent, 1)
                dve.wait_ge(lcent, 3 * NC)
                for g in range(3):
                    dve.wait_ge(lstd, g + 1)
                    dve.reciprocal(lnstd[:, g, :], lnstd[:, g, :]).then_inc(lrec, 1)
                    dve.wait_ge(lrec, g + 1)
                    for c in range(NC):
                        y = yT[:, c, g * GC:(g + 1) * GC]
                        dve.tensor_tensor(y, y, lnstd[:, g, :], ALU.mult).then_inc(lnorm, 1)

            @block.scalar
            def _(act):
                for g in range(3):
                    for c in range(NC):
                        act.wait_ge(lcent, g * NC + c + 1)
                        act.activation(sq4[:, g, c, :], yT[:, c, g * GC:(g + 1) * GC], ACT.Square).then_inc(lsq, 1)
                act.wait_ge(turned_u, 1)
                act.activation(lastu[0:HALO], psum[0:HALO, 6, :].rearrange("p (c n) -> p c n", c=NC), ACT.Copy)\
                   .then_inc(u_rows, 1)
                act.activation(lastsu[0:NB], psum[0:NB, 7, :].rearrange("p (c n) -> p c n", c=NC), ACT.Copy)\
                   .then_inc(u_rows, 1)
                for g in range(3):
                    act.wait_ge(lvar, g + 1)
                    act.activation(lnstd[:, g, :], psum[:, 3 + g, 0:GC], ACT.Sqrt, bias=eps, scale=1.0 / CH)\
                       .then_inc(lstd, 1)
                for g in range(3):
                    for c in range(NC):
                        y = yT[:, c, g * GC:(g + 1) * GC]
                        act.wait_ge(lnorm, g * NC + c + 1)
                        act.activation(y, y, ACT.Silu, bias=lnb[:, c:c + 1], scale=lng[:, c:c + 1])\
                           .then_inc(lsilu, 1)

            @block.sync
            def _(sp):
                sp.wait_ge(u_rows, 2)
                store(sp, conv_p, lastu[0:HALO].rearrange("p c n -> p (c n)"))
                store(sp, conv_s[:, HALO - 1, :], lastsu[0:NB].rearrange("p c n -> p (c n)"))
                store(sp, k_p, kN[:, 0, :])
                store(sp, k_s[:, WIN - 1, :], kN[0:NB, 1, :])
                store(sp, v_p, vN[:, NT, :])
                store(sp, v_s[:, WIN - 1, :], vN[0:NB, NT + 1, :])
                for t in range(2):
                    store(sp, mk_p[t * P:(t + 1) * P, :], memN[:, t, 0:CH])
                    store(sp, mv_p[t * P:(t + 1) * P, :], memN[:, t, CH:2 * CH])
                sp.wait_ge(stores, n_stores[0])

        bias = at(MG, HEADS, 2 * P)
        bias0 = at(MG + 2048, HEADS, 2 * P)
        prob = at(MG + 4096, 2, 4, 2 * P)
        probT = at(MG + 6144, 2, 8, P)
        oh = at(RG, LINE)
        tab = at(RG + LINE, HEADS)
        line = at(RG + LINE + HEADS, LINE)
        Q0 = RG + 800
        kring = at(Q0, 2, NC, MEM)
        vring = at(Q0 + 2048, 2, 2, CH)
        ck = at(Q0 + 4096, NB, WIN + 1)
        cv = at(Q0 + 5128, NB, P)
        qmask = at(Q0 + 6152, NB, 32)
        qmmask = at(Q0 + 6408, 32, 32)
        ps_ = at(Q0 + 7432, 2, WIN + 1)
        psm = at(Q0 + 7690, MEM)
        pst = at(Q0 + 7946, 2, 32)
        pslast = at(Q0 + 8010, 2, 32)
        pmt = at(Q0 + 8074, 2, 32)
        vlast = at(Q0 + 8138, NB, P)
        bias_s = at(Q0 + 9162, 2, WIN + 1)
        flipped = at(MG + 4096, HEADS, 2 * P)
        flip = at(Q0 + 9420, P)
        stat = small[:, 0:320]
        units = [("swa", n, h) for n in range(NT) for h in range(2)] + [("mem", n, 0) for n in range(NT)]
        NU = len(units)
        mx, nm, rs, es, rd = (stat[:, 8 * i:8 * i + 8].rearrange("p (b h) -> p b h", b=2) for i in range(5))
        mxs, nms, rss, ess, rds = (stat[:, 40 + 2 * i:42 + 2 * i] for i in range(5))
        mxm, nmm, rsm, rdm = (stat[:, 50 + i:51 + i] for i in range(4))

        tab_here = sem("bias_table_here")
        tab_fill = sem("bias_table_filled")
        line_mm = sem("line_multiplied")
        line_ready = sem("line_ready")
        line_out = sem("line_out")
        bias_here = sem("flipped_bias_here")
        bias_s_here = sem("sample_bias_here")
        unflipped = sem("bias_unflipped")
        bias_ready = sem("bias_ready")
        s_done = sem("scores_done")
        pre_done = sem("maxima_done")
        exp_done = sem("exp_done")
        norm_done = sem("probs_normed")
        t_done = sem("probs_turned")
        tev_done = sem("turned_probs_copied")
        pv_done = sem("pv_done")
        o_done = sem("attention_copied")
        mk_turned = sem("mem_k_turned")
        mk_copied = sem("mem_k_copied")
        dve2 = sem("dve2")
        smp_in = sem("sample_swa_cache_here")
        vs_out = sem("vs_out")
        kr_here = [sem("mem_k0_here"), sem("mem_k1_here")]
        vr_here = [sem("mem_v0_here"), sem("mem_v1_here")]
        masked = sem("queries_masked")
        ss_done = sem("sample_scores_done")
        kr_used = sem("mem_k_used")
        vr_used = sem("mem_v_used")
        smax = sem("sample_maxima")
        sexp = sem("sample_exp")
        snorm = sem("sample_normed")
        sturn = sem("sample_turned")
        scopy = sem("sample_copied")
        spv = sem("sample_pv")
        so = sem("sample_attention_copied")

        with nc.Block() as block:
            @block.sync
            def _(sp):
                sp.dma_start(oh[0:33, 0:LINE - 1], onehot).then_inc(tab_here, 16)
                sp.dma_start(tab[0:32, :], bias_tab).then_inc(tab_here, 16)
                sp.dma_start(scratch_vs, vN[0:NB, NT + 1, :]).then_inc(vs_out, 16)
                sp.dma_start(ck[:, :, 0:WIN], cache_kT).then_inc(smp_in, 16)
                sp.dma_start(cv, cache_v.rearrange("b w d -> w b d")).then_inc(smp_in, 16)
                sp.wait_ge(line_ready, 1)
                sp.dma_start(scratch_line[:, 0:LINE - 1], line[0:HEADS, 0:LINE - 1]).then_inc(line_out, 16)
                sp.wait_ge(line_out, 16)
                skew = bass.AP(tensor=scratch_line.tensor, offset=0, ap=[[1, P], [LINE, HEADS], [1, 2 * P]])
                sp.dma_start(flipped, skew).then_inc(bias_here, 16)
                for c in range(4):
                    src = bass.AP(tensor=scratch_line.tensor, offset=((c // 2) * 4 + c % 2) * LINE + P - 1,
                                  ap=[[0, NB], [2 * LINE, 2], [1, WIN + 1]])
                    sp.dma_start(bias_s[c * NB:(c + 1) * NB], src).then_inc(bias_s_here, 16)
                sp.wait_ge(vs_out, 16)
                sp.dma_start(vlast[0:1], scratch_vs.rearrange("(o b) d -> o b d", o=1)).then_inc(smp_in, 16)
                for b in range(NB):
                    if b >= 2:
                        sp.wait_ge(kr_used, b - 1)
                    sp.dma_start(kring[:, b % 2], memkT[b]).then_inc(kr_here[b % 2], 16)
                for b in range(NB):
                    if b >= 2:
                        sp.wait_ge(vr_used, b - 1)
                    sp.dma_start(vring[:, b % 2], cache_mv[b].rearrange("(t p) n -> p t n", p=P))\
                      .then_inc(vr_here[b % 2], 16)

            @block.gpsimd
            def _(pool):
                pool.memset(tab[32:33, :], NEG).then_inc(tab_fill, 1)
                pool.wait_ge(tab_fill, 1)
                pool.memset(flip, 0.0).then_inc(tab_fill, 1)
                pool.wait_ge(tab_fill, 2)
                pool.affine_select(out=flip, in_=flip, compare_op=ALU.not_equal, fill=1.0, base=-(P - 1),
                                   pattern=[[1, P]], channel_multiplier=1).then_inc(tab_fill, 1)
                pool.memset(bias0[:, :, 0:P], NEG).then_inc(bias_ready, 1)
                pool.memset(qmask, 0.0).then_inc(masked, 1)
                pool.memset(qmmask, 0.0).then_inc(masked, 1)
                pool.wait_ge(masked, 2)
                for c in range(NC):
                    qm_d = bass.AP(tensor=arena.ap().tensor if callable(arena.ap) else arena, offset=Q0 + 6152 + c * NB,
                                   ap=[[52100, P], [33, NB]])
                    pool.tensor_copy(qm_d, qT[:, c, SEQ:T]).then_inc(masked, 1)
                    qmm_d = bass.AP(tensor=arena.ap().tensor if callable(arena.ap) else arena,
                                    offset=Q0 + 6408 + 33 * c * NB, ap=[[52100, P], [33, NB]])
                    pool.tensor_copy(qmm_d, qmT[:, c, SEQ:T]).then_inc(masked, 1)
                pool.wait_ge(smp_in, 48)
                pool.tensor_copy(ck[:, :, WIN], kT[:, P + SEQ:P + T]).then_inc(masked, 1)

            @block.tensor
            def _(pe):
                pe.wait_ge(tab_here, 32)
                pe.wait_ge(tab_fill, 1)
                pe.matmul(psum[0:HEADS, 7, 0:LINE - 1], tab[0:33, :], oh[0:33, 0:LINE - 1], start=True, stop=True)\
                  .then_inc(line_mm, 1)
                for t in range(2):
                    for h in range(NC):
                        mm = pe.transpose(psum[:, 4 + t, h * P:(h + 1) * P], memN[:, t, h * P:(h + 1) * P], ident)
                mm.then_inc(mk_turned, 1)
                pe.wait_ge(bias_here, 16)
                pe.wait_ge(tab_fill, 3)
                for h in range(HEADS):
                    mm = pe.matmul(psum[:, h // 2, (h % 2) * 256:(h % 2) * 256 + 256], flip, flipped[:, h, :],
                                   start=True, stop=True)
                mm.then_inc(unflipped, 1)
                pe.wait_ge(mk_copied, 2)
                pe.wait_ge(bias_ready, 3)
                for s in range(NU + 2):
                    if s < NU:
                        kind, n, hf = units[s]
                        if s >= 2:
                            pe.wait_ge(pre_done if kind == "swa" or units[s - 2][0] == "swa" else exp_done, s - 1)
                            if kind == "mem":
                                pe.wait_ge(exp_done, s - 1)
                        S = psum[:, 2 * (s % 2):2 * (s % 2) + 2, :].rearrange("p b (h k) -> p (b h) k", k=2 * P)
                        for i in range(4):
                            if kind == "swa":
                                j, c = i // 2, 2 * hf + i % 2
                                rows = slice(64 * j, 64 * j + 64)
                                mm = pe.matmul(S[:, i, :], qT[rows, c, n * P:(n + 1) * P],
                                               kT[rows, n * P:n * P + 2 * P], start=True, stop=True)
                            else:
                                mm = pe.matmul(S[:, i, :], qmT[:, i, n * P:(n + 1) * P], memKT[:, i, :],
                                               start=True, stop=True)
                        mm.then_inc(s_done, 1)
                    if 1 <= s <= NU:
                        u = s - 1
                        pe.wait_ge(norm_done, u + 1)
                        if u >= 1:
                            pe.wait_ge(tev_done, u)
                        for i in range(8):
                            mm = pe.transpose(psum[:, 4 + i // 4, (i % 4) * P:(i % 4 + 1) * P],
                                              prob[:, u % 2, i // 2, (i % 2) * P:(i % 2 + 1) * P], ident)
                        mm.then_inc(t_done, 1)
                    if s >= 2:
                        u = s - 2
                        kind, n, hf = units[u]
                        pe.wait_ge(tev_done, u + 1)
                        if u >= 1:
                            pe.wait_ge(o_done, u)
                        for i in range(4):
                            for kt in range(2):
                                pt = probT[:, u % 2, 2 * i + kt, :]
                                if kind == "swa":
                                    j, cc = i // 2, i % 2
                                    mm = pe.matmul(psum[64 * j:64 * j + 64, 6, cc * P:(cc + 1) * P],
                                                   vN[:, n + kt, 64 * j:64 * j + 64], pt, start=(kt == 0), stop=(kt == 1))
                                else:
                                    mm = pe.matmul(psum[:, 6, i * P:(i + 1) * P],
                                                   memN[:, kt, CH + i * P:CH + (i + 1) * P], pt,
                                                   start=(kt == 0), stop=(kt == 1))
                        mm.then_inc(pv_done, 1)
                pe.wait_ge(masked, 11)
                pe.wait_ge(norm_done, NU)
                for j in range(2):
                    rows = slice(64 * j, 64 * j + 64)
                    for b in range(NB):
                        mm = pe.matmul(psum[0:32, j, 0:WIN + 1], qmask[rows, b, :], ck[rows, b, :],
                                       start=(b == 0), stop=(b == NB - 1))
                mm.then_inc(ss_done, 1)
                for b in range(NB):
                    pe.wait_ge(kr_here[b % 2], 16 * (b // 2 + 1))
                    for h in range(NC):
                        mm = pe.matmul(psum[0:32, 2, 0:MEM], qmmask[:, h * NB + b, :], kring[:, b % 2, h, :],
                                       start=(b == 0 and h == 0), stop=(b == NB - 1 and h == NC - 1))
                    mm.then_inc(kr_used, 1)
                pe.wait_ge(snorm, 2)
                pe.wait_ge(tev_done, NU)
                for j in range(2):
                    pe.transpose(psum[:, 4, j * 32:(j + 1) * 32], ps_[0:32, j, 0:WIN], ident[0:32, 0:32])
                for j in range(2):
                    pe.transpose(psum[:, 4, 64 + j * 32:64 + (j + 1) * 32], psm[0:32, j * P:(j + 1) * P],
                                 ident[0:32, 0:32])
                for j in range(2):
                    mm = pe.transpose(psum[0:1, 5, j * 32:(j + 1) * 32], ps_[0:32, j, WIN:WIN + 1],
                                      ident[0:32, 0:32])
                mm.then_inc(sturn, 1)
                pe.wait_ge(scopy, 3)
                pe.wait_ge(smp_in, 48)
                pe.wait_ge(o_done, NU)
                for b in range(NB):
                    for j in range(2):
                        o = psum[64 * j:64 * j + 64, 6, 0:32].rearrange("p (c b) -> p c b", b=NB)[:, :, b]
                        w = pst[:, j, :].rearrange("p (c b) -> p c b", b=NB)[:, :, b]
                        wl = pslast[0:1, j, :].rearrange("p (c b) -> p c b", b=NB)[:, :, b]
                        pe.matmul(o, cv[:, b, 64 * j:64 * j + 64], w, start=True, stop=False)
                        mm = pe.matmul(o, vlast[0:1, b, 64 * j:64 * j + 64], wl, start=False, stop=True)
                mm.then_inc(spv, 1)
                for b in range(NB):
                    pe.wait_ge(vr_here[b % 2], 16 * (b // 2 + 1))
                    for h in range(NC):
                        r = h * NB + b
                        for t in range(2):
                            mm = pe.matmul(psum[:, 7, r:r + 1], vring[:, b % 2, t, h * P:(h + 1) * P],
                                           pmt[:, t, r:r + 1], start=(t == 0), stop=(t == 1))
                    mm.then_inc(vr_used, 1)

            @block.vector
            def _(dve):
                n_ = [0]

                def link(ins):
                    n_[0] += 1
                    ins.then_inc(dve2, 1)
                    dve.wait_ge(dve2, n_[0])

                dve.wait_ge(unflipped, 1)
                dve.wait_ge(bias_ready, 3)
                for s in range(NU + 1):
                    if s < NU:
                        kind, n, hf = units[s]
                        b = s % 2
                        S = psum[:, 2 * b:2 * b + 2, :].rearrange("p b (h k) -> p (b h) k", k=2 * P)
                        dve.wait_ge(s_done, s + 1)
                        if s >= 2:
                            dve.wait_ge(t_done, s - 1)
                        if kind == "swa":
                            bb = (bias if n else bias0)[:, 4 * hf:4 * hf + 4, :]
                            link(dve.scalar_tensor_tensor(out=prob[:, b], in0=S, scalar=SCALE, in1=bb,
                                                          op0=ALU.mult, op1=ALU.add))
                            link(dve.tensor_reduce(mx[:, b], prob[:, b], AX.X, ALU.max))
                            link(dve.tensor_tensor(mx[:, b], mx[:, b], sink[:, 4 * hf:4 * hf + 4], ALU.max))
                            link(dve.tensor_tensor(es[:, b], sink[:, 4 * hf:4 * hf + 4], mx[:, b], ALU.subtract))
                            dve.tensor_scalar(nm[:, b], mx[:, b], -1.0, None, ALU.mult).then_inc(pre_done, 1)
                        else:
                            link(dve.tensor_reduce(mx[:, b], S, AX.X, ALU.max))
                            dve.tensor_scalar(nm[:, b], mx[:, b], -MSCALE, None, ALU.mult).then_inc(pre_done, 1)
                    if s >= 1:
                        u = s - 1
                        b = u % 2
                        dve.wait_ge(exp_done, u + 1)
                        if units[u][0] == "swa":
                            link(dve.tensor_tensor(rs[:, b], rs[:, b], es[:, b], ALU.add))
                        link(dve.reciprocal(rd[:, b], rs[:, b]))
                        dve.tensor_tensor(prob[:, b], prob[:, b],
                                          rd[:, b].unsqueeze(2).broadcast_to([P, 4, 2 * P]), ALU.mult)\
                           .then_inc(norm_done, 1)
                dve.wait_ge(ss_done, 1)
                dve.wait_ge(bias_s_here, 16 * 4)
                sw = ps_[0:32]
                link(dve.scalar_tensor_tensor(out=sw, in0=psum[0:32, 0:2, 0:WIN + 1], scalar=SCALE,
                                              in1=bias_s[0:32], op0=ALU.mult, op1=ALU.add))
                link(dve.tensor_reduce(mxs[0:32], sw, AX.X, ALU.max))
                link(dve.tensor_tensor(mxs[0:32], mxs[0:32], sink_s[0:32], ALU.max))
                link(dve.tensor_tensor(ess[0:32], sink_s[0:32], mxs[0:32], ALU.subtract))
                dve.tensor_scalar(nms[0:32], mxs[0:32], -1.0, None, ALU.mult).then_inc(smax, 1)
                dve.wait_ge(kr_used, NB)
                link(dve.tensor_reduce(mxm[0:32], psum[0:32, 2, 0:MEM], AX.X, ALU.max))
                dve.tensor_scalar(nmm[0:32], mxm[0:32], -MSCALE, None, ALU.mult).then_inc(smax, 1)
                dve.wait_ge(sexp, 2)
                link(dve.tensor_tensor(rss[0:32], rss[0:32], ess[0:32], ALU.add))
                link(dve.reciprocal(rds[0:32], rss[0:32]))
                dve.tensor_tensor(sw, sw, rds[0:32].unsqueeze(2).broadcast_to([32, 2, WIN + 1]), ALU.mult)\
                   .then_inc(snorm, 1)
                link(dve.reciprocal(rdm[0:32], rsm[0:32]))
                dve.tensor_scalar(psm[0:32], psm[0:32], rdm[0:32], None, ALU.mult).then_inc(snorm, 1)

            @block.scalar
            def _(act):
                act.wait_ge(line_mm, 1)
                act.activation(line[0:HEADS, 0:LINE - 1], psum[0:HEADS, 7, 0:LINE - 1], ACT.Copy)\
                   .then_inc(line_ready, 1)
                act.wait_ge(mk_turned, 1)
                for t in range(2):
                    act.activation(memKT[:, :, t * P:(t + 1) * P],
                                   psum[:, 4 + t, :].rearrange("p (h n) -> p h n", h=NC), ACT.Copy)\
                       .then_inc(mk_copied, 1)
                act.wait_ge(unflipped, 1)
                turned_back = psum[:, 0:4, :].rearrange("p b (h k) -> p (b h) k", k=2 * P)
                act.activation(bias, turned_back, ACT.Copy).then_inc(bias_ready, 1)
                act.activation(bias0[:, :, P:2 * P], turned_back[:, :, P:2 * P], ACT.Copy).then_inc(bias_ready, 1)
                for s in range(NU + 2):
                    if s < NU:
                        kind, n, hf = units[s]
                        b = s % 2
                        S = psum[:, 2 * b:2 * b + 2, :].rearrange("p b (h k) -> p (b h) k", k=2 * P)
                        act.wait_ge(pre_done, s + 1)
                        if kind == "swa":
                            act.activation(es[:, b], es[:, b], ACT.Exp)
                        for i in range(4):
                            src = prob[:, b, i, :] if kind == "swa" else S[:, i, :]
                            ins = act.activation(prob[:, b, i, :], src, ACT.Exp, bias=nm[:, b, i:i + 1],
                                                 scale=1.0 if kind == "swa" else MSCALE,
                                                 accum_out=rs[:, b, i:i + 1])
                        ins.then_inc(exp_done, 1)
                    if 1 <= s <= NU:
                        u = s - 1
                        act.wait_ge(t_done, u + 1)
                        if u >= 2:
                            act.wait_ge(pv_done, u - 1)
                        act.activation(probT[:, u % 2],
                                       psum[:, 4:6, :].rearrange("p b (i n) -> p (b i) n", n=P), ACT.Copy)\
                           .then_inc(tev_done, 1)
                    if s >= 2:
                        u = s - 2
                        kind, n, hf = units[u]
                        act.wait_ge(pv_done, u + 1)
                        if kind == "swa":
                            dst = qT[:, 2 * hf:2 * hf + 2, n * P:(n + 1) * P]
                            src = psum[:, 6, 0:2 * P].rearrange("p (c n) -> p c n", c=2)
                        else:
                            dst = qmT[:, :, n * P:(n + 1) * P]
                            src = psum[:, 6, :].rearrange("p (c n) -> p c n", c=4)
                        act.activation(dst, src, ACT.Copy).then_inc(o_done, 1)
                act.wait_ge(smax, 1)
                act.activation(ess[0:32], ess[0:32], ACT.Exp)
                for j in range(2):
                    ins = act.activation(ps_[0:32, j, :], ps_[0:32, j, :], ACT.Exp, bias=nms[0:32, j:j + 1],
                                         accum_out=rss[0:32, j:j + 1])
                ins.then_inc(sexp, 1)
                act.wait_ge(smax, 2)
                act.activation(psm[0:32], psum[0:32, 2, 0:MEM], ACT.Exp, bias=nmm[0:32], scale=MSCALE,
                               accum_out=rsm[0:32]).then_inc(sexp, 1)
                act.wait_ge(sturn, 1)
                act.activation(pst, psum[:, 4, 0:64].rearrange("p (j r) -> p j r", j=2), ACT.Copy).then_inc(scopy, 1)
                act.activation(pmt, psum[:, 4, 64:128].rearrange("p (j r) -> p j r", j=2), ACT.Copy)\
                   .then_inc(scopy, 1)
                act.activation(pslast[0:1], psum[0:1, 5, 0:64].rearrange("p (j r) -> p j r", j=2), ACT.Copy)\
                   .then_inc(scopy, 1)
                act.wait_ge(spv, 1)
                act.wait_ge(masked, 10)
                act.activation(qT[:, :, SEQ:T], psum[:, 6, 0:32].rearrange("p (c b) -> p c b", b=NB), ACT.Copy)\
                   .then_inc(so, 1)
                act.wait_ge(vr_used, NB)
                act.activation(qmT[:, :, SEQ:T], psum[:, 7, 0:32].rearrange("p (c b) -> p c b", b=NB), ACT.Copy)\
                   .then_inc(so, 1)

        GRING = 5
        gw = at(RG, GRING, KD + NC, P)
        gsig = at(RG + GRING * 1536, 2, GC)
        gprod = at(RG + GRING * 1536 + 2 * GC, 2, GC)
        gw_here = [sem(f"gate_weights_here{i}") for i in range(GRING)]
        pair_done = sem("pair_done")
        gate_ready = sem("gate_ready")
        taken = sem("pair_taken")
        added = sem("added")
        branch = [yT, qT, qmT]
        pairs = [(m, br, g) for m in range(KD) for br in range(3) for g in range(3)]

        with nc.Block() as block:
            @block.sync
            def _(sp):
                for i in range(3 * KD):
                    if i >= GRING:
                        sp.wait_ge(pair_done, 3 * (i - GRING + 1))
                    sp.dma_start(gw[:, i % GRING], w_gates[i]).then_inc(gw_here[i % GRING], 16)

            @block.tensor
            def _(pe):
                for i, (m, br, g) in enumerate(pairs):
                    w = gw[:, (i // 3) % GRING]
                    if g == 0:
                        pe.wait_ge(gw_here[(i // 3) % GRING], 16 * (i // 3 // GRING + 1))
                    if i >= 4:
                        pe.wait_ge(taken, i - 3)
                    cols = slice(g * GC, (g + 1) * GC)
                    b = 2 * (i % 4)
                    for k in range(KD):
                        pe.matmul(psum[:, b, 0:GC], w[:, k, :], hT[:, k, cols], start=(k == 0), stop=(k == KD - 1))
                    for c in range(NC):
                        mm = pe.matmul(psum[:, b + 1, 0:GC], w[:, KD + c, :], branch[br][:, c, cols],
                                       start=(c == 0), stop=(c == NC - 1))
                    mm.then_inc(pair_done, 1)

            @block.scalar
            def _(act):
                for i in range(len(pairs)):
                    act.wait_ge(pair_done, i + 1)
                    if i >= 2:
                        act.wait_ge(taken, i - 1)
                    act.activation(gsig[:, i % 2, :], psum[:, 2 * (i % 4), 0:GC], ACT.Sigmoid)\
                       .then_inc(gate_ready, 1)

            @block.vector
            def _(dve):
                n_add = 0
                for i, (m, br, g) in enumerate(pairs):
                    dve.wait_ge(gate_ready, i + 1)
                    out = mergedT[:, m, g * GC:(g + 1) * GC]
                    dst = out if br == 0 else gprod[:, i % 2, :]
                    if n_add:
                        dve.wait_ge(added, n_add)
                    dve.tensor_tensor(dst, gsig[:, i % 2, :], psum[:, 2 * (i % 4) + 1, 0:GC], ALU.mult)\
                       .then_inc(taken, 1)
                    if br:
                        dve.wait_ge(taken, i + 1)
                        dve.tensor_tensor(out, out, dst, ALU.add).then_inc(added, 1)
                        n_add += 1

        xb = at(0, NT, D)
        wq = at(8192, KD, D)
        keys = at(16384, HEADS, 2 * NKEYS)
        scur = at(18432, HEADS, 2, NKEYS)
        xcur = at(20480, D)
        x1cur = at(21504, D)
        gfb = at(22528, D)
        ybuf = at(23552, D)
        xbT = at(24576, KD, P)
        pqT = at(25600, HEADS, P)
        E0 = 26624
        oneh = at(E0, 2, TOPK, TOPK)
        oneh2 = at(E0 + 512, 2, TOPK, TOPK)
        cand = at(E0 + 1024, TOPK, TOPK)
        cand2 = at(E0 + 1280, TOPK, TOPK)
        stmp = at(E0 + 1536, 2, NKEYS)
        E1 = E0 + 1792
        sv = at(E1, HEADS, 2, TOPK)
        si = at(E1 + 256, HEADS, 2, TOPK).bitcast(U32)
        sif = at(E1 + 512, HEADS, 2, TOPK)
        best = at(E1 + 768, HEADS, TOPK)
        ci = at(E1 + 896, HEADS, TOPK).bitcast(U32)
        ij = at(E1 + 1024, HEADS, 2, TOPK).bitcast(U32)
        ijf = at(E1 + 1280, HEADS, 2, TOPK)
        pick = at(E1 + 1536, HEADS, 2, TOPK)
        idN = at(E1 + 1792, SLOTS).bitcast(U32)
        idD = at(E1 + 1920, SLOTS).bitcast(U32)
        idU = at(E1 + 2048, SLOTS).bitcast(U32)
        gateN = at(E1 + 2176, HEADS, TOPK)
        gateD = at(E1 + 2304, SLOTS)
        dots = at(E1 + 2432, SLOTS)
        coef = at(E1 + 2560, SLOTS)
        gel = at(E1 + 2688, SLOTS)
        diag = at(E1 + 2816, 4, P)
        xnext = at(E1 + 3328, D)
        assert E1 + 3328 + D <= MG
        wo = at(RG, KD, D)
        x1s = at(RG + 8192, D)
        xbs = at(RG + 9216, D)
        xin = at(21504, 2, D)
        g2b = at(23552, D)
        scs = at(MG, HEADS, 2 * NKEYS)
        rowD = at(MG, DRING, D)
        rowU = at(MG + DRING * D, URING, D)
        R2 = NB * HEADS
        st2 = small[:, 320:352]
        st3 = small[:, 352:400]
        hsum, hrec = st3[:, 0:8], st3[:, 8:16]
        msq, mrec = st3[:, 16:17], st3[:, 17:18]

        x1_out = [sem("x1_out0"), sem("x1_out1")]
        x_here = [sem("x_here0"), sem("x_here1")]
        wo_here = sem("w_out_here")
        o_mm = sem("out_product")
        x1_done = sem("x1_done")
        x1_sq = sem("x1_squared")
        x1_std = sem("x1_std")
        x1_rec = sem("x1_reciprocal")
        xb_done = sem("xb_done")
        wq_here = sem("peer_w_q_here")
        key_zero = sem("key_zero")
        xnext_ready = sem("next_x_copied")
        xT_done = sem("xb_turned")
        xT_copied = sem("xb_turned_copied")
        pq_done = sem("peer_q_done")
        pq_copied = sem("peer_q_copied")
        sc_done = sem("peer_scores_done")
        sc_copied = sem("peer_scores_copied")
        smp_out = sem("sample_rows_out")
        sel = sem("select_step")
        sel_exp = sem("select_exp")

        xcur_here = sem("block_x_copied")
        ids_ready = sem("expert_lists_ready")
        gD = [sem(f"down_rows_here{i}") for i in range(DRING)]
        gU = [sem(f"up_rows_here{i}") for i in range(URING)]
        dot_done = sem("dots_done")
        gelu1 = sem("gelu_first_half")
        gelu2 = sem("gelu_second_half")
        coef1 = sem("coefficients_first_half")
        coef2 = sem("coefficients_second_half")
        gates_moved = sem("gates_moved")
        diag_ready = sem("diagonal_ready")
        up_done = sem("up_products_done")
        x1_here = sem("x1_here")
        y_sum = sem("y_summed")
        y_sq = sem("y_squared")
        y_std = sem("y_std")
        y_rec = sem("y_reciprocal")
        y_ready = sem("y_ready")
        y_out = sem("y_out")
        gf_here = sem("final_gain_here")

        def tile_rows(n):
            return P if n < NT else NB

        def turn_x(pe, run, src, r):
            for k in range(KD):
                mm = pe.transpose(psum[:, 4 + k // 4, (k % 4) * P:(k % 4) * P + r], src[:, k * P:(k + 1) * P],
                                  ident[0:r, 0:r])
            mm.then_inc(xT_done, 1)

        def query_head(pe, run, h, r):
            for k in range(KD):
                mm = pe.matmul(psum[:, 6 + h // 4, (h % 4) * P:(h % 4) * P + r], wq[:, k, h * P:(h + 1) * P],
                               xbT[:, k, 0:r], start=(k == 0), stop=(k == KD - 1))
            if h == HEADS - 1:
                mm.then_inc(pq_done, 1)

        def score_keys(pe, run, r):
            for h in range(HEADS):
                mm = pe.matmul(psum[0:r, 4 + h // 2, (h % 2) * 256:(h % 2) * 256 + 256], pqT[:, h, 0:r],
                               keys[:, h, :], start=True, stop=True)
            mm.then_inc(sc_done, 1)

        def copy_xT(act, run, r):
            act.activation(xbT[:, :, 0:r], psum[:, 4:6, :].rearrange("p b (k n) -> p (b k) n", n=P)[:, :, 0:r],
                           ACT.Copy).then_inc(xT_copied, 1)

        def copy_q(act, run, r):
            act.activation(pqT[:, :, 0:r], psum[:, 6:8, :].rearrange("p b (k n) -> p (b k) n", n=P)[:, :, 0:r],
                           ACT.Copy).then_inc(pq_copied, 1)

        def copy_scores(act, dst, r):
            act.activation(dst[0:r].rearrange("p (b h) n -> p b (h n)", b=4), psum[0:r, 4:8, :], ACT.Copy)\
               .then_inc(sc_copied, 1)

        scur_heads = scur.rearrange("p h c n -> p h (c n)")

        def select_head_keys(link, p, s2, svh, sih):
            dve = nc.vector
            for c in range(2):
                link(dve.max(svh[:, c, 0:8], s2[:, c, :]))
                link(dve.max_index(sih[:, c, 0:8], svh[:, c, 0:8], s2[:, c, :]))
                link(dve.match_replace(stmp[0:p, c, :], svh[:, c, 0:8], s2[:, c, :], LOW))
                link(dve.max(svh[:, c, 8:16], stmp[0:p, c, :]))
                link(dve.max_index(sih[:, c, 8:16], svh[:, c, 8:16], stmp[0:p, c, :]))

        def select_head_ids(link, p, svh, sih, sfh, bh, cih, ijh, ijfh, pk, idh):
            dve = nc.vector
            cd, c2 = cand[0:p], cand2[0:p]
            link(dve.tensor_tensor(cd, svh[:, 0, :].unsqueeze(2).broadcast_to([p, TOPK, TOPK]),
                                   svh[:, 1, :].unsqueeze(1).broadcast_to([p, TOPK, TOPK]), ALU.add))
            cf, cf2 = cd.rearrange("p i j -> p (i j)"), c2.rearrange("p i j -> p (i j)")
            link(dve.max(bh[:, 0:8], cf))
            link(dve.max_index(cih[:, 0:8], bh[:, 0:8], cf))
            link(dve.match_replace(cf2, bh[:, 0:8], cf, LOW))
            link(dve.max(bh[:, 8:16], cf2))
            link(dve.max_index(cih[:, 8:16], bh[:, 8:16], cf2))
            link(dve.tensor_scalar(ijh[:, 0, :], cih, 4, None, ALU.logical_shift_right))
            link(dve.tensor_scalar(ijh[:, 1, :], cih, 15, None, ALU.bitwise_and))
            link(dve.tensor_copy(ijfh, ijh))
            link(dve.tensor_copy(sfh, sih))
            o1, o2 = oneh[0:p], oneh2[0:p]
            full = [p, 2, TOPK, TOPK]
            link(dve.tensor_tensor(o1, iota16[0:p].unsqueeze(1).unsqueeze(1).broadcast_to(full),
                                   ijfh.unsqueeze(3).broadcast_to(full), ALU.is_equal))
            link(dve.tensor_tensor(o2, o1, sfh.unsqueeze(2).broadcast_to(full), ALU.mult))
            link(dve.tensor_reduce(pk, o2, AX.X, ALU.add))
            link(dve.scalar_tensor_tensor(out=idh, in0=pk[:, 0, :], scalar=float(NKEYS), in1=pk[:, 1, :],
                                          op0=ALU.mult, op1=ALU.add))

        def linker(dve, first):
            k = [0]

            def link(ins):
                k[0] += 1
                ins.then_inc(sel, 1)
                wait_loop(dve, sel, first + k[0])

            return link

        gate_full = [P, HEADS, TOPK]

        def block_keys(link, h):
            select_head_keys(link, P, scur[:, h], sv[:, h], si[:, h])

        def block_ids(link, h):
            select_head_ids(link, P, sv[:, h], si[:, h], sif[:, h], best[:, h], ci[:, h], ij[:, h], ijf[:, h],
                            pick[:, h], idN[:, h * TOPK:(h + 1) * TOPK])

        def gates_shift(link):
            link(nc.vector.tensor_tensor(gateN, best, best[:, :, 0:1].broadcast_to(gate_full), ALU.subtract))

        def gates_norm(link):
            link(nc.vector.tensor_reduce(hsum, gateN, AX.X, ALU.add))
            link(nc.vector.reciprocal(hrec, hsum))
            link(nc.vector.tensor_tensor(gateN, gateN, hrec.unsqueeze(2).broadcast_to(gate_full), ALU.mult))

        RUNS = {1: (0, 0), NT: (1, NT), NT + 1: (2, 1)}

        with nc.Block() as block:
            @block.sync
            def _(sp):
                sp.dma_start(wo, w_o).then_inc(wo_here, 16)
                sp.dma_start(g2b, bass.AP(tensor=g2.tensor, offset=g2.offset, ap=[[0, P], [1, D]])).then_inc(wo_here, 16)
                for n in range(NT + 1):
                    if n >= 2 and n < NT:
                        sp.wait_ge(x1_out[n % 2], 16 * (n // 2))
                        sp.wait_ge(xb_done, n - 1)
                    if n < NT:
                        sp.dma_start(xin[:, n % 2, :], x_prompt[n * P:(n + 1) * P, :]).then_inc(x_here[n % 2], 16)
                    else:
                        sp.dma_start(x1s[0:NB, :], x_sample).then_inc(x_here[0], 16)
                    if n == 1:
                        sp.dma_start(wq, w_q).then_inc(wq_here, 16)
                        sp.wait_ge(key_zero, 1)
                        sp.dma_start(keys[0:64, :, 0:NKEYS], keysT[0:64]).then_inc(wq_here, 16)
                        sp.dma_start(keys[64:128, :, NKEYS:2 * NKEYS], keysT[64:128]).then_inc(wq_here, 16)
                    if 1 <= n:
                        sp.wait_ge(x1_done, n)
                        sp.dma_start(scratch_x1[(n - 1) * P:n * P, :], xin[:, (n - 1) % 2, :])\
                          .then_inc(x1_out[(n - 1) % 2], 16)
                sp.wait_ge(x1_done, NT + 1)
                sp.dma_start(scratch_x1[SEQ:T, :], x1s[0:NB, :]).then_inc(x1_out[0], 16)
                sp.wait_ge(xb_done, NT + 1)
                sp.dma_start(scratch_xb, xbs[0:NB, :]).then_inc(smp_out, 16)
                sp.wait_ge(sc_copied, 2)
                sp.dma_start(scratch_sc.rearrange("(b h) n -> b (h n)", h=HEADS),
                             scs[0:NB].rearrange("p h n -> p (h n)")).then_inc(smp_out, 16)
                sp.wait_ge(smp_out, 32)
                sp.wait_ge(x1_out[0], 16 * 5)
                sp.wait_ge(x1_out[1], 16 * 4)

            @block.gpsimd
            def _(pool):
                pool.memset(keys, 0.0).then_inc(key_zero, 1)
                pool.wait_ge(sel, SEL_OPS)
                pool.tensor_copy(idD, idN).then_inc(ids_ready, 1)

            @block.tensor
            def _(pe):
                pe.wait_ge(wo_here, 32)
                for n in range(NT + 2):
                    if n <= NT:
                        r = tile_rows(n)
                        if n >= 2:
                            pe.wait_ge(x1_done, n - 1)
                        for k in range(KD):
                            for h in range(2):
                                mm = pe.matmul(psum[0:r, 2 * (n % 2) + h, :], mergedT[:, k, n * P:n * P + r],
                                               wo[:, k, h * 512:(h + 1) * 512], start=(k == 0), stop=(k == KD - 1))
                        mm.then_inc(o_mm, 1)
                    if n in RUNS:
                        run, tile = RUNS[n]
                        r = tile_rows(tile)
                        pe.wait_ge(xb_done, tile + 1)
                        if run:
                            pe.wait_ge(sc_copied, run)
                        turn_x(pe, run, xb[:, tile, :] if tile < NT else xbs[0:NB, :], r)
                        pe.wait_ge(wq_here, 48)
                        pe.wait_ge(xT_copied, run + 1)
                        for h in range(HEADS):
                            query_head(pe, run, h, r)
                        pe.wait_ge(pq_copied, run + 1)
                        score_keys(pe, run, r)

            @block.vector
            def _(dve):
                link = linker(dve, 0)
                for n in range(NT + 1):
                    r = tile_rows(n)
                    x1 = xin[:, n % 2, :] if n < NT else x1s[0:NB, :]
                    dst = xb[:, n, :] if n < NT else xbs[0:NB, :]
                    dve.wait_ge(o_mm, n + 1)
                    dve.wait_ge(x_here[n % 2], 16 * (n // 2 + 1))
                    dve.tensor_tensor(x1.rearrange("p (h n) -> p h n", h=2), x1.rearrange("p (h n) -> p h n", h=2),
                                      psum[0:r, 2 * (n % 2):2 * (n % 2) + 2, :], ALU.add).then_inc(x1_done, 1)
                    dve.wait_ge(x1_std, n + 1)
                    dve.reciprocal(st2[0:r, n:n + 1], st2[0:r, n:n + 1]).then_inc(x1_rec, 1)
                    dve.wait_ge(x1_rec, n + 1)
                    dve.scalar_tensor_tensor(out=dst, in0=x1, scalar=st2[0:r, n:n + 1], in1=g2b[0:r, :],
                                             op0=ALU.mult, op1=ALU.mult).then_inc(xb_done, 1)
                    if 2 <= n < 6:
                        dve.wait_ge(sc_copied, 1)
                        for h in (2 * n - 4, 2 * n - 3):
                            block_keys(link, h)
                            block_ids(link, h)
                    if n == 6:
                        gates_shift(link)
                    if n == 7:
                        dve.wait_ge(sel_exp, 1)
                        gates_norm(link)
                        dve.tensor_copy(gateD, gateN.rearrange("p h k -> p (h k)")).then_inc(gates_moved, 1)

            @block.scalar
            def _(act):
                act.wait_ge(initialised, 5)
                for n in range(NT + 2):
                    if n <= NT:
                        r = tile_rows(n)
                        x1 = xin[:, n % 2, :] if n < NT else x1s[0:NB, :]
                        dst = xb[:, n, :] if n < NT else xbs[0:NB, :]
                        s_ = st2[0:r, n:n + 1]
                        act.wait_ge(x1_done, n + 1)
                        act.activation(dst, x1, ACT.Square, accum_out=s_).then_inc(x1_sq, 1)
                        act.wait_ge(x1_sq, n + 1)
                        act.activation(s_, s_, ACT.Sqrt, bias=eps[0:r], scale=1.0 / D).then_inc(x1_std, 1)
                    if n in RUNS:
                        run, tile = RUNS[n]
                        r = tile_rows(tile)
                        act.wait_ge(xT_done, run + 1)
                        copy_xT(act, run, r)
                        act.wait_ge(pq_done, run + 1)
                        copy_q(act, run, r)
                        act.wait_ge(sc_done, run + 1)
                        if run == 1:
                            copy_scores(act, scs, r)
                        else:
                            if run == 2:
                                act.wait_ge(sel, SEL_OPS)
                            copy_scores(act, scur_heads, r)
                    if n == 6:
                        act.wait_ge(sel, SEL_OPS - 3)
                        act.activation(gateN, gateN, ACT.Exp).then_inc(sel_exp, 1)
                act.activation(xcur, xb[:, 0, :], ACT.Copy).then_inc(xcur_here, 1)

        G0 = MG + (DRING + URING) * D
        HALF = SLOTS // 2
        ssc = at(G0, 2, NKEYS)
        ids_s = at(G0 + 256, TOPK).bitcast(U32)
        gate_s = at(G0 + 272, TOPK)
        idcols = at(G0 + 288, NB).bitcast(U32)
        gatecols, dcols, ccols, gcols = (at(G0 + 296 + 8 * i, NB) for i in range(4))
        cmask = at(G0 + 328, NB, NB)
        ys = at(G0 + 1024, D)
        ysq = at(G0 + 2048, D)
        x1keep = at(G0 + 3072, D)
        xbc = at(0, NB, D)

        ss_here = sem("sample_scores_here")
        xbc_here = sem("sample_x_here")
        sel2 = sem("sample_select_step")
        sx = sem("sample_select_exp")
        lists_out = sem("sample_lists_out")
        lists_in = sem("sample_lists_in")
        SAMPLE_DOWN = (NT * SLOTS // DRING + 1) * 16
        SAMPLE_UP = SAMPLE_DOWN + 16
        sdot = sem("sample_dots")
        sgel = sem("sample_gelu")
        scoef = sem("sample_coefficients")
        smask = sem("sample_mask")
        sup = sem("sample_up")
        sy = sem("sample_y")
        sysq = sem("sample_y_squared")
        systd = sem("sample_y_std")

        AT_SUM, AT_COEF2, AT_OUT = 1, 8, 12
        AT_KEYS = {16 + 10 * h: h for h in range(HEADS)}
        AT_IDS = {21 + 10 * h: h for h in range(HEADS)}
        AT_COEF1, AT_GATES, AT_GATES_NORM = 74, 98, 112
        AT_LISTS2, AT_LISTS1 = 24, 96
        KEYS_READ = 24 * (HEADS - 1) + 10

        with nc.Block() as block:
            def steps(body, eng):
                for it in range(3):
                    body(it)
                with eng.Fori(3, NT - 1) as it:
                    body(it)
                body(NT - 1)
                body(NT)

            def kind(it):
                if not isinstance(it, int):
                    return True, True, True, None, True
                return it < NT, it >= 1, it + 1 < NT, it + 2 < NT, it >= 2

            @block.gpsimd
            def _(pool):
                def step(it):
                    down, up, _, _, _ = kind(it)
                    last = isinstance(it, int) and it == NT
                    for j in range(SLOTS):
                        if j == AT_LISTS2 and up:
                            wait_loop(pool, up_done, (it - 1) * SLOTS)
                            wait_loop(pool, dot_done, it * SLOTS)
                            pool.tensor_copy(idU[:, HALF:], idD[:, HALF:]).then_inc(ids_ready, 1)
                            wait_loop(pool, ids_ready, it * 4)
                            wait_loop(pool, sel, (it + 1) * SEL_OPS if not last else NT * SEL_OPS)
                            pool.tensor_copy(idD[:, HALF:], idN[:, HALF:]).then_inc(ids_ready, 1)
                            wait_loop(pool, ids_ready, it * 4 + 1)
                        if j == AT_LISTS1 and down:
                            wait_loop(pool, dot_done, it * SLOTS + HALF)
                            if up:
                                wait_loop(pool, up_done, (it - 1) * SLOTS + HALF)
                            pool.tensor_copy(idU[:, :HALF], idD[:, :HALF]).then_inc(ids_ready, 1)
                            wait_loop(pool, ids_ready, it * 4 + 2)
                            if kind(it)[2]:
                                wait_loop(pool, sel, (it + 1) * SEL_OPS + 24 * HEADS // 2)
                            pool.tensor_copy(idD[:, :HALF], idN[:, :HALF]).then_inc(ids_ready, 1)
                            wait_loop(pool, ids_ready, it * 4 + 3)
                        if up:
                            wait_loop(pool, up_done, (it - 1) * SLOTS + j - URING + 1)
                            pool.indirect_dma_start(rowU[:, j % URING, :], None, w_up,
                                                    bass.IndirectOffsetOnAxis(ap=idU[:, j:j + 1], axis=0))\
                                .then_inc(gU[j % URING], 16)
                        if down:
                            wait_loop(pool, dot_done, it * SLOTS + j - DRING + 1)
                            pool.indirect_dma_start(rowD[:, j % DRING, :], None, w_down,
                                                    bass.IndirectOffsetOnAxis(ap=idD[:, j:j + 1], axis=0))\
                                .then_inc(gD[j % DRING], 16)
                        if last and j == 32:
                            pool.wait_ge(lists_in, 32)
                            for b in range(NB):
                                pool.indirect_dma_start(rowD[:, b, :], None, w_down,
                                                        bass.IndirectOffsetOnAxis(ap=idcols[:, b:b + 1], axis=0))\
                                    .then_inc(gD[b], 16)
                        if last and j == 56:
                            for b in range(NB):
                                pool.wait_ge(sdot, b + 1)
                                pool.indirect_dma_start(rowD[:, b, :], None, w_up,
                                                        bass.IndirectOffsetOnAxis(ap=idcols[:, b:b + 1], axis=0))\
                                    .then_inc(gD[b], 16)

                pool.memset(cmask, 0.0).then_inc(smask, 1)
                pool.wait_ge(ids_ready, 1)
                steps(step, pool)

            @block.vector
            def _(dve):
                def sum_up(it):
                    wait_loop(dve, up_done, (it - 1) * SLOTS)
                    wait_loop(dve, x1_here, (it - 1) * 16)
                    wait_loop(dve, y_out, (it - 2) * 16)
                    dve.tensor_tensor(ybuf.rearrange("p (h n) -> p h n", h=2),
                                      x1cur.rearrange("p (h n) -> p h n", h=2), psum[:, 0:2, :], ALU.add)\
                       .then_inc(y_sum, 1)

                def norm_out(it):
                    wait_loop(dve, y_std, it - 1)
                    dve.reciprocal(mrec, msq).then_inc(y_rec, 1)
                    wait_loop(dve, y_rec, it - 1)
                    dve.scalar_tensor_tensor(out=ybuf, in0=ybuf, scalar=mrec, in1=gfb, op0=ALU.mult,
                                             op1=ALU.mult).then_inc(y_ready, 1)

                def second_half(it):
                    wait_loop(dve, gelu2, it)
                    dve.tensor_tensor(coef[:, HALF:], gel[:, HALF:], gateD[:, HALF:], ALU.mult).then_inc(coef2, 1)
                    wait_loop(dve, coef2, it)
                    if kind(it)[0]:
                        dve.tensor_copy(gateD, gateN.rearrange("p h k -> p (h k)")).then_inc(gates_moved, 1)

                def step(it):
                    down, up, select, _, write = kind(it)
                    link = linker(dve, (it + 1) * SEL_OPS) if select else None
                    if not down:
                        return
                    for j in range(SLOTS):
                        if j == AT_SUM and write:
                            sum_up(it)
                        if j == AT_COEF2 and up:
                            second_half(it)
                        if j == AT_OUT and write:
                            norm_out(it)
                        if select and j in AT_KEYS:
                            if AT_KEYS[j] == 0:
                                wait_loop(dve, sc_copied, it + 3)
                            block_keys(link, AT_KEYS[j])
                        if select and j in AT_IDS:
                            if AT_IDS[j] == 0 and up:
                                wait_loop(dve, ids_ready, it * 4 - 1)
                            if AT_IDS[j] == HEADS // 2:
                                wait_loop(dve, ids_ready, it * 4 + 1)
                            block_ids(link, AT_IDS[j])
                        if j == AT_COEF1:
                            wait_loop(dve, gelu1, it + 1)
                            wait_loop(dve, gates_moved, it + 1)
                            dve.tensor_tensor(coef[:, :HALF], gel[:, :HALF], gateD[:, :HALF], ALU.mult)\
                               .then_inc(coef1, 1)
                        if select and j == AT_GATES:
                            gates_shift(link)
                        if select and j == AT_GATES_NORM:
                            wait_loop(dve, sel_exp, it + 2)
                            gates_norm(link)
                        if j == 0:
                            wait_loop(dve, xcur_here, it + 1)
                        wait_loop(dve, gD[j % DRING], (it * (SLOTS // DRING) + j // DRING + 1) * 16)
                        dve.tensor_tensor_reduce(rowD[:, j % DRING, :], rowD[:, j % DRING, :], xcur, 1.0, 0.0,
                                                 ALU.mult, ALU.add, dots[:, j:j + 1]).then_inc(dot_done, 1)

                dve.wait_ge(gf_here, 16)
                dve.wait_ge(gates_moved, 1)
                steps(step, dve)
                sum_up(NT)
                second_half(NT)
                norm_out(NT)
                k = [0]

                def link2(ins):
                    k[0] += 1
                    ins.then_inc(sel2, 1)
                    dve.wait_ge(sel2, k[0])

                dve.wait_ge(ss_here, 32)
                select_head_keys(link2, R2, ssc[0:R2], sv[0:R2, 0], si[0:R2, 0])
                select_head_ids(link2, R2, sv[0:R2, 0], si[0:R2, 0], sif[0:R2, 0], best[0:R2, 0], ci[0:R2, 0],
                                ij[0:R2, 0], ijf[0:R2, 0], pick[0:R2, 0], ids_s[0:R2])
                gg = gate_s[0:R2]
                link2(dve.tensor_scalar(gg, best[0:R2, 0, :], best[0:R2, 0, 0:1], None, ALU.subtract))
                dve.wait_ge(sx, 1)
                link2(dve.tensor_reduce(hsum[0:R2, 0:1], gg, AX.X, ALU.add))
                link2(dve.reciprocal(hrec[0:R2, 0:1], hsum[0:R2, 0:1]))
                link2(dve.tensor_scalar(gg, gg, hrec[0:R2, 0:1], None, ALU.mult))
                dve.wait_ge(xbc_here, 16 * NB)
                for b in range(NB):
                    dve.wait_ge(gD[b], SAMPLE_DOWN)
                    dve.tensor_tensor_reduce(rowD[:, b, :], rowD[:, b, :], xbc[:, b, :], 1.0, 0.0, ALU.mult,
                                             ALU.add, dcols[:, b:b + 1]).then_inc(sdot, 1)
                dve.wait_ge(sgel, 1)
                dve.wait_ge(lists_in, 32)
                dve.tensor_tensor(ccols, gcols, gatecols, ALU.mult).then_inc(scoef, 1)
                dve.wait_ge(scoef, 1)
                dve.wait_ge(smask, 1)
                for b in range(NB):
                    dve.tensor_copy(cmask[:, b, b:b + 1], ccols[:, b:b + 1]).then_inc(smask, 1)
                dve.wait_ge(sup, NB)
                dve.tensor_tensor(ys[0:NB].rearrange("p (h n) -> p h n", h=2),
                                  x1keep[0:NB].rearrange("p (h n) -> p h n", h=2), psum[0:NB, 2:4, :], ALU.add)\
                   .then_inc(sy, 1)
                dve.wait_ge(systd, 1)
                dve.reciprocal(mrec[0:NB, ], msq[0:NB]).then_inc(sy, 1)
                dve.wait_ge(sy, 2)
                dve.scalar_tensor_tensor(out=ys[0:NB], in0=ys[0:NB], scalar=mrec[0:NB], in1=gfb[0:NB], op0=ALU.mult,
                                         op1=ALU.mult).then_inc(sy, 1)
                dve.wait_ge(sy, 3)
                sum_up(NT + 1)
                norm_out(NT + 1)

            @block.scalar
            def _(act):
                def squares(it):
                    wait_loop(act, y_sum, it - 1)
                    act.activation(x1cur, ybuf, ACT.Square, accum_out=msq).then_inc(y_sq, 1)
                    wait_loop(act, y_sq, it - 1)
                    act.activation(msq, msq, ACT.Sqrt, bias=eps, scale=1.0 / D).then_inc(y_std, 1)

                def step(it):
                    down, up, select, score, write = kind(it)
                    if score is None:
                        score = it_scores[0]
                    last = isinstance(it, int) and it == NT
                    for j in range(SLOTS):
                        if j == 2 and score:
                            act.activation(xnext, xb[:, bass.ds(it + 2, 1), :].rearrange("p a d -> p (a d)"),
                                           ACT.Copy).then_inc(xnext_ready, 1)
                        if j == 4 and up:
                            wait_loop(act, dot_done, it * SLOTS)
                            wait_loop(act, coef2, it - 1)
                            act.activation(gel[:, HALF:], dots[:, HALF:], ACT.Gelu).then_inc(gelu2, 1)
                        if j == 6 and write:
                            squares(it)
                        if j == 14 and score:
                            wait_loop(act, xT_done, it + 4)
                            copy_xT(act, None, P)
                        if j == 56 and score:
                            wait_loop(act, pq_done, it + 4)
                            copy_q(act, None, P)
                        if j == 70 and down:
                            wait_loop(act, dot_done, it * SLOTS + HALF)
                            if up:
                                wait_loop(act, coef1, it)
                            act.activation(gel[:, :HALF], dots[:, :HALF], ACT.Gelu).then_inc(gelu1, 1)
                        if j == 94 and score:
                            wait_loop(act, sc_done, it + 4)
                            wait_loop(act, sel, (it + 1) * SEL_OPS + KEYS_READ)
                            copy_scores(act, scur_heads, P)
                        if j == 106 and select:
                            wait_loop(act, sel, (it + 2) * SEL_OPS - 3)
                            act.activation(gateN, gateN, ACT.Exp).then_inc(sel_exp, 1)
                        if last and j == 16:
                            act.wait_ge(sel2, 25)
                            act.activation(gate_s[0:R2], gate_s[0:R2], ACT.Exp).then_inc(sx, 1)
                        if last and j == 60:
                            act.wait_ge(sdot, NB)
                            act.activation(gcols, dcols, ACT.Gelu).then_inc(sgel, 1)
                        if up:
                            if j == 0:
                                wait_loop(act, coef1, it)
                            if j == HALF:
                                wait_loop(act, coef2, it)
                            wait_loop(act, up_done, (it - 1) * SLOTS + j - 3)
                            act.activation(diag[:, j % 4, :], ident, ACT.Copy, scale=coef[:, j:j + 1])\
                               .then_inc(diag_ready, 1)
                    if select:
                        wait_loop(act, dot_done, (it + 1) * SLOTS)
                        act.activation(xcur, xb[:, bass.ds(it + 1, 1), :].rearrange("p a d -> p (a d)"),
                                       ACT.Copy).then_inc(xcur_here, 1)

                it_scores = [True]
                for it in range(3):
                    step(it)
                with act.Fori(3, NT - 2) as it:
                    step(it)
                for it in range(NT - 2, NT + 1):
                    step(it)
                act.wait_ge(sy, 1)
                act.activation(ysq[0:NB], ys[0:NB], ACT.Square, accum_out=msq[0:NB]).then_inc(sysq, 1)
                act.wait_ge(sysq, 1)
                act.activation(msq[0:NB], msq[0:NB], ACT.Sqrt, bias=eps[0:NB], scale=1.0 / D).then_inc(systd, 1)
                act.wait_ge(sy, 2)
                squares(NT + 1)

            @block.tensor
            def _(pe):
                def step(it):
                    down, up, _, score, _ = kind(it)
                    if score is None:
                        score = True
                    last = isinstance(it, int) and it == NT
                    for j in range(SLOTS):
                        if score and j == 8:
                            wait_loop(pe, xnext_ready, it + 1)
                            wait_loop(pe, sc_copied, it + 3)
                            turn_x(pe, None, xnext, P)
                        if score and 18 <= j < 50 and j % 4 == 2:
                            if j == 18:
                                wait_loop(pe, xT_copied, it + 4)
                            query_head(pe, None, (j - 18) // 4, P)
                        if score and j == 62:
                            wait_loop(pe, pq_copied, it + 4)
                            score_keys(pe, None, P)
                        if last and j == 100:
                            pe.wait_ge(smask, NB + 1)
                            for b in range(NB):
                                pe.wait_ge(gD[b], SAMPLE_UP)
                                for h in range(2):
                                    mm = pe.matmul(psum[0:NB, 2 + h, :], cmask[:, b, :],
                                                   rowD[:, b, h * 512:(h + 1) * 512], start=(b == 0),
                                                   stop=(b == NB - 1))
                                mm.then_inc(sup, 1)
                        if up:
                            if j == 0:
                                wait_loop(pe, y_sum, it - 1)
                            wait_loop(pe, gU[j % URING], ((it - 1) * (SLOTS // URING) + j // URING + 1) * 16)
                            wait_loop(pe, diag_ready, (it - 1) * SLOTS + j + 1)
                            for h in range(2):
                                mm = pe.matmul(psum[:, h, :], diag[:, j % 4, :],
                                               rowU[:, j % URING, h * 512:(h + 1) * 512],
                                               start=(j == 0), stop=(j == SLOTS - 1))
                            mm.then_inc(up_done, 1)

                for it in range(3):
                    step(it)
                with pe.Fori(3, NT - 2) as it:
                    step(it)
                for it in range(NT - 2, NT + 1):
                    step(it)

            @block.sync
            def _(sp):
                def step(it):
                    if not kind(it)[4]:
                        return
                    wait_loop(sp, y_std, it - 2)
                    sp.dma_start(x1cur, scratch_x1[bass.ds((it - 2) * P, P), :]).then_inc(x1_here, 16)
                    wait_loop(sp, y_ready, it - 1)
                    sp.dma_start(y_prompt[bass.ds((it - 2) * P, P), :], ybuf).then_inc(y_out, 16)

                sp.dma_start(gfb, bass.AP(tensor=gf.tensor, offset=gf.offset, ap=[[0, P], [1, D]])).then_inc(gf_here, 16)
                sp.dma_start(ssc[0:R2], scratch_sc.rearrange("r (c n) -> r c n", c=2)).then_inc(ss_here, 16)
                sp.dma_start(x1keep[0:NB], scratch_x1[SEQ:T, :]).then_inc(ss_here, 16)
                for it in range(3):
                    step(it)
                with sp.Fori(3, NT - 1) as it:
                    step(it)
                step(NT - 1)
                sp.wait_ge(dot_done, NT * SLOTS)
                for b in range(NB):
                    sp.dma_start(xbc[:, b, :], bass.AP(tensor=scratch_xb.tensor, offset=b * D, ap=[[0, P], [1, D]]))\
                      .then_inc(xbc_here, 16)
                step(NT)
                sp.wait_ge(sel2, 24 + 4)
                sp.dma_start(scratch_ids.rearrange("b (h k) -> (b h) k", h=HEADS), ids_s[0:R2]).then_inc(lists_out, 16)
                sp.dma_start(scratch_gate.rearrange("b (h k) -> (b h) k", h=HEADS), gate_s[0:R2])\
                  .then_inc(lists_out, 16)
                sp.wait_ge(lists_out, 32)
                with nc.allow_non_contiguous_dma("a list of 1024 words, turned"):
                    sp.dma_start(idcols, scratch_ids.rearrange("b s -> s b")).then_inc(lists_in, 16)
                    sp.dma_start(gatecols, scratch_gate.rearrange("b s -> s b")).then_inc(lists_in, 16)
                sp.wait_ge(sy, 3)
                store(sp, y_sample, ys[0:NB, :])
                step(NT + 1)
                sp.wait_ge(y_out, 16 * NT)

        with nc.Block() as block:
            @block.sync
            def _(sp):
                sp.wait_ge(stores, n_stores[0])


_NAMES = ["x_prompt", "x_sample", "xT", "memT", "w_chunks", "w_gates", "w_o", "w_q", "keysT", "bias_tab", "onehot",
          "sinks_bc", "sinks_s", "g1", "gm", "g2", "gf", "conv_w", "conv_b", "ln_g", "ln_b", "cacheT", "cache_conv",
          "cache_k", "cache_v", "cache_kT", "memkT", "cache_mv", "w_down", "w_up"]
_OUTS = [((SEQ, D), (1, SEQ, D)), ((NB, D), (NB, 1, D)), ((HALO, CH), (1, 1, HALO, CH)),
         ((WIN, P), (1, 1, WIN, 2, HD)), ((WIN, P), (1, 1, WIN, 2, HD)),
         ((MEM, CH), (1, 1, MEM, 4, P)), ((MEM, CH), (1, 1, MEM, 4, P)),
         ((NB, HALO, CH), (1, NB, HALO, CH)), ((NB, WIN, P), (1, NB, WIN, 2, HD)), ((NB, WIN, P), (1, NB, WIN, 2, HD))]


def bucket_rows():
    oh = np.zeros((33, LINE - 1), np.float32)
    for r in range(LINE - 1):
        dist = 2 * P - 1 - r
        if dist < 0 or dist > WIN:
            oh[32, r] = 1
        elif dist < 16:
            oh[dist, r] = 1
        else:
            oh[min(31, 16 + int(math.log(dist / 16) / math.log(128 / 16) * 16)), r] = 1
    return oh


def lay_out(x_prompt, x_sample, cache_conv, cache_swa_k, cache_swa_v, cache_mem_k, cache_mem_v, mem_prompt,
            rel_bias_table, norm1_g, w_in, conv_dw_w, conv_dw_b, conv_ln_g, conv_ln_b, w_conv_out, swa_sinks,
            w_swa_out, mem_norm_g, w_mem_kv, w_mem_out, w_out, norm2_g, peer_w_q, peer_keys, peer_w_down,
            peer_w_up, final_norm_g):
    xp, xs = x_prompt[0], x_sample[:, 0]

    def slices(w):
        return w.reshape(-1, P, w.shape[1]).transpose(1, 0, 2)

    w = w_in[0]
    q_cols = [np.r_[c * HD:(c + 1) * HD, (c + 4) * HD:(c + 5) * HD] for c in range(4)]
    q0, k0 = 2 * CH, 2 * CH + 512
    v0, m0, gate0 = k0 + P, k0 + 2 * P, k0 + 2 * P + 512
    start = {"a": 0, "b": CH, "k": k0, "v": v0, "qm": m0}
    chunks = []
    for kind, c in CHUNKS:
        if kind == "q":
            part = w[:, q0 + q_cols[c]]
        elif kind == "mem":
            part = w_mem_kv[0][:, c * P:(c + 1) * P]
        else:
            part = w[:, start[kind] + c * P:start[kind] + (c + 1) * P]
        chunks.append(slices(part))
    outs = [w_conv_out[0], w_swa_out[0][np.concatenate(q_cols)], w_mem_out[0]]
    gates = []
    for m in range(KD):
        for br in range(3):
            g = slices(w[:, gate0 + br * D + m * P:gate0 + br * D + (m + 1) * P])
            gates.append(np.concatenate([g, slices(outs[br][:, m * P:(m + 1) * P])], axis=1))
    order = [2 * hf + cc + 4 * j for hf in range(2) for j in range(2) for cc in range(2)]
    sinks = swa_sinks[0]
    return {
        "x_prompt": xp, "x_sample": xs,
        "xT": slices(np.concatenate([xp, xs]).T), "memT": slices(mem_prompt[0].T),
        "w_chunks": np.stack(chunks), "w_gates": np.stack(gates),
        "w_o": slices(w_out[0]), "w_q": slices(peer_w_q[0]),
        "keysT": peer_keys[0].transpose(1, 3, 0, 2).reshape(P, HEADS, NKEYS),
        "bias_tab": rel_bias_table[:, order], "onehot": bucket_rows(),
        "sinks_bc": np.broadcast_to(sinks[order], (P, 8)),
        "sinks_s": np.repeat(sinks.reshape(2, 4).T, NB, axis=0),
        "g1": norm1_g[0].reshape(KD, P).T, "gm": mem_norm_g[0].reshape(KD, P).T,
        "g2": norm2_g[0], "gf": final_norm_g,
        "conv_w": conv_dw_w[0].reshape(TAPS, NC, P).transpose(2, 1, 0),
        "conv_b": conv_dw_b[0].reshape(NC, P).T, "ln_g": conv_ln_g[0].reshape(NC, P).T,
        "ln_b": conv_ln_b[0].reshape(NC, P).T,
        "cacheT": cache_conv[0].transpose(2, 0, 1).reshape(NC, P, NB, HALO).transpose(1, 0, 2, 3),
        "cache_conv": cache_conv[0], "cache_k": cache_swa_k[0].reshape(NB, WIN, P),
        "cache_v": cache_swa_v[0].reshape(NB, WIN, P),
        "cache_kT": cache_swa_k[0].reshape(NB, WIN, P).transpose(2, 0, 1),
        "memkT": cache_mem_k[0].transpose(0, 3, 2, 1), "cache_mv": cache_mem_v[0].reshape(NB, MEM, CH),
        "w_down": peer_w_down[0], "w_up": peer_w_up[0],
    }


def kernel(**inputs):
    import concourse.bacc as bacc
    from concourse.bass_utils import run_bass_kernel_spmd

    laid = lay_out(**{k: np.asarray(v) for k, v in inputs.items()})
    nc = bacc.Bacc("TRN2", target_bir_lowering=False, num_devices=1)
    arrays, args = {}, []
    for name in _NAMES:
        a = np.ascontiguousarray(laid[name])
        arrays[f"in_{name}"] = a
        args.append(nc.dram_tensor(f"in_{name}", a.shape, mybir.dt.from_np(a.dtype), kind="ExternalInput").ap())
    for i, (shape, _) in enumerate(_OUTS):
        args.append(nc.dram_tensor(f"out_{i}", shape, F32, kind="ExternalOutput").ap())
    build_kernel(nc, *args)
    r = run_bass_kernel_spmd(nc, [arrays], core_ids=[0])
    return tuple(r.results[0][f"out_{i}"].reshape(full) for i, (_, full) in enumerate(_OUTS))
```

```python
from contextlib import ExitStack

import concourse.bass as bass
from concourse import mybir
import math
import numpy as np

ALU = mybir.AluOpType
ACT = mybir.ActivationFunctionType
AX = mybir.AxisListType
F32 = mybir.dt.float32
U32 = mybir.dt.uint32

P = 128
D = 1024
SEQ = 1024
NB = 8
T = SEQ + NB
KD = D // P
NT = SEQ // P
GC = T // 3
MEM = 256
CH = 512
NC = CH // P
TAPS = 31
HALO = TAPS - 1
WIN = 128
HD = 64
SCALE = HD ** -0.5
MSCALE = 128 ** -0.5
NEG = -1e30
EPS = 1e-6
LINE = 384
HEADS = 8
TOPK = 16
SLOTS = HEADS * TOPK
NKEYS = 128
LOW = -3.0e38

CHUNKS = [("b", 0), ("a", 0), ("b", 1), ("a", 1), ("b", 2), ("a", 2), ("b", 3), ("a", 3), ("k", 0), ("v", 0)] + \
         [("q", c) for c in range(4)] + [("qm", c) for c in range(4)] + [("mem", c) for c in range(8)]
WRING = 6
DRING = 8
URING = 4
SEL_OPS = HEADS * 24 + 4
KEYS_READ = 24 * (HEADS - 1) + 10
LAG = 80


def build_kernel(nc, x_prompt, x_sample, xT, memT, w_chunks, w_gates, w_o, w_q, keysT, bias_tab, onehot, sinks_bc,
                 sinks_s, g1, gm, g2, gf, conv_w, conv_b, ln_g, ln_b, cacheT, cache_conv, cache_k, cache_v,
                 cache_kT, memkT, cache_mv, w_down, w_up,
                 y_prompt, y_sample, conv_p, k_p, v_p, mk_p, mv_p, conv_s, k_s, v_s):
    scratch_line = nc.dram_tensor("scratch_line", (HEADS, LINE), F32, kind="Internal").ap()
    scratch_vs = nc.dram_tensor("scratch_vs", (NB, P), F32, kind="Internal").ap()
    scratch_x1 = nc.dram_tensor("scratch_x1", (T, D), F32, kind="Internal").ap()
    scratch_xb = nc.dram_tensor("scratch_xb", (NB, D), F32, kind="Internal").ap()
    scratch_sc = nc.dram_tensor("scratch_sc", (NB * HEADS, 2 * NKEYS), F32, kind="Internal").ap()
    scratch_ids = nc.dram_tensor("scratch_ids", (NB, SLOTS), U32, kind="Internal").ap()
    scratch_gate = nc.dram_tensor("scratch_gate", (NB, SLOTS), F32, kind="Internal").ap()

    with ExitStack() as ctx:
        arena = ctx.enter_context(nc.sbuf_tensor("arena", [P, 52100], F32))
        consts = ctx.enter_context(nc.sbuf_tensor("constants", [P, 1000], F32))
        psum = ctx.enter_context(nc.psum_tensor("psum", [P, 8, 512], F32))

        def sem(name):
            return ctx.enter_context(nc.semaphore(name))

        def at(offset, *shape):
            n = math.prod(shape)
            v = arena[:, offset:offset + n]
            names = "abcde"[:len(shape)]
            if len(shape) > 1:
                v = v.rearrange(f"p ({' '.join(names)}) -> p {' '.join(names)}",
                                **{n: s for n, s in zip(names, shape)})
            return v

        ident = consts[:, 0:128]
        ones = consts[:, 128:256]
        eps = consts[:, 256:257]
        g1s, gms = consts[:, 257:265], consts[:, 265:273]
        cw = consts[:, 273:273 + NC * TAPS].rearrange("p (c t) -> p c t", c=NC)
        cb, lng, lnb = consts[:, 400:404], consts[:, 404:408], consts[:, 408:412]
        sink = consts[:, 412:420]
        sink_s = consts[:, 420:422]
        iota16 = consts[:, 432:448]
        small = consts[:, 448:1000]

        hT = at(0, KD, T)
        uT = at(8256, NC, HALO + T)
        yT = at(12504, NC, T)
        qT = at(16632, NC, T)
        kT = at(20760, P + T)
        vN = at(21920, NT + 2, P)
        qmT = at(23200, NC, T)
        memN = at(27328, 2, 8 * P)
        memKT = at(29376, NC, MEM)
        kN = at(30400, 2, P)
        lastu = at(30656, NC, P)
        us = at(31168, NC, NB, TAPS)
        MG = 32768
        mergedT = at(MG, NT, KD, P)
        mergedS = at(MG + NT * KD * P, KD, NB)
        RG = MG + KD * T

        initialised = sem("initialised")
        loads = sem("loads")

        passed = sem("loop_waits_passed")

        def wait_loop(eng, sem, value):
            if isinstance(value, int) and value <= 0:
                return
            eng.wait_ge(sem, value)
            if not isinstance(value, int):
                eng.sem_inc(passed, 1)

        stores = sem("stores")
        n_stores = [0]

        def store(eng, dst, src):
            n_stores[0] += 16
            eng.dma_start(dst, src).then_inc(stores, 16)

        sq = at(MG, 2, T)
        sig = at(MG + 2 * T, 2, T)
        mT = at(MG + 4 * T, KD, MEM)
        std = at(RG + WRING * 1024, T)
        stdm = at(RG + WRING * 1024 + T, MEM)
        prod = at(RG + WRING * 1024 + T + MEM, NB, TAPS)
        wr = at(RG, WRING, KD, P)

        w_here = [sem(f"weights_here{i}") for i in range(WRING)]
        parts_here = [sem(f"part{i}_here") for i in range(4)]
        squared = sem("squared")
        summed = sem("summed")
        std_ready = sem("std_ready")
        h_ready = sem("h_ready")
        chunk_done = sem("chunk_done")
        set_free = [sem("psum_set0_free"), sem("psum_set1_free")]
        sig_ready = sem("sig_ready")
        dve1 = sem("dve1")
        cache_here = sem("conv_cache_here")
        padded = sem("padded")

        tab_here = sem("bias_table_here")
        tab_fill = sem("bias_table_filled")
        line_mm = sem("line_multiplied")
        line_ready = sem("line_ready")
        line_out = sem("line_out")
        bias_here = sem("flipped_bias_here")
        flipped = at(48900, HEADS, 2 * P)
        oh = at(50948, LINE)
        tab = at(50948 + LINE, HEADS)
        line = at(50948 + LINE + HEADS, LINE)

        def groups(s):
            return psum[:, 3 * s:3 * s + 3, 0:GC]

        with nc.Block() as block:
            @block.sync
            def _(sp):
                for i in range(4):
                    sp.dma_start(hT[:, 2 * i:2 * i + 2, :], xT[:, 2 * i:2 * i + 2, :]).then_inc(parts_here[i], 16)
                for dst, src in ((mT, memT), (g1s, g1), (gms, gm), (cw, conv_w), (cb, conv_b), (lng, ln_g),
                                 (lnb, ln_b), (sink, sinks_bc), (sink_s[0:32, :], sinks_s)):
                    sp.dma_start(dst, src).then_inc(loads, 16)
                for i in range(len(CHUNKS)):
                    if i == 4:
                        sp.dma_start(oh[0:33, 0:LINE - 1], onehot).then_inc(tab_here, 16)
                        sp.dma_start(tab[0:32, :], bias_tab).then_inc(tab_here, 16)
                    if i == WRING + 3:
                        sp.wait_ge(line_ready, 1)
                        sp.dma_start(scratch_line[:, 0:LINE - 1], line[0:HEADS, 0:LINE - 1]).then_inc(line_out, 16)
                        sp.wait_ge(line_out, 16)
                        skew = bass.AP(tensor=scratch_line.tensor, offset=0, ap=[[1, P], [LINE, HEADS], [1, 2 * P]])
                        sp.dma_start(flipped, skew).then_inc(bias_here, 16)
                    if i == WRING:
                        for c in range(NC):
                            sp.dma_start(us[:, c, :, 0:HALO], cacheT[:, c]).then_inc(cache_here, 16)
                    if i >= WRING:
                        sp.wait_ge(chunk_done, i - WRING + 1)
                    sp.dma_start(wr[:, i % WRING], w_chunks[i]).then_inc(w_here[i % WRING], 16)
                store(sp, conv_s[:, 0:HALO - 1, :], cache_conv[:, 1:HALO, :])
                store(sp, k_s[:, 0:WIN - 1, :], cache_k[:, 1:WIN, :])
                store(sp, v_s[:, 0:WIN - 1, :], cache_v[:, 1:WIN, :])

            @block.gpsimd
            def _(pool):
                pool.memset(ident, 0.0).then_inc(initialised, 1)
                pool.memset(ones, 1.0).then_inc(initialised, 1)
                pool.memset(eps, EPS).then_inc(initialised, 1)
                pool.iota(iota16, [[1, TOPK]], base=0, channel_multiplier=0,
                          allow_small_or_imprecise_dtypes=True).then_inc(initialised, 1)
                pool.wait_ge(initialised, 4)
                pool.affine_select(out=ident, in_=ident, compare_op=ALU.not_equal, fill=1.0, base=0,
                                   pattern=[[-1, P]], channel_multiplier=1).then_inc(initialised, 1)
                pool.wait_ge(initialised, 5)
                pool.memset(tab[32:33, :], NEG).then_inc(tab_fill, 1)
                pool.wait_ge(tab_fill, 1)
                pool.memset(uT[:, :, 0:HALO], 0.0).then_inc(padded, 1)
                pool.memset(kT[:, 0:P], 0.0).then_inc(padded, 1)
                pool.memset(vN[:, 0, :], 0.0).then_inc(padded, 1)

            @block.scalar
            def _(act):
                act.wait_ge(initialised, 5)
                for k in range(2 * KD):
                    if k < KD and k % 2 == 0:
                        act.wait_ge(parts_here[k // 2], 16)
                    if k == KD:
                        act.wait_ge(summed, KD)
                        act.activation(std.rearrange("p (g n) -> p g n", g=3), groups(0), ACT.Sqrt, bias=eps,
                                       scale=1.0 / D).then_inc(std_ready, 1)
                        act.wait_ge(loads, 16 * 9)
                    if k >= 2:
                        act.wait_ge(summed, k - 1)
                    src = hT[:, k, :] if k < KD else mT[:, k - KD, :]
                    act.activation(sq[:, k % 2, 0:src.shape[1]], src, ACT.Square).then_inc(squared, 1)
                act.wait_ge(summed, 2 * KD)
                act.activation(stdm, psum[:, 3, 0:MEM], ACT.Sqrt, bias=eps, scale=1.0 / D).then_inc(std_ready, 1)
                for i, (kind, c) in enumerate(CHUNKS):
                    if kind == "a":
                        continue
                    if i == 4:
                        act.wait_ge(line_mm, 1)
                        act.activation(line[0:HEADS, 0:LINE - 1], psum[0:HEADS, 7, 0:LINE - 1], ACT.Copy)\
                           .then_inc(line_ready, 1)
                    act.wait_ge(chunk_done, i + 1)
                    src = groups(i % 2)
                    if kind == "b":
                        if c >= 2:
                            act.wait_ge(set_free[1], c - 1)
                        act.activation(sig[:, c % 2, :].rearrange("p (g n) -> p g n", g=3), src, ACT.Sigmoid)\
                           .then_inc(sig_ready, 1)
                        act.wait_ge(sig_ready, c + 1)
                        act.sem_inc(set_free[0], 1)
                        continue
                    if kind == "k":
                        act.activation(kN[:, 0, :], psum[:, 6, 0:P], ACT.Copy)
                        act.activation(kN[0:NB, 1, :], psum[0:NB, 6, P:2 * P], ACT.Copy)
                        dst = kT[:, P:P + T].rearrange("p (g n) -> p g n", g=3)
                    elif kind == "v":
                        for b in range(2):
                            act.activation(vN[:, 1 + 4 * b:5 + 4 * b, :],
                                           psum[:, 3 * (i % 2) + b, :].rearrange("p (t n) -> p t n", n=P), ACT.Copy)
                        dst, src = vN[0:NB, NT + 1, :], psum[0:NB, 3 * (i % 2) + 2, 0:P]
                    elif kind == "mem":
                        dst, src = memN[:, :, c * P:(c + 1) * P], psum[:, 3 * (i % 2):3 * (i % 2) + 2, 0:P]
                    else:
                        dst = (qT if kind == "q" else qmT)[:, c, :].rearrange("p (g n) -> p g n", g=3)
                    act.activation(dst, src, ACT.Copy).then_inc(set_free[i % 2], 1)

            @block.tensor
            def _(pe):
                pe.wait_ge(initialised, 5)
                for k in range(2 * KD):
                    pe.wait_ge(squared, k + 1)
                    if k < KD:
                        for g in range(3):
                            mm = pe.matmul(psum[:, g, 0:GC], ones, sq[:, k % 2, g * GC:(g + 1) * GC],
                                           start=(k == 0), stop=(k == KD - 1))
                    else:
                        mm = pe.matmul(psum[:, 3, 0:MEM], ones, sq[:, k % 2, 0:MEM],
                                       start=(k == KD), stop=(k == 2 * KD - 1))
                    mm.then_inc(summed, 1)
                for i, (kind, c) in enumerate(CHUNKS):
                    if i == 3:
                        pe.wait_ge(tab_here, 32)
                        pe.wait_ge(tab_fill, 1)
                        pe.matmul(psum[0:HEADS, 7, 0:LINE - 1], tab[0:33, :], oh[0:33, 0:LINE - 1], start=True, stop=True)\
                          .then_inc(line_mm, 1)
                    pe.wait_ge(w_here[i % WRING], 16 * (i // WRING + 1))
                    if i < 2:
                        pe.wait_ge(std_ready, i + 1)
                    if i >= 2:
                        pe.wait_ge(set_free[i % 2], i // 2)
                    w = wr[:, i % WRING]
                    s = 3 * (i % 2)
                    for k in range(KD):
                        if i == 0:
                            pe.wait_ge(h_ready, k + 1)
                        first, last = k == 0, k == KD - 1
                        if kind in ("a", "b", "k", "q", "qm"):
                            for g in range(3):
                                mm = pe.matmul(psum[:, s + g, 0:GC], w[:, k, :], hT[:, k, g * GC:(g + 1) * GC],
                                               start=first, stop=last)
                    if kind == "k":
                        for k in range(KD):
                            pe.matmul(psum[:, 6, 0:P], hT[:, k, SEQ - P:SEQ], w[:, k, :],
                                      start=(k == 0), stop=(k == KD - 1))
                        for k in range(KD):
                            mm = pe.matmul(psum[0:NB, 6, P:2 * P], hT[:, k, SEQ:T], w[:, k, :],
                                           start=(k == 0), stop=(k == KD - 1))
                    if kind == "v":
                        for t in range(NT):
                            for k in range(KD):
                                pe.matmul(psum[:, s + t // 4, (t % 4) * P:(t % 4 + 1) * P],
                                          hT[:, k, t * P:(t + 1) * P], w[:, k, :],
                                          start=(k == 0), stop=(k == KD - 1))
                        for k in range(KD):
                            mm = pe.matmul(psum[0:NB, s + 2, 0:P], hT[:, k, SEQ:T], w[:, k, :],
                                           start=(k == 0), stop=(k == KD - 1))
                    if kind == "mem":
                        if c == 0:
                            pe.wait_ge(h_ready, 2 * KD)
                        for t in range(2):
                            for k in range(KD):
                                mm = pe.matmul(psum[:, s + t, 0:P], mT[:, k, t * P:(t + 1) * P], w[:, k, :],
                                               start=(k == 0), stop=(k == KD - 1))
                    mm.then_inc(chunk_done, 1)

            @block.vector
            def _(dve):
                n = [0]

                def link(ins):
                    n[0] += 1
                    ins.then_inc(dve1, 1)
                    dve.wait_ge(dve1, n[0])

                dve.wait_ge(std_ready, 1)
                dve.wait_ge(loads, 16 * 9)
                link(dve.reciprocal(std, std))
                for k in range(KD):
                    dve.scalar_tensor_tensor(out=hT[:, k, :], in0=hT[:, k, :], scalar=g1s[:, k:k + 1], in1=std,
                                             op0=ALU.mult, op1=ALU.mult).then_inc(h_ready, 1)
                dve.wait_ge(std_ready, 2)
                link(dve.reciprocal(stdm, stdm))
                for k in range(KD):
                    dve.scalar_tensor_tensor(out=mT[:, k, :], in0=mT[:, k, :], scalar=gms[:, k:k + 1], in1=stdm,
                                             op0=ALU.mult, op1=ALU.mult).then_inc(h_ready, 1)
                for c in range(NC):
                    dve.wait_ge(chunk_done, 2 * c + 2)
                    dve.wait_ge(sig_ready, c + 1)
                    dve.tensor_tensor(uT[:, c, HALO:HALO + T].rearrange("p (g n) -> p g n", g=3), groups(1),
                                      sig[:, c % 2, :].rearrange("p (g n) -> p g n", g=3), ALU.mult)\
                       .then_inc(set_free[1], 1)
                dve.wait_ge(padded, 3)
                dve.wait_ge(set_free[1], NC)
                dve.wait_ge(cache_here, 16 * NC)
                for c in range(NC):
                    acc = yT[:, c, 0:SEQ]
                    link(dve.tensor_scalar(acc, uT[:, c, 0:SEQ], cw[:, c, 0:1], cb[:, c:c + 1], ALU.mult, ALU.add))
                    for t in range(1, TAPS):
                        link(dve.scalar_tensor_tensor(out=acc, in0=uT[:, c, t:t + SEQ], scalar=cw[:, c, t:t + 1],
                                                      in1=acc, op0=ALU.mult, op1=ALU.add))
                    link(dve.tensor_copy(us[:, c, :, HALO], uT[:, c, HALO + SEQ:HALO + T]))
                    link(dve.tensor_tensor(prod, us[:, c], cw[:, c, :].unsqueeze(1).broadcast_to([P, NB, TAPS]),
                                           ALU.mult))
                    link(dve.tensor_reduce(yT[:, c, SEQ:T], prod, AX.X, ALU.add))
                    link(dve.tensor_scalar(yT[:, c, SEQ:T], yT[:, c, SEQ:T], cb[:, c:c + 1], None, ALU.add))

        lsum = sem("ln_summed")
        lcent = sem("ln_centred")
        lsq = sem("ln_squared")
        lvar = sem("ln_variance")
        lstd = sem("ln_std")
        lrec = sem("ln_reciprocal")
        lnorm = sem("ln_normed")
        lsilu = sem("ln_silu")
        turned_u = sem("conv_rows_turned")
        u_rows = sem("conv_rows_here")
        sq4 = at(MG, 3, NC, GC)
        lnstd = at(MG + 3 * NC * GC, 3, GC)
        lastsu = at(RG, NC, P)

        with nc.Block() as block:
            @block.tensor
            def _(pe):
                for g in range(3):
                    for c in range(NC):
                        mm = pe.matmul(psum[:, g, 0:GC], ones, yT[:, c, g * GC:(g + 1) * GC],
                                       start=(c == 0), stop=(c == NC - 1))
                    mm.then_inc(lsum, 1)
                for c in range(NC):
                    pe.transpose(psum[0:HALO, 6, c * P:(c + 1) * P], uT[:, c, SEQ:SEQ + HALO], ident)
                for c in range(NC):
                    mm = pe.transpose(psum[0:NB, 7, c * P:(c + 1) * P], uT[:, c, HALO + SEQ:HALO + T], ident)
                mm.then_inc(turned_u, 1)
                for g in range(3):
                    pe.wait_ge(lsq, NC * (g + 1))
                    for c in range(NC):
                        mm = pe.matmul(psum[:, 3 + g, 0:GC], ones, sq4[:, g, c, :],
                                       start=(c == 0), stop=(c == NC - 1))
                    mm.then_inc(lvar, 1)

            @block.vector
            def _(dve):
                for g in range(3):
                    dve.wait_ge(lsum, g + 1)
                    for c in range(NC):
                        y = yT[:, c, g * GC:(g + 1) * GC]
                        dve.scalar_tensor_tensor(out=y, in0=psum[:, g, 0:GC], scalar=-1.0 / CH, in1=y,
                                                 op0=ALU.mult, op1=ALU.add).then_inc(lcent, 1)
                dve.wait_ge(lcent, 3 * NC)
                for g in range(3):
                    dve.wait_ge(lstd, g + 1)
                    dve.reciprocal(lnstd[:, g, :], lnstd[:, g, :]).then_inc(lrec, 1)
                    dve.wait_ge(lrec, g + 1)
                    for c in range(NC):
                        y = yT[:, c, g * GC:(g + 1) * GC]
                        dve.tensor_tensor(y, y, lnstd[:, g, :], ALU.mult).then_inc(lnorm, 1)

            @block.scalar
            def _(act):
                for g in range(3):
                    for c in range(NC):
                        act.wait_ge(lcent, g * NC + c + 1)
                        act.activation(sq4[:, g, c, :], yT[:, c, g * GC:(g + 1) * GC], ACT.Square).then_inc(lsq, 1)
                act.wait_ge(turned_u, 1)
                act.activation(lastu[0:HALO], psum[0:HALO, 6, :].rearrange("p (c n) -> p c n", c=NC), ACT.Copy)\
                   .then_inc(u_rows, 1)
                act.activation(lastsu[0:NB], psum[0:NB, 7, :].rearrange("p (c n) -> p c n", c=NC), ACT.Copy)\
                   .then_inc(u_rows, 1)
                for g in range(3):
                    act.wait_ge(lvar, g + 1)
                    act.activation(lnstd[:, g, :], psum[:, 3 + g, 0:GC], ACT.Sqrt, bias=eps, scale=1.0 / CH)\
                       .then_inc(lstd, 1)
                for g in range(3):
                    for c in range(NC):
                        y = yT[:, c, g * GC:(g + 1) * GC]
                        act.wait_ge(lnorm, g * NC + c + 1)
                        act.activation(y, y, ACT.Silu, bias=lnb[:, c:c + 1], scale=lng[:, c:c + 1])\
                           .then_inc(lsilu, 1)

            @block.sync
            def _(sp):
                sp.wait_ge(u_rows, 2)
                store(sp, conv_p, lastu[0:HALO].rearrange("p c n -> p (c n)"))
                store(sp, conv_s[:, HALO - 1, :], lastsu[0:NB].rearrange("p c n -> p (c n)"))
                store(sp, k_p, kN[:, 0, :])
                store(sp, k_s[:, WIN - 1, :], kN[0:NB, 1, :])
                store(sp, v_p, vN[:, NT, :])
                store(sp, v_s[:, WIN - 1, :], vN[0:NB, NT + 1, :])
                for t in range(2):
                    store(sp, mk_p[t * P:(t + 1) * P, :], memN[:, t, 0:CH])
                    store(sp, mv_p[t * P:(t + 1) * P, :], memN[:, t, CH:2 * CH])
                sp.wait_ge(stores, n_stores[0])

        WT = 6
        A0 = MG + WT * KD * P
        bias = at(A0, HEADS, 2 * P)
        bias0 = at(A0 + 2048, HEADS, 2 * P)
        prob = at(A0 + 4096, 2, 4, 2 * P)
        probT = at(A0 + 6144, 2, 8, P)
        Q0 = A0 + 8192
        kv_slots = [at(Q0, CH * 2), at(Q0 + 1024, CH * 2)] + [at(A0 + 1024 * i, CH * 2) for i in range(4)]
        KV = len(kv_slots)

        def ring_keys(b):
            return kv_slots[b % KV].rearrange("p (h n) -> p h n", h=NC)

        def ring_values(b):
            return kv_slots[(NB + b) % KV].rearrange("p (t n) -> p t n", t=2)

        ck = at(Q0 + 2048, NB, WIN + 1)
        cv = at(Q0 + 3080, NB, P)
        bias_s = at(Q0 + 4104, 2, WIN + 1)
        csig = at(Q0 + 4362, 2 * P)
        assert Q0 + 4362 + 2 * P <= 52100
        QM = 30400
        qmask = at(QM, NB, 32)
        qmmask = at(QM + 256, 32, 32)
        ps_ = at(QM + 1280, 2, WIN + 1)
        psm = at(QM + 1538, MEM)
        pst = at(QM + 1794, 2, 32)
        pslast = at(QM + 1858, 2, 32)
        pmt = at(QM + 1922, 2, 32)
        flip = at(QM + 1986, P)
        cgw = at(8256, 2, KD + NC, P)
        vlast = at(8256 + 2 * 1536, NB, P)
        GRING = 6
        gw = [cgw[:, i] for i in range(2)] + [at(RG + i * 1536, KD + NC, P) for i in range(GRING - 2)]
        stat = small[:, 0:320]
        units = [("swa", n, h) for n in range(NT) for h in range(2)] + [("mem", n, 0) for n in range(NT)]
        NU = len(units)
        mx, nm, rs, es, rd = (stat[:, 8 * i:8 * i + 8].rearrange("p (b h) -> p b h", b=2) for i in range(5))
        mxs, nms, rss, ess, rds = (stat[:, 40 + 2 * i:42 + 2 * i] for i in range(5))
        mxm, nmm, rsm, rdm = (stat[:, 50 + i:51 + i] for i in range(4))

        bias_s_here = sem("sample_bias_here")
        unflipped = sem("bias_unflipped")
        bias_ready = sem("bias_ready")
        s_done = sem("scores_done")
        pre_done = sem("maxima_done")
        exp_done = sem("exp_done")
        norm_done = sem("probs_normed")
        t_done = sem("probs_turned")
        tev_done = sem("turned_probs_copied")
        pv_done = sem("pv_done")
        o_done = sem("attention_copied")
        mk_turned = sem("mem_k_turned")
        mk_copied = sem("mem_k_copied")
        dve2 = sem("dve2")
        smp_in = sem("sample_swa_cache_here")
        vs_out = sem("vs_out")
        kv_here = [sem(f"sample_memory{i}_here") for i in range(KV)]
        masked = sem("queries_masked")
        ss_done = sem("sample_scores_done")
        kv_used = sem("sample_memory_used")
        smax = sem("sample_maxima")
        sexp = sem("sample_exp")
        snorm = sem("sample_normed")
        sturn = sem("sample_turned")
        scopy = sem("sample_copied")
        spv = sem("sample_pv")
        so = sem("sample_attention_copied")
        cgw_here = [sem("conv_gate_weights0_here"), sem("conv_gate_weights1_here")]
        gw_here = [sem(f"gate_weights_here{i}") for i in range(GRING)]
        cpair = sem("conv_pair_done")
        cgate = sem("conv_gate_ready")
        ctaken = sem("conv_pair_taken")
        WG = WT // 2
        assert NU == KD * WG

        with nc.Block() as block:
            @block.sync
            def _(sp):
                for m in range(2):
                    sp.dma_start(cgw[:, m], w_gates[3 * m]).then_inc(cgw_here[m], 16)
                sp.dma_start(scratch_vs, vN[0:NB, NT + 1, :]).then_inc(vs_out, 16)
                sp.wait_ge(unflipped, 1)
                sp.dma_start(ck[:, :, 0:WIN], cache_kT).then_inc(smp_in, 16)
                sp.dma_start(cv, cache_v.rearrange("b w d -> w b d")).then_inc(smp_in, 16)
                for c in range(4):
                    src = bass.AP(tensor=scratch_line.tensor, offset=((c // 2) * 4 + c % 2) * LINE + P - 1,
                                  ap=[[0, NB], [2 * LINE, 2], [1, WIN + 1]])
                    sp.dma_start(bias_s[c * NB:(c + 1) * NB], src).then_inc(bias_s_here, 16)
                sp.wait_ge(vs_out, 16)
                sp.dma_start(vlast[0:1], scratch_vs.rearrange("(o b) d -> o b d", o=1)).then_inc(smp_in, 16)
                def memory(i):
                    if i < NB:
                        sp.dma_start(ring_keys(i), memkT[i]).then_inc(kv_here[i % KV], 16)
                    else:
                        sp.dma_start(ring_values(i - NB), cache_mv[i - NB].rearrange("(t p) n -> p t n", p=P))\
                          .then_inc(kv_here[i % KV], 16)

                for i in range(2):
                    memory(i)
                for m in range(2, KD + 2):
                    sp.wait_ge(cpair, WG * (m - 1))
                    if m < KD:
                        sp.dma_start(cgw[:, m % 2], w_gates[3 * m]).then_inc(cgw_here[m % 2], 16)
                    if m == KD - 1:
                        sp.wait_ge(norm_done, 2 * NT)
                        for i in range(2, KV):
                            memory(i)
                    if m >= KD:
                        sp.dma_start(gw[m - KD], w_gates[m - KD]).then_inc(gw_here[m - KD], 16)
                for i in range(KV, 2 * NB):
                    sp.wait_ge(kv_used, i - KV + 1)
                    memory(i)

            @block.gpsimd
            def _(pool):
                pool.memset(flip, 0.0).then_inc(tab_fill, 1)
                pool.wait_ge(tab_fill, 2)
                pool.affine_select(out=flip, in_=flip, compare_op=ALU.not_equal, fill=1.0, base=-(P - 1),
                                   pattern=[[1, P]], channel_multiplier=1).then_inc(tab_fill, 1)
                pool.memset(bias0[:, :, 0:P], NEG).then_inc(bias_ready, 1)
                pool.memset(qmask, 0.0).then_inc(masked, 1)
                pool.memset(qmmask, 0.0).then_inc(masked, 1)
                pool.wait_ge(masked, 2)
                for c in range(NC):
                    qm_d = bass.AP(tensor=arena.ap().tensor if callable(arena.ap) else arena, offset=QM + c * NB,
                                   ap=[[52100, P], [33, NB]])
                    pool.tensor_copy(qm_d, qT[:, c, SEQ:T]).then_inc(masked, 1)
                    qmm_d = bass.AP(tensor=arena.ap().tensor if callable(arena.ap) else arena,
                                    offset=QM + 256 + 33 * c * NB, ap=[[52100, P], [33, NB]])
                    pool.tensor_copy(qmm_d, qmT[:, c, SEQ:T]).then_inc(masked, 1)
                pool.wait_ge(smp_in, 48)
                pool.tensor_copy(ck[:, :, WIN], kT[:, P + SEQ:P + T]).then_inc(masked, 1)

            @block.tensor
            def _(pe):
                for t in range(2):
                    for h in range(NC):
                        mm = pe.transpose(psum[:, 4 + t, h * P:(h + 1) * P], memN[:, t, h * P:(h + 1) * P], ident)
                mm.then_inc(mk_turned, 1)
                pe.wait_ge(bias_here, 16)
                pe.wait_ge(tab_fill, 3)
                for h in range(HEADS):
                    mm = pe.matmul(psum[:, h // 2, (h % 2) * 256:(h % 2) * 256 + 256], flip, flipped[:, h, :],
                                   start=True, stop=True)
                mm.then_inc(unflipped, 1)
                pe.wait_ge(mk_copied, 2)
                pe.wait_ge(bias_ready, 3)
                for s in range(NU + 2):
                    if s < NU:
                        kind, n, hf = units[s]
                        if s >= 2:
                            pe.wait_ge(pre_done if kind == "swa" or units[s - 2][0] == "swa" else exp_done, s - 1)
                            if kind == "mem":
                                pe.wait_ge(exp_done, s - 1)
                        S = psum[:, 2 * (s % 2):2 * (s % 2) + 2, :].rearrange("p b (h k) -> p (b h) k", k=2 * P)
                        for i in range(4):
                            if kind == "swa":
                                j, c = i // 2, 2 * hf + i % 2
                                rows = slice(64 * j, 64 * j + 64)
                                mm = pe.matmul(S[:, i, :], qT[rows, c, n * P:(n + 1) * P],
                                               kT[rows, n * P:n * P + 2 * P], start=True, stop=True)
                            else:
                                mm = pe.matmul(S[:, i, :], qmT[:, i, n * P:(n + 1) * P], memKT[:, i, :],
                                               start=True, stop=True)
                        mm.then_inc(s_done, 1)
                        m, g = s // WG, s % WG
                        if g == 0:
                            pe.wait_ge(cgw_here[m % 2], 16 * (m // 2 + 1))
                        if s:
                            pe.wait_ge(ctaken, s)
                        cols = slice(2 * g * P, 2 * (g + 1) * P)
                        for k in range(KD):
                            pe.matmul(psum[:, 7, 0:2 * P], cgw[:, m % 2, k, :], hT[:, k, cols],
                                      start=(k == 0), stop=(k == KD - 1))
                        for c in range(NC):
                            mm = pe.matmul(psum[:, 7, 2 * P:4 * P], cgw[:, m % 2, KD + c, :], yT[:, c, cols],
                                           start=(c == 0), stop=(c == NC - 1))
                        mm.then_inc(cpair, 1)
                    if 1 <= s <= NU:
                        u = s - 1
                        pe.wait_ge(norm_done, u + 1)
                        if u >= 1:
                            pe.wait_ge(tev_done, u)
                        for i in range(8):
                            mm = pe.transpose(psum[:, 4 + i // 4, (i % 4) * P:(i % 4 + 1) * P],
                                              prob[:, u % 2, i // 2, (i % 2) * P:(i % 2 + 1) * P], ident)
                        mm.then_inc(t_done, 1)
                    if s >= 2:
                        u = s - 2
                        kind, n, hf = units[u]
                        pe.wait_ge(tev_done, u + 1)
                        if u >= 1:
                            pe.wait_ge(o_done, u)
                        for i in range(4):
                            for kt in range(2):
                                pt = probT[:, u % 2, 2 * i + kt, :]
                                if kind == "swa":
                                    j, cc = i // 2, i % 2
                                    mm = pe.matmul(psum[64 * j:64 * j + 64, 6, cc * P:(cc + 1) * P],
                                                   vN[:, n + kt, 64 * j:64 * j + 64], pt, start=(kt == 0), stop=(kt == 1))
                                else:
                                    mm = pe.matmul(psum[:, 6, i * P:(i + 1) * P],
                                                   memN[:, kt, CH + i * P:CH + (i + 1) * P], pt,
                                                   start=(kt == 0), stop=(kt == 1))
                        mm.then_inc(pv_done, 1)
                pe.wait_ge(masked, 11)
                pe.wait_ge(norm_done, NU)
                pe.wait_ge(ctaken, NU)
                for j in range(2):
                    rows = slice(64 * j, 64 * j + 64)
                    for b in range(NB):
                        mm = pe.matmul(psum[0:32, j, 0:WIN + 1], qmask[rows, b, :], ck[rows, b, :],
                                       start=(b == 0), stop=(b == NB - 1))
                mm.then_inc(ss_done, 1)
                for b in range(NB):
                    pe.wait_ge(kv_here[b % KV], 16 * (b // KV + 1))
                    for h in range(NC):
                        mm = pe.matmul(psum[0:32, 2, 0:MEM], qmmask[:, h * NB + b, :], ring_keys(b)[:, h, :],
                                       start=(b == 0 and h == 0), stop=(b == NB - 1 and h == NC - 1))
                    mm.then_inc(kv_used, 1)
                pe.wait_ge(snorm, 2)
                pe.wait_ge(tev_done, NU)
                for j in range(2):
                    pe.transpose(psum[:, 4, j * 32:(j + 1) * 32], ps_[0:32, j, 0:WIN], ident[0:32, 0:32])
                for j in range(2):
                    pe.transpose(psum[:, 4, 64 + j * 32:64 + (j + 1) * 32], psm[0:32, j * P:(j + 1) * P],
                                 ident[0:32, 0:32])
                for j in range(2):
                    mm = pe.transpose(psum[0:1, 5, j * 32:(j + 1) * 32], ps_[0:32, j, WIN:WIN + 1],
                                      ident[0:32, 0:32])
                mm.then_inc(sturn, 1)
                pe.wait_ge(scopy, 3)
                pe.wait_ge(smp_in, 48)
                pe.wait_ge(o_done, NU)
                for b in range(NB):
                    for j in range(2):
                        o = psum[64 * j:64 * j + 64, 6, 0:32].rearrange("p (c b) -> p c b", b=NB)[:, :, b]
                        w = pst[:, j, :].rearrange("p (c b) -> p c b", b=NB)[:, :, b]
                        wl = pslast[0:1, j, :].rearrange("p (c b) -> p c b", b=NB)[:, :, b]
                        pe.matmul(o, cv[:, b, 64 * j:64 * j + 64], w, start=True, stop=False)
                        mm = pe.matmul(o, vlast[0:1, b, 64 * j:64 * j + 64], wl, start=False, stop=True)
                mm.then_inc(spv, 1)
                for b in range(NB):
                    pe.wait_ge(kv_here[(NB + b) % KV], 16 * ((NB + b) // KV + 1))
                    for h in range(NC):
                        r = h * NB + b
                        for t in range(2):
                            mm = pe.matmul(psum[:, 7, r:r + 1], ring_values(b)[:, t, h * P:(h + 1) * P],
                                           pmt[:, t, r:r + 1], start=(t == 0), stop=(t == 1))
                    mm.then_inc(kv_used, 1)

            @block.vector
            def _(dve):
                n_ = [0]

                def link(ins):
                    n_[0] += 1
                    ins.then_inc(dve2, 1)
                    dve.wait_ge(dve2, n_[0])

                dve.wait_ge(unflipped, 1)
                dve.wait_ge(bias_ready, 3)
                for s in range(NU + 1):
                    if s >= 1:
                        m, g = (s - 1) // WG, (s - 1) % WG
                        dve.wait_ge(cgate, s)
                        dve.tensor_tensor(mergedT[:, 2 * g:2 * g + 2, m, :], csig.rearrange("p (t n) -> p t n", t=2),
                                          psum[:, 7, 2 * P:4 * P].rearrange("p (t n) -> p t n", t=2), ALU.mult)\
                           .then_inc(ctaken, 1)
                    if s < NU:
                        kind, n, hf = units[s]
                        b = s % 2
                        S = psum[:, 2 * b:2 * b + 2, :].rearrange("p b (h k) -> p (b h) k", k=2 * P)
                        dve.wait_ge(s_done, s + 1)
                        if s >= 2:
                            dve.wait_ge(t_done, s - 1)
                        if kind == "swa":
                            bb = (bias if n else bias0)[:, 4 * hf:4 * hf + 4, :]
                            link(dve.scalar_tensor_tensor(out=prob[:, b], in0=S, scalar=SCALE, in1=bb,
                                                          op0=ALU.mult, op1=ALU.add))
                            link(dve.tensor_reduce(mx[:, b], prob[:, b], AX.X, ALU.max))
                            link(dve.tensor_tensor(mx[:, b], mx[:, b], sink[:, 4 * hf:4 * hf + 4], ALU.max))
                            link(dve.tensor_tensor(es[:, b], sink[:, 4 * hf:4 * hf + 4], mx[:, b], ALU.subtract))
                            dve.tensor_scalar(nm[:, b], mx[:, b], -1.0, None, ALU.mult).then_inc(pre_done, 1)
                        else:
                            link(dve.tensor_reduce(mx[:, b], S, AX.X, ALU.max))
                            dve.tensor_scalar(nm[:, b], mx[:, b], -MSCALE, None, ALU.mult).then_inc(pre_done, 1)
                    if s >= 1:
                        u = s - 1
                        b = u % 2
                        dve.wait_ge(exp_done, u + 1)
                        if units[u][0] == "swa":
                            link(dve.tensor_tensor(rs[:, b], rs[:, b], es[:, b], ALU.add))
                        link(dve.reciprocal(rd[:, b], rs[:, b]))
                        dve.tensor_tensor(prob[:, b], prob[:, b],
                                          rd[:, b].unsqueeze(2).broadcast_to([P, 4, 2 * P]), ALU.mult)\
                           .then_inc(norm_done, 1)
                dve.wait_ge(ss_done, 1)
                dve.wait_ge(bias_s_here, 16 * 4)
                sw = ps_[0:32]
                link(dve.scalar_tensor_tensor(out=sw, in0=psum[0:32, 0:2, 0:WIN + 1], scalar=SCALE,
                                              in1=bias_s[0:32], op0=ALU.mult, op1=ALU.add))
                link(dve.tensor_reduce(mxs[0:32], sw, AX.X, ALU.max))
                link(dve.tensor_tensor(mxs[0:32], mxs[0:32], sink_s[0:32], ALU.max))
                link(dve.tensor_tensor(ess[0:32], sink_s[0:32], mxs[0:32], ALU.subtract))
                dve.tensor_scalar(nms[0:32], mxs[0:32], -1.0, None, ALU.mult).then_inc(smax, 1)
                dve.wait_ge(kv_used, NB)
                link(dve.tensor_reduce(mxm[0:32], psum[0:32, 2, 0:MEM], AX.X, ALU.max))
                dve.tensor_scalar(nmm[0:32], mxm[0:32], -MSCALE, None, ALU.mult).then_inc(smax, 1)
                dve.wait_ge(sexp, 2)
                link(dve.tensor_tensor(rss[0:32], rss[0:32], ess[0:32], ALU.add))
                link(dve.reciprocal(rds[0:32], rss[0:32]))
                dve.tensor_tensor(sw, sw, rds[0:32].unsqueeze(2).broadcast_to([32, 2, WIN + 1]), ALU.mult)\
                   .then_inc(snorm, 1)
                link(dve.reciprocal(rdm[0:32], rsm[0:32]))
                dve.tensor_scalar(psm[0:32], psm[0:32], rdm[0:32], None, ALU.mult).then_inc(snorm, 1)

            @block.scalar
            def _(act):
                act.wait_ge(mk_turned, 1)
                for t in range(2):
                    act.activation(memKT[:, :, t * P:(t + 1) * P],
                                   psum[:, 4 + t, :].rearrange("p (h n) -> p h n", h=NC), ACT.Copy)\
                       .then_inc(mk_copied, 1)
                act.wait_ge(unflipped, 1)
                turned_back = psum[:, 0:4, :].rearrange("p b (h k) -> p (b h) k", k=2 * P)
                act.activation(bias, turned_back, ACT.Copy).then_inc(bias_ready, 1)
                act.activation(bias0[:, :, P:2 * P], turned_back[:, :, P:2 * P], ACT.Copy).then_inc(bias_ready, 1)
                for s in range(NU + 2):
                    if s < NU:
                        kind, n, hf = units[s]
                        b = s % 2
                        S = psum[:, 2 * b:2 * b + 2, :].rearrange("p b (h k) -> p (b h) k", k=2 * P)
                        act.wait_ge(pre_done, s + 1)
                        if kind == "swa":
                            act.activation(es[:, b], es[:, b], ACT.Exp)
                        for i in range(4):
                            src = prob[:, b, i, :] if kind == "swa" else S[:, i, :]
                            ins = act.activation(prob[:, b, i, :], src, ACT.Exp, bias=nm[:, b, i:i + 1],
                                                 scale=1.0 if kind == "swa" else MSCALE,
                                                 accum_out=rs[:, b, i:i + 1])
                        ins.then_inc(exp_done, 1)
                        act.wait_ge(cpair, s + 1)
                        if s:
                            act.wait_ge(ctaken, s)
                        act.activation(csig, psum[:, 7, 0:2 * P], ACT.Sigmoid).then_inc(cgate, 1)
                    if 1 <= s <= NU:
                        u = s - 1
                        act.wait_ge(t_done, u + 1)
                        if u >= 2:
                            act.wait_ge(pv_done, u - 1)
                        act.activation(probT[:, u % 2],
                                       psum[:, 4:6, :].rearrange("p b (i n) -> p (b i) n", n=P), ACT.Copy)\
                           .then_inc(tev_done, 1)
                    if s >= 2:
                        u = s - 2
                        kind, n, hf = units[u]
                        act.wait_ge(pv_done, u + 1)
                        if kind == "swa":
                            dst = qT[:, 2 * hf:2 * hf + 2, n * P:(n + 1) * P]
                            src = psum[:, 6, 0:2 * P].rearrange("p (c n) -> p c n", c=2)
                        else:
                            dst = qmT[:, :, n * P:(n + 1) * P]
                            src = psum[:, 6, :].rearrange("p (c n) -> p c n", c=4)
                        act.activation(dst, src, ACT.Copy).then_inc(o_done, 1)
                act.wait_ge(smax, 1)
                act.activation(ess[0:32], ess[0:32], ACT.Exp)
                for j in range(2):
                    ins = act.activation(ps_[0:32, j, :], ps_[0:32, j, :], ACT.Exp, bias=nms[0:32, j:j + 1],
                                         accum_out=rss[0:32, j:j + 1])
                ins.then_inc(sexp, 1)
                act.wait_ge(smax, 2)
                act.activation(psm[0:32], psum[0:32, 2, 0:MEM], ACT.Exp, bias=nmm[0:32], scale=MSCALE,
                               accum_out=rsm[0:32]).then_inc(sexp, 1)
                act.wait_ge(sturn, 1)
                act.activation(pst, psum[:, 4, 0:64].rearrange("p (j r) -> p j r", j=2), ACT.Copy).then_inc(scopy, 1)
                act.activation(pmt, psum[:, 4, 64:128].rearrange("p (j r) -> p j r", j=2), ACT.Copy)\
                   .then_inc(scopy, 1)
                act.activation(pslast[0:1], psum[0:1, 5, 0:64].rearrange("p (j r) -> p j r", j=2), ACT.Copy)\
                   .then_inc(scopy, 1)
                act.wait_ge(spv, 1)
                act.wait_ge(masked, 10)
                act.activation(qT[:, :, SEQ:T], psum[:, 6, 0:32].rearrange("p (c b) -> p c b", b=NB), ACT.Copy)\
                   .then_inc(so, 1)
                act.wait_ge(kv_used, 2 * NB)
                act.activation(qmT[:, :, SEQ:T], psum[:, 7, 0:32].rearrange("p (c b) -> p c b", b=NB), ACT.Copy)\
                   .then_inc(so, 1)

        groups3 = [(0, 3 * P), (3 * P, 3 * P), (6 * P, 2 * P + NB)]
        gsig = at(RG + (GRING - 2) * 1536, 2, 3 * P)
        gprod = at(RG + (GRING - 2) * 1536 + 6 * P, 2, 3 * P)
        pair_done = sem("pair_done")
        gate_ready = sem("gate_ready")
        taken = sem("pair_taken")
        added = sem("added")
        branch = [yT, qT, qmT]
        pairs = [(m, br, g) for m in range(KD) for br in range(3) for g in range(3) if br or g == 2]

        def merged_parts(m, g):
            if g < 2:
                return [(mergedT[:, 3 * g:3 * g + 3, m, :], 0, 3)]
            return [(mergedT[:, 6:8, m, :], 0, 2), (mergedS[:, m:m + 1, :], 2 * P, 0)]

        def columns(v, first, tiles):
            return v[:, first:first + tiles * P].rearrange("p (t n) -> p t n", t=tiles) if tiles else \
                v[:, first:first + NB].rearrange("p (t n) -> p t n", t=1)

        with nc.Block() as block:
            @block.sync
            def _(sp):
                for i in range(2, 3 * KD):
                    if i >= GRING:
                        q = i - GRING
                        sp.wait_ge(pair_done, 7 * (q // 3) + (1, 4, 7)[q % 3])
                    sp.dma_start(gw[i % GRING], w_gates[i]).then_inc(gw_here[i % GRING], 16)

            @block.tensor
            def _(pe):
                for i, (m, br, g) in enumerate(pairs):
                    load = 3 * m + br
                    w = gw[load % GRING]
                    pe.wait_ge(gw_here[load % GRING], 16 * (load // GRING + 1))
                    if i >= 4:
                        pe.wait_ge(taken, i - 3)
                    first, n = groups3[g]
                    cols = slice(first, first + n)
                    b = 2 * (i % 4)
                    for k in range(KD):
                        pe.matmul(psum[:, b, 0:n], w[:, k, :], hT[:, k, cols], start=(k == 0), stop=(k == KD - 1))
                    for c in range(NC):
                        mm = pe.matmul(psum[:, b + 1, 0:n], w[:, KD + c, :], branch[br][:, c, cols],
                                       start=(c == 0), stop=(c == NC - 1))
                    mm.then_inc(pair_done, 1)

            @block.scalar
            def _(act):
                for i, (m, br, g) in enumerate(pairs):
                    n = groups3[g][1]
                    act.wait_ge(pair_done, i + 1)
                    if i >= 2:
                        act.wait_ge(taken, i - 1)
                    act.activation(gsig[:, i % 2, 0:n], psum[:, 2 * (i % 4), 0:n], ACT.Sigmoid)\
                       .then_inc(gate_ready, 1)

            @block.vector
            def _(dve):
                n_add = 0
                for i, (m, br, g) in enumerate(pairs):
                    n = groups3[g][1]
                    dve.wait_ge(gate_ready, i + 1)
                    if n_add:
                        dve.wait_ge(added, n_add)
                    value = psum[:, 2 * (i % 4) + 1, :]
                    if br:
                        dve.tensor_tensor(gprod[:, i % 2, 0:n], gsig[:, i % 2, 0:n], value[:, 0:n], ALU.mult)\
                           .then_inc(taken, 1)
                        dve.wait_ge(taken, i + 1)
                        for out, first, tiles in merged_parts(m, g):
                            dve.tensor_tensor(out, out, columns(gprod[:, i % 2, :], first, tiles), ALU.add)\
                               .then_inc(added, 1)
                            n_add += 1
                    else:
                        parts = merged_parts(m, g)
                        for out, first, tiles in parts:
                            dve.tensor_tensor(out, columns(gsig[:, i % 2, :], first, tiles),
                                              columns(value, first, tiles), ALU.mult)\
                               .then_inc(taken if out is parts[-1][0] else added, 1)
                        n_add += len(parts) - 1

        xb = at(0, NT, D)
        wq = at(8192, KD, D)
        keys = at(16384, HEADS, 2 * NKEYS)
        scur = at(18432, HEADS, 2, NKEYS)
        xcur = at(20480, D)
        x1cur = at(21504, D)
        gfb = at(22528, D)
        ybuf = at(23552, D)
        xbT = at(24576, KD, P)
        pqT = at(25600, HEADS, P)
        E0 = 26624
        oneh = at(E0, 2, TOPK, TOPK)
        oneh2 = at(E0 + 512, 2, TOPK, TOPK)
        cand = at(E0 + 1024, TOPK, TOPK)
        cand2 = at(E0 + 1280, TOPK, TOPK)
        stmp = at(E0 + 1536, 2, NKEYS)
        E1 = E0 + 1792
        sv = at(E1, HEADS, 2, TOPK)
        si = at(E1 + 256, HEADS, 2, TOPK).bitcast(U32)
        sif = at(E1 + 512, HEADS, 2, TOPK)
        best = at(E1 + 768, HEADS, TOPK)
        ci = at(E1 + 896, HEADS, TOPK).bitcast(U32)
        ij = at(E1 + 1024, HEADS, 2, TOPK).bitcast(U32)
        ijf = at(E1 + 1280, HEADS, 2, TOPK)
        pick = at(E1 + 1536, HEADS, 2, TOPK)
        idN = at(E1 + 1792, SLOTS).bitcast(U32)
        idD = at(E1 + 1920, SLOTS).bitcast(U32)
        idU = at(E1 + 2048, SLOTS).bitcast(U32)
        gateN = at(E1 + 2176, HEADS, TOPK)
        gateD = at(E1 + 2304, SLOTS)
        dots = at(E1 + 2432, SLOTS)
        coef = at(E1 + 2560, SLOTS)
        gel = at(E1 + 2688, SLOTS)
        diag = at(E1 + 2816, 4, P)
        xnext = at(E1 + 3328, D)
        assert E1 + 3328 + D <= MG
        wo = at(RG, KD, D)
        x1s = at(RG + 8192, D)
        xbs = at(RG + 9216, D)
        xin = at(21504, 2, D)
        g2b = at(23552, D)
        rowD = at(MG, DRING, D)
        rowU = at(MG + DRING * D, URING, D)
        R2 = NB * HEADS
        st2 = small[:, 320:352]
        st3 = small[:, 352:400]
        hsum, hrec = st3[:, 0:8], st3[:, 8:16]
        msq, mrec = st3[:, 16:17], st3[:, 17:18]

        x1_out = [sem("x1_out0"), sem("x1_out1")]
        x_here = [sem("x_here0"), sem("x_here1")]
        g2_here = sem("second_gain_here")
        WO_SLICES = ((0, 1), (1, 2), (2, 4), (4, KD))
        o_mm = sem("out_product")
        x1_done = sem("x1_done")
        x1_sq = sem("x1_squared")
        x1_std = sem("x1_std")
        x1_rec = sem("x1_reciprocal")
        xb_done = sem("xb_done")
        wq_here = sem("peer_w_q_here")
        key_zero = sem("key_zero")
        xnext_ready = sem("next_x_copied")
        xT_done = sem("xb_turned")
        xT_copied = sem("xb_turned_copied")
        pq_done = sem("peer_q_done")
        pq_copied = sem("peer_q_copied")
        sc_done = sem("peer_scores_done")
        sc_copied = sem("peer_scores_copied")
        smp_out = sem("sample_rows_out")
        sel = sem("select_step")
        sel_exp = sem("select_exp")

        xcur_here = sem("block_x_copied")
        ids_ready = sem("expert_lists_ready")
        gD = [sem(f"down_rows_here{i}") for i in range(DRING)]
        gU = [sem(f"up_rows_here{i}") for i in range(URING)]
        dot_done = sem("dots_done")
        gelu1 = sem("gelu_first_half")
        gelu2 = sem("gelu_second_half")
        coef1 = sem("coefficients_first_half")
        coef2 = sem("coefficients_second_half")
        gates_moved = sem("gates_moved")
        diag_ready = sem("diagonal_ready")
        up_done = sem("up_products_done")
        x1_here = sem("x1_here")
        y_sum = sem("y_summed")
        y_sq = sem("y_squared")
        y_std = sem("y_std")
        y_rec = sem("y_reciprocal")
        y_ready = sem("y_ready")
        y_out = sem("y_out")
        gf_here = sem("final_gain_here")

        def tile_rows(n):
            return P if n < NT else NB

        def turn_x(pe, src, r):
            for k in range(KD):
                mm = pe.transpose(psum[:, 4 + k // 4, (k % 4) * P:(k % 4) * P + r], src[:, k * P:(k + 1) * P],
                                  ident[0:r, 0:r])
            mm.then_inc(xT_done, 1)

        def query_head(pe, h, r):
            for k in range(KD):
                mm = pe.matmul(psum[:, 6 + h // 4, (h % 4) * P:(h % 4) * P + r], wq[:, k, h * P:(h + 1) * P],
                               xbT[:, k, 0:r], start=(k == 0), stop=(k == KD - 1))
            if h == HEADS - 1:
                mm.then_inc(pq_done, 1)

        def score_keys(pe, r):
            for h in range(HEADS):
                mm = pe.matmul(psum[0:r, 4 + h // 2, (h % 2) * 256:(h % 2) * 256 + 256], pqT[:, h, 0:r],
                               keys[:, h, :], start=True, stop=True)
            mm.then_inc(sc_done, 1)

        def copy_xT(act, r):
            act.activation(xbT[:, :, 0:r], psum[:, 4:6, :].rearrange("p b (k n) -> p (b k) n", n=P)[:, :, 0:r],
                           ACT.Copy).then_inc(xT_copied, 1)

        def copy_q(act, r):
            act.activation(pqT[:, :, 0:r], psum[:, 6:8, :].rearrange("p b (k n) -> p (b k) n", n=P)[:, :, 0:r],
                           ACT.Copy).then_inc(pq_copied, 1)

        def copy_scores(act, dst, r):
            act.activation(dst[0:r].rearrange("p (b h) n -> p b (h n)", b=4), psum[0:r, 4:8, :], ACT.Copy)\
               .then_inc(sc_copied, 1)

        scur_heads = scur.rearrange("p h c n -> p h (c n)")

        def select_head_keys(link, p, s2, svh, sih):
            dve = nc.vector
            for c in range(2):
                link(dve.max(svh[:, c, 0:8], s2[:, c, :]))
                link(dve.max_index(sih[:, c, 0:8], svh[:, c, 0:8], s2[:, c, :]))
                link(dve.match_replace(stmp[0:p, c, :], svh[:, c, 0:8], s2[:, c, :], LOW))
                link(dve.max(svh[:, c, 8:16], stmp[0:p, c, :]))
                link(dve.max_index(sih[:, c, 8:16], svh[:, c, 8:16], stmp[0:p, c, :]))

        def select_head_ids(link, p, svh, sih, sfh, bh, cih, ijh, ijfh, pk, idh):
            dve = nc.vector
            cd, c2 = cand[0:p], cand2[0:p]
            link(dve.tensor_tensor(cd, svh[:, 0, :].unsqueeze(2).broadcast_to([p, TOPK, TOPK]),
                                   svh[:, 1, :].unsqueeze(1).broadcast_to([p, TOPK, TOPK]), ALU.add))
            cf, cf2 = cd.rearrange("p i j -> p (i j)"), c2.rearrange("p i j -> p (i j)")
            link(dve.max(bh[:, 0:8], cf))
            link(dve.max_index(cih[:, 0:8], bh[:, 0:8], cf))
            link(dve.match_replace(cf2, bh[:, 0:8], cf, LOW))
            link(dve.max(bh[:, 8:16], cf2))
            link(dve.max_index(cih[:, 8:16], bh[:, 8:16], cf2))
            link(dve.tensor_scalar(ijh[:, 0, :], cih, 4, None, ALU.logical_shift_right))
            link(dve.tensor_scalar(ijh[:, 1, :], cih, 15, None, ALU.bitwise_and))
            link(dve.tensor_copy(ijfh, ijh))
            link(dve.tensor_copy(sfh, sih))
            o1, o2 = oneh[0:p], oneh2[0:p]
            full = [p, 2, TOPK, TOPK]
            link(dve.tensor_tensor(o1, iota16[0:p].unsqueeze(1).unsqueeze(1).broadcast_to(full),
                                   ijfh.unsqueeze(3).broadcast_to(full), ALU.is_equal))
            link(dve.tensor_tensor(o2, o1, sfh.unsqueeze(2).broadcast_to(full), ALU.mult))
            link(dve.tensor_reduce(pk, o2, AX.X, ALU.add))
            link(dve.scalar_tensor_tensor(out=idh, in0=pk[:, 0, :], scalar=float(NKEYS), in1=pk[:, 1, :],
                                          op0=ALU.mult, op1=ALU.add))

        def linker(dve, first):
            k = [0]

            def link(ins):
                k[0] += 1
                ins.then_inc(sel, 1)
                wait_loop(dve, sel, first + k[0])

            return link

        gate_full = [P, HEADS, TOPK]

        def block_keys(link, h):
            select_head_keys(link, P, scur[:, h], sv[:, h], si[:, h])

        def block_ids(link, h):
            select_head_ids(link, P, sv[:, h], si[:, h], sif[:, h], best[:, h], ci[:, h], ij[:, h], ijf[:, h],
                            pick[:, h], idN[:, h * TOPK:(h + 1) * TOPK])

        def gates_shift(link):
            link(nc.vector.tensor_tensor(gateN, best, best[:, :, 0:1].broadcast_to(gate_full), ALU.subtract))

        def gates_norm(link):
            link(nc.vector.tensor_reduce(hsum, gateN, AX.X, ALU.add))
            link(nc.vector.reciprocal(hrec, hsum))
            link(nc.vector.tensor_tensor(gateN, gateN, hrec.unsqueeze(2).broadcast_to(gate_full), ALU.mult))

        HALF = SLOTS // 2

        with nc.Block() as block:
            @block.sync
            def _(sp):
                for i, (k0, k1) in enumerate(WO_SLICES):
                    sp.dma_start(wo[:, k0:k1, :], w_o[:, k0:k1, :]).then_inc(parts_here[i], 16)
                sp.dma_start(g2b, bass.AP(tensor=g2.tensor, offset=g2.offset, ap=[[0, P], [1, D]])).then_inc(g2_here, 16)
                for n in range(NT + 1):
                    if n >= 2 and n < NT:
                        sp.wait_ge(x1_out[n % 2], 16 * (n // 2))
                        sp.wait_ge(xb_done, n - 1)
                    if n < NT:
                        sp.dma_start(xin[:, n % 2, :], x_prompt[n * P:(n + 1) * P, :]).then_inc(x_here[n % 2], 16)
                    else:
                        sp.dma_start(x1s[0:NB, :], x_sample).then_inc(x_here[0], 16)
                    if n == 0:
                        sp.dma_start(wq, w_q).then_inc(wq_here, 16)
                        sp.wait_ge(key_zero, 1)
                        sp.dma_start(keys[0:64, :, 0:NKEYS], keysT[0:64]).then_inc(wq_here, 16)
                        sp.dma_start(keys[64:128, :, NKEYS:2 * NKEYS], keysT[64:128]).then_inc(wq_here, 16)
                    if 1 <= n:
                        sp.wait_ge(x1_done, n)
                        sp.dma_start(scratch_x1[(n - 1) * P:n * P, :], xin[:, (n - 1) % 2, :])\
                          .then_inc(x1_out[(n - 1) % 2], 16)
                sp.wait_ge(x1_done, NT + 1)
                sp.dma_start(scratch_x1[SEQ:T, :], x1s[0:NB, :]).then_inc(x1_out[0], 16)
                sp.wait_ge(xb_done, NT + 1)
                sp.dma_start(scratch_xb, xbs[0:NB, :]).then_inc(smp_out, 16)
                sp.wait_ge(smp_out, 16)
                sp.wait_ge(x1_out[0], 16 * 5)
                sp.wait_ge(x1_out[1], 16 * 4)

            @block.gpsimd
            def _(pool):
                pool.memset(keys, 0.0).then_inc(key_zero, 1)
                pool.wait_ge(sel, 24 * HEADS // 2)
                pool.tensor_copy(idD[:, :HALF], idN[:, :HALF]).then_inc(ids_ready, 1)
                pool.wait_ge(ids_ready, 1)
                for j in range(HALF):
                    if j < DRING:
                        pool.wait_ge(o_mm, j + 1)
                    else:
                        pool.wait_ge(dot_done, j - DRING + 1)
                    pool.indirect_dma_start(rowD[:, j % DRING, :], None, w_down,
                                            bass.IndirectOffsetOnAxis(ap=idD[:, j:j + 1], axis=0))\
                        .then_inc(gD[j % DRING], 16)
                pool.wait_ge(sel, 24 * HEADS)
                pool.tensor_copy(idD[:, HALF:], idN[:, HALF:]).then_inc(ids_ready, 1)

            @block.tensor
            def _(pe):
                for n in range(NT + 1):
                    r = tile_rows(n)
                    if n >= 2:
                        pe.wait_ge(x1_done, n - 1)
                    for k in range(KD):
                        if n == 0:
                            for i, (k0, _) in enumerate(WO_SLICES):
                                if k == k0:
                                    pe.wait_ge(parts_here[i], 32)
                        for h in range(2):
                            mm = pe.matmul(psum[0:r, 2 * (n % 2) + h, :],
                                           mergedT[:, n, k, :] if n < NT else mergedS[:, k, :],
                                           wo[:, k, h * 512:(h + 1) * 512], start=(k == 0), stop=(k == KD - 1))
                    mm.then_inc(o_mm, 1)
                    if n == 0:
                        pe.wait_ge(xb_done, 1)
                        turn_x(pe, xb[:, 0, :], P)
                        pe.wait_ge(wq_here, 48)
                        pe.wait_ge(xT_copied, 1)
                        for h in range(HEADS):
                            query_head(pe, h, P)
                        pe.wait_ge(pq_copied, 1)
                        score_keys(pe, P)
                pe.wait_ge(xb_done, 2)
                pe.wait_ge(sc_copied, 1)
                turn_x(pe, xb[:, 1, :], P)
                pe.wait_ge(xT_copied, 2)
                for h in range(HEADS):
                    query_head(pe, h, P)
                pe.wait_ge(pq_copied, 2)
                score_keys(pe, P)

            @block.vector
            def _(dve):
                link = linker(dve, 0)

                def residual_and_norm(n):
                    r = tile_rows(n)
                    x1 = xin[:, n % 2, :] if n < NT else x1s[0:NB, :]
                    dst = xb[:, n, :] if n < NT else xbs[0:NB, :]
                    dve.wait_ge(o_mm, n + 1)
                    dve.wait_ge(x_here[n % 2], 16 * (n // 2 + 1))
                    dve.tensor_tensor(x1.rearrange("p (h n) -> p h n", h=2), x1.rearrange("p (h n) -> p h n", h=2),
                                      psum[0:r, 2 * (n % 2):2 * (n % 2) + 2, :], ALU.add).then_inc(x1_done, 1)
                    dve.wait_ge(x1_std, n + 1)
                    dve.reciprocal(st2[0:r, n:n + 1], st2[0:r, n:n + 1]).then_inc(x1_rec, 1)
                    dve.wait_ge(x1_rec, n + 1)
                    dve.scalar_tensor_tensor(out=dst, in0=x1, scalar=st2[0:r, n:n + 1], in1=g2b[0:r, :],
                                             op0=ALU.mult, op1=ALU.mult).then_inc(xb_done, 1)

                def dots_of_block_0(first, last):
                    for j in range(first, last):
                        dve.wait_ge(gD[j % DRING], (j // DRING + 1) * 16)
                        dve.tensor_tensor_reduce(rowD[:, j % DRING, :], rowD[:, j % DRING, :], xcur, 1.0, 0.0,
                                                 ALU.mult, ALU.add, dots[:, j:j + 1]).then_inc(dot_done, 1)

                dve.wait_ge(g2_here, 16)
                residual_and_norm(0)
                dve.wait_ge(sc_copied, 1)
                for h in range(HEADS // 2):
                    block_keys(link, h)
                    block_ids(link, h)
                    if h:
                        residual_and_norm(h)
                dve.wait_ge(xcur_here, 1)
                done = [0, 3, 5, 7, 12, 20]
                for n in range(4, NT + 1):
                    residual_and_norm(n)
                    dots_of_block_0(done[n - 4], done[n - 3])
                    if n < HEADS:
                        block_keys(link, n)
                        block_ids(link, n)
                gates_shift(link)
                dots_of_block_0(done[-1], HALF)
                dve.wait_ge(sel_exp, 1)
                gates_norm(link)
                dve.tensor_copy(gateD, gateN.rearrange("p h k -> p (h k)")).then_inc(gates_moved, 1)

            @block.scalar
            def _(act):
                act.wait_ge(initialised, 5)
                for n in range(NT + 1):
                    r = tile_rows(n)
                    x1 = xin[:, n % 2, :] if n < NT else x1s[0:NB, :]
                    dst = xb[:, n, :] if n < NT else xbs[0:NB, :]
                    s_ = st2[0:r, n:n + 1]
                    act.wait_ge(x1_done, n + 1)
                    act.activation(dst, x1, ACT.Square, accum_out=s_).then_inc(x1_sq, 1)
                    act.wait_ge(x1_sq, n + 1)
                    act.activation(s_, s_, ACT.Sqrt, bias=eps[0:r], scale=1.0 / D).then_inc(x1_std, 1)
                    if n == 0:
                        act.wait_ge(xb_done, 1)
                        act.activation(xcur, xb[:, 0, :], ACT.Copy).then_inc(xcur_here, 1)
                        act.wait_ge(xT_done, 1)
                        copy_xT(act, P)
                        act.wait_ge(pq_done, 1)
                        copy_q(act, P)
                        act.wait_ge(sc_done, 1)
                        copy_scores(act, scur_heads, P)
                act.wait_ge(xT_done, 2)
                copy_xT(act, P)
                act.wait_ge(pq_done, 2)
                copy_q(act, P)
                act.wait_ge(sc_done, 2)
                act.wait_ge(sel, KEYS_READ)
                copy_scores(act, scur_heads, P)
                act.wait_ge(sel, SEL_OPS - 3)
                act.activation(gateN, gateN, ACT.Exp).then_inc(sel_exp, 1)

        G0 = MG + (DRING + URING) * D
        ssc = at(G0, 2, NKEYS)
        ids_s = at(G0 + 256, TOPK).bitcast(U32)
        gate_s = at(G0 + 272, TOPK)
        idcols = at(G0 + 288, NB).bitcast(U32)
        gatecols, dcols, ccols, gcols = (at(G0 + 296 + 8 * i, NB) for i in range(4))
        cmask = at(G0 + 328, NB, NB)
        ys = at(G0 + 1024, D)
        ysq = at(G0 + 2048, D)
        acc = at(G0 + 4096, D)
        x1keep = at(G0 + 3072, D)
        xbc = at(0, NB, D)
        scs = at(G0 + 1024, HEADS, 2 * NKEYS)

        ss_here = sem("sample_scores_here")
        xbc_here = sem("sample_x_here")
        sel2 = sem("sample_select_step")
        sx = sem("sample_select_exp")
        lists_out = sem("sample_lists_out")
        lists_in = sem("sample_lists_in")
        SAMPLE_DOWN = (NT * SLOTS // DRING + 1) * 16
        SAMPLE_UP = SAMPLE_DOWN + 16
        sdot = sem("sample_dots")
        sgel = sem("sample_gelu")
        scoef = sem("sample_coefficients")
        smask = sem("sample_mask")
        up_dve = sem("up_products_of_dve")
        sup = sem("sample_up")
        sy = sem("sample_y")
        sysq = sem("sample_y_squared")
        systd = sem("sample_y_std")

        AT_COEF2, AT_COEF1 = 8, 72
        AT_SUM, AT_SQUARES, AT_OUT = LAG + 1, LAG + 6, LAG + 12
        AT_KEYS = {16 + 10 * h: h for h in range(HEADS)}
        AT_IDS = {21 + 10 * h: h for h in range(HEADS)}
        AT_GATES, AT_GATES_NORM = 98, 112
        AT_UP2, AT_DOWN2, AT_UP1, AT_DOWN1 = 14, 24, LAG - 2, 96
        UPS = NT * SLOTS - LAG

        def has_up(it, j):
            if not isinstance(it, int):
                return True
            return j < LAG if it == NT else it >= 1 or j >= LAG

        def on_dve(it, j):
            return isinstance(it, int) and it == NT and j % URING == URING - 1

        def wait_row_used(eng, it, j):
            if isinstance(it, int) and it == NT and j >= URING:
                if on_dve(it, j):
                    eng.wait_ge(up_dve, j // URING)
                else:
                    eng.wait_ge(up_done, UPS + (j // URING - 1) * (URING - 1) + j % URING + 1)
            else:
                wait_loop(eng, up_done, (it - 1) * SLOTS + (j + SLOTS - LAG - URING + 1))

        def begun(it, j):
            return isinstance(it, int) and it == 0 and j < HALF

        with nc.Block() as block:
            def steps(body, eng):
                for it in range(3):
                    body(it)
                with eng.Fori(3, NT - 1) as it:
                    body(it)
                body(NT - 1)
                body(NT)

            def kind(it):
                if not isinstance(it, int):
                    return True, True, True, None, True
                return it < NT, it >= 1, it + 1 < NT, it + 2 <= NT, 1 <= it < NT

            @block.gpsimd
            def _(pool):
                def step(it):
                    down, before, select, _, _ = kind(it)
                    last = isinstance(it, int) and it == NT
                    for j in range(LAG if last else SLOTS):
                        if j == AT_UP2 and before:
                            wait_loop(pool, up_done, (it - 1) * SLOTS)
                            pool.tensor_copy(idU[:, HALF:], idD[:, HALF:]).then_inc(ids_ready, 1)
                            wait_loop(pool, ids_ready, it * 4 + (0 if last else 1))
                        if j == AT_DOWN2 and before and down:
                            wait_loop(pool, dot_done, it * SLOTS)
                            wait_loop(pool, sel, (it + 1) * SEL_OPS)
                            pool.tensor_copy(idD[:, HALF:], idN[:, HALF:]).then_inc(ids_ready, 1)
                            wait_loop(pool, ids_ready, it * 4 + 2)
                        if j == AT_UP1 and down:
                            if before:
                                wait_loop(pool, up_done, (it - 1) * SLOTS + HALF)
                            pool.tensor_copy(idU[:, :HALF], idD[:, :HALF]).then_inc(ids_ready, 1)
                            wait_loop(pool, ids_ready, it * 4 + 3)
                        if j == AT_DOWN1 and select:
                            wait_loop(pool, dot_done, it * SLOTS + HALF)
                            wait_loop(pool, sel, (it + 1) * SEL_OPS + 24 * HEADS // 2)
                            pool.tensor_copy(idD[:, :HALF], idN[:, :HALF]).then_inc(ids_ready, 1)
                            wait_loop(pool, ids_ready, it * 4 + 4)
                        if has_up(it, j):
                            wait_row_used(pool, it, j)
                            u = (j - LAG) % SLOTS
                            pool.indirect_dma_start(rowU[:, j % URING, :], None, w_up,
                                                    bass.IndirectOffsetOnAxis(ap=idU[:, u:u + 1], axis=0))\
                                .then_inc(gU[j % URING], 16)
                        if down and not begun(it, j):
                            wait_loop(pool, dot_done, it * SLOTS + j - DRING + 1)
                            pool.indirect_dma_start(rowD[:, j % DRING, :], None, w_down,
                                                    bass.IndirectOffsetOnAxis(ap=idD[:, j:j + 1], axis=0))\
                                .then_inc(gD[j % DRING], 16)
                        if last and 8 <= j < 8 + NB:
                            b = j - 8
                            if b == 0:
                                pool.wait_ge(lists_in, 32)
                            pool.indirect_dma_start(rowD[:, b, :], None, w_down,
                                                    bass.IndirectOffsetOnAxis(ap=idcols[:, b:b + 1], axis=0))\
                                .then_inc(gD[b], 16)
                        if last and 36 <= j < 36 + NB:
                            b = j - 36
                            pool.wait_ge(sdot, b + 1)
                            pool.indirect_dma_start(rowD[:, b, :], None, w_up,
                                                    bass.IndirectOffsetOnAxis(ap=idcols[:, b:b + 1], axis=0))\
                                .then_inc(gD[b], 16)

                pool.memset(cmask, 0.0).then_inc(smask, 1)
                pool.wait_ge(ids_ready, 2)
                steps(step, pool)

            @block.vector
            def _(dve):
                def sum_up(n, products):
                    wait_loop(dve, up_done, products)
                    wait_loop(dve, x1_here, n * 16)
                    wait_loop(dve, y_out, (n - 1) * 16)
                    dve.tensor_tensor(ybuf.rearrange("p (h n) -> p h n", h=2),
                                      x1cur.rearrange("p (h n) -> p h n", h=2), psum[:, 0:2, :], ALU.add)\
                       .then_inc(y_sum, 1)

                def norm_out(n):
                    wait_loop(dve, y_std, n)
                    dve.reciprocal(mrec, msq).then_inc(y_rec, 1)
                    wait_loop(dve, y_rec, n)
                    dve.scalar_tensor_tensor(out=ybuf, in0=ybuf, scalar=mrec, in1=gfb, op0=ALU.mult,
                                             op1=ALU.mult).then_inc(y_ready, 1)

                def second_half(it):
                    wait_loop(dve, gelu2, it)
                    dve.tensor_tensor(coef[:, HALF:], gel[:, HALF:], gateD[:, HALF:], ALU.mult).then_inc(coef2, 1)
                    wait_loop(dve, coef2, it)
                    if kind(it)[0]:
                        dve.tensor_copy(gateD, gateN.rearrange("p h k -> p (h k)")).then_inc(gates_moved, 1)

                def step(it):
                    down, up, select, _, write = kind(it)
                    link = linker(dve, (it + 1) * SEL_OPS) if select else None
                    samples_chosen = isinstance(it, int) and it + 1 == NT
                    at_keys, at_ids, at_gates, at_gates_norm = AT_KEYS, AT_IDS, AT_GATES, AT_GATES_NORM
                    if isinstance(it, int) and it == 0:
                        at_keys = {HALF + 7 * h: h for h in range(HEADS)}
                        at_ids = {HALF + 7 * h + 3: h for h in range(HEADS)}
                        at_gates, at_gates_norm = 118, 126
                    if not down:
                        return
                    for j in range(SLOTS):
                        if j == AT_SUM and write:
                            sum_up(it, it * SLOTS)
                        if j == AT_COEF2 and up:
                            second_half(it)
                        if j == AT_OUT and write:
                            norm_out(it)
                        if select and j in at_keys:
                            if at_keys[j] == 0:
                                wait_loop(dve, sc_copied, it + 2)
                            block_keys(link, at_keys[j])
                        if select and j in at_ids:
                            if at_ids[j] == 0 and up:
                                wait_loop(dve, ids_ready, it * 4)
                            if at_ids[j] == HEADS // 2:
                                wait_loop(dve, ids_ready, it * 4 + 2)
                            block_ids(link, at_ids[j])
                        if j == AT_COEF1:
                            wait_loop(dve, gelu1, it + 1)
                            wait_loop(dve, gates_moved, it + 1)
                            dve.tensor_tensor(coef[:, :HALF], gel[:, :HALF], gateD[:, :HALF], ALU.mult)\
                               .then_inc(coef1, 1)
                        if select and j == at_gates:
                            gates_shift(link)
                        if select and j == at_gates_norm:
                            wait_loop(dve, sel_exp, it + 2)
                            gates_norm(link)
                        if samples_chosen and j == 40:
                            dve.wait_ge(ss_here, 32)
                            select_head_keys(link2, R2, ssc[0:R2], sv[0:R2, 0], si[0:R2, 0])
                        if samples_chosen and j == 50:
                            select_head_ids(link2, R2, sv[0:R2, 0], si[0:R2, 0], sif[0:R2, 0], best[0:R2, 0],
                                            ci[0:R2, 0], ij[0:R2, 0], ijf[0:R2, 0], pick[0:R2, 0], ids_s[0:R2])
                            link2(dve.tensor_scalar(gg, best[0:R2, 0, :], best[0:R2, 0, 0:1], None, ALU.subtract))
                        if samples_chosen and j == 96:
                            dve.wait_ge(sx, 1)
                            link2(dve.tensor_reduce(hsum[0:R2, 0:1], gg, AX.X, ALU.add))
                            link2(dve.reciprocal(hrec[0:R2, 0:1], hsum[0:R2, 0:1]))
                            link2(dve.tensor_scalar(gg, gg, hrec[0:R2, 0:1], None, ALU.mult))
                        if begun(it, j):
                            continue
                        if j == 0:
                            wait_loop(dve, xcur_here, it + 1)
                        wait_loop(dve, gD[j % DRING], (it * (SLOTS // DRING) + j // DRING + 1) * 16)
                        dve.tensor_tensor_reduce(rowD[:, j % DRING, :], rowD[:, j % DRING, :], xcur, 1.0, 0.0,
                                                 ALU.mult, ALU.add, dots[:, j:j + 1]).then_inc(dot_done, 1)

                k = [0]

                def link2(ins):
                    k[0] += 1
                    ins.then_inc(sel2, 1)
                    dve.wait_ge(sel2, k[0])

                gg = gate_s[0:R2]
                dve.wait_ge(gf_here, 16)
                dve.wait_ge(gates_moved, 1)
                steps(step, dve)
                second_half(NT)
                for j in range(URING - 1, LAG, URING):
                    q = j // URING
                    dve.wait_ge(gU[URING - 1], (UPS // URING + q + 1) * 16)
                    row, u = rowU[:, URING - 1, :], j + SLOTS - LAG
                    if q == 0:
                        dve.tensor_scalar(acc, row, coef[:, u:u + 1], None, ALU.mult).then_inc(up_dve, 1)
                    else:
                        dve.wait_ge(up_dve, q)
                        dve.scalar_tensor_tensor(out=acc, in0=row, scalar=coef[:, u:u + 1], in1=acc, op0=ALU.mult,
                                                 op1=ALU.add).then_inc(up_dve, 1)
                    if q == 4:
                        dve.wait_ge(xbc_here, 16 * NB)
                    if 4 <= q < 8:
                        for b in (2 * q - 8, 2 * q - 7):
                            dve.wait_ge(gD[b], SAMPLE_DOWN)
                            dve.tensor_tensor_reduce(rowD[:, b, :], rowD[:, b, :], xbc[:, b, :], 1.0, 0.0, ALU.mult,
                                                     ALU.add, dcols[:, b:b + 1]).then_inc(sdot, 1)
                    if q == 12:
                        dve.wait_ge(sgel, 1)
                        dve.wait_ge(lists_in, 32)
                        dve.tensor_tensor(ccols, gcols, gatecols, ALU.mult).then_inc(scoef, 1)
                        dve.wait_ge(scoef, 1)
                        dve.wait_ge(smask, 1)
                        for b in range(NB):
                            dve.tensor_copy(cmask[:, b, b:b + 1], ccols[:, b:b + 1]).then_inc(smask, 1)
                    if q == 18:
                        dve.wait_ge(sup, NB)
                        dve.tensor_tensor(ys[0:NB].rearrange("p (h n) -> p h n", h=2),
                                          x1keep[0:NB].rearrange("p (h n) -> p h n", h=2), psum[0:NB, 2:4, :],
                                          ALU.add).then_inc(sy, 1)
                    if q == 19:
                        dve.wait_ge(systd, 1)
                        dve.reciprocal(mrec[0:NB, ], msq[0:NB]).then_inc(sy, 1)
                        dve.wait_ge(sy, 2)
                        dve.scalar_tensor_tensor(out=ys[0:NB], in0=ys[0:NB], scalar=mrec[0:NB], in1=gfb[0:NB],
                                                 op0=ALU.mult, op1=ALU.mult).then_inc(sy, 1)
                dve.wait_ge(sy, 3)
                dve.wait_ge(up_dve, LAG // URING)
                dve.wait_ge(x1_here, NT * 16)
                dve.tensor_tensor(x1cur, x1cur, acc, ALU.add).then_inc(up_dve, 1)
                dve.wait_ge(up_dve, LAG // URING + 1)
                sum_up(NT, NT * SLOTS - LAG // URING)
                norm_out(NT)

            @block.scalar
            def _(act):
                def squares(n):
                    wait_loop(act, y_sum, n)
                    act.activation(x1cur, ybuf, ACT.Square, accum_out=msq).then_inc(y_sq, 1)
                    wait_loop(act, y_sq, n)
                    act.activation(msq, msq, ACT.Sqrt, bias=eps, scale=1.0 / D).then_inc(y_std, 1)

                def step(it):
                    down, up, select, score, write = kind(it)
                    if score is None:
                        score = it_scores[0]
                    last = isinstance(it, int) and it == NT
                    samples = isinstance(it, int) and it + 2 == NT
                    samples_chosen = isinstance(it, int) and it + 1 == NT
                    r = NB if samples else P
                    first = isinstance(it, int) and it == 0
                    for j in range(LAG if last else SLOTS):
                        if j == 2 and score and not samples:
                            act.activation(xnext, xb[:, bass.ds(it + 2, 1), :].rearrange("p a d -> p (a d)"),
                                           ACT.Copy).then_inc(xnext_ready, 1)
                        if j == 4 and up:
                            wait_loop(act, dot_done, it * SLOTS)
                            wait_loop(act, coef2, it - 1)
                            act.activation(gel[:, HALF:], dots[:, HALF:], ACT.Gelu).then_inc(gelu2, 1)
                        if j == AT_SQUARES and write:
                            squares(it)
                        if j == 14 and score:
                            wait_loop(act, xT_done, it + 3)
                            copy_xT(act, r)
                        if j == 56 and score:
                            wait_loop(act, pq_done, it + 3)
                            copy_q(act, r)
                        if j == AT_COEF1 - 4 and down:
                            wait_loop(act, dot_done, it * SLOTS + HALF)
                            if up:
                                wait_loop(act, coef1, it)
                            act.activation(gel[:, :HALF], dots[:, :HALF], ACT.Gelu).then_inc(gelu1, 1)
                        if j == (116 if first else 94) and score:
                            wait_loop(act, sc_done, it + 3)
                            wait_loop(act, sel, (it + 1) * SEL_OPS + KEYS_READ)
                            copy_scores(act, scs if samples else scur_heads, r)
                        if j == (124 if first else 106) and select:
                            wait_loop(act, sel, (it + 2) * SEL_OPS - 3)
                            act.activation(gateN, gateN, ACT.Exp).then_inc(sel_exp, 1)
                        if samples_chosen and j == 86:
                            act.wait_ge(sel2, 25)
                            act.activation(gate_s[0:R2], gate_s[0:R2], ACT.Exp).then_inc(sx, 1)
                        if last and j == 40:
                            act.wait_ge(sdot, NB)
                            act.activation(gcols, dcols, ACT.Gelu).then_inc(sgel, 1)
                        if last and j == LAG - 3:
                            act.wait_ge(sy, 1)
                            act.activation(ysq[0:NB], ys[0:NB], ACT.Square, accum_out=msq[0:NB]).then_inc(sysq, 1)
                            act.wait_ge(sysq, 1)
                            act.activation(msq[0:NB], msq[0:NB], ACT.Sqrt, bias=eps[0:NB], scale=1.0 / D)\
                               .then_inc(systd, 1)
                        if has_up(it, j):
                            u = (j - LAG) % SLOTS
                            if u == 0:
                                wait_loop(act, coef1, it + 1)
                            if u == HALF:
                                wait_loop(act, coef2, it)
                            if on_dve(it, j):
                                continue
                            wait_row_used(act, it, j)
                            act.activation(diag[:, j % 4, :], ident, ACT.Copy, scale=coef[:, u:u + 1])\
                               .then_inc(diag_ready, 1)
                    if select:
                        wait_loop(act, dot_done, (it + 1) * SLOTS)
                        act.activation(xcur, xb[:, bass.ds(it + 1, 1), :].rearrange("p a d -> p (a d)"),
                                       ACT.Copy).then_inc(xcur_here, 1)

                it_scores = [True]
                for it in range(3):
                    step(it)
                with act.Fori(3, NT - 2) as it:
                    step(it)
                for it in range(NT - 2, NT + 1):
                    step(it)
                act.wait_ge(sy, 2)
                squares(NT)

            @block.tensor
            def _(pe):
                def step(it):
                    down, up, _, score, _ = kind(it)
                    if score is None:
                        score = True
                    last = isinstance(it, int) and it == NT
                    samples = isinstance(it, int) and it + 2 == NT
                    r = NB if samples else P
                    for j in range(LAG if last else SLOTS):
                        if score and j == 8:
                            if not samples:
                                wait_loop(pe, xnext_ready, it + 1)
                            wait_loop(pe, sc_copied, it + 2)
                            turn_x(pe, xbs[0:NB, :] if samples else xnext, r)
                        if score and 18 <= j < 50 and j % 4 == 2:
                            if j == 18:
                                wait_loop(pe, xT_copied, it + 3)
                            query_head(pe, (j - 18) // 4, r)
                        if score and j == 62:
                            wait_loop(pe, pq_copied, it + 3)
                            score_keys(pe, r)
                        if last and 56 <= j < 56 + 2 * NB and j % 2 == 0:
                            b = (j - 56) // 2
                            if b == 0:
                                pe.wait_ge(smask, NB + 1)
                            pe.wait_ge(gD[b], SAMPLE_UP)
                            for h in range(2):
                                mm = pe.matmul(psum[0:NB, 2 + h, :], cmask[:, b, :],
                                               rowD[:, b, h * 512:(h + 1) * 512], start=(b == 0), stop=(b == NB - 1))
                            mm.then_inc(sup, 1)
                        if has_up(it, j) and not on_dve(it, j):
                            u = (j - LAG) % SLOTS
                            if u == 0:
                                wait_loop(pe, y_sum, it)
                            wait_loop(pe, gU[j % URING], (it * (SLOTS // URING) + (j - LAG) // URING + 1) * 16)
                            if last:
                                pe.wait_ge(diag_ready, UPS + j // URING * (URING - 1) + j % URING + 1)
                            else:
                                wait_loop(pe, diag_ready, it * SLOTS + (j - LAG) + 1)
                            for h in range(2):
                                mm = pe.matmul(psum[:, h, :], diag[:, j % 4, :],
                                               rowU[:, j % URING, h * 512:(h + 1) * 512],
                                               start=(u == 0), stop=(u == (SLOTS - 2 if last else SLOTS - 1)))
                            mm.then_inc(up_done, 1)

                for it in range(3):
                    step(it)
                with pe.Fori(3, NT - 2) as it:
                    step(it)
                for it in range(NT - 2, NT + 1):
                    step(it)

            @block.sync
            def _(sp):
                def fetch_x1(n):
                    wait_loop(sp, y_std, n - 1)
                    sp.dma_start(x1cur, scratch_x1[bass.ds((n - 1) * P, P), :]).then_inc(x1_here, 16)

                def write_block(n):
                    wait_loop(sp, y_ready, n)
                    sp.dma_start(y_prompt[bass.ds((n - 1) * P, P), :], ybuf).then_inc(y_out, 16)

                def step(n):
                    fetch_x1(n)
                    write_block(n)

                sp.dma_start(gfb, bass.AP(tensor=gf.tensor, offset=gf.offset, ap=[[0, P], [1, D]])).then_inc(gf_here, 16)
                sp.dma_start(x1keep[0:NB], scratch_x1[SEQ:T, :]).then_inc(ss_here, 16)
                for n in (1, 2):
                    step(n)
                with sp.Fori(3, NT - 1) as n:
                    step(n)
                fetch_x1(NT - 1)
                sp.wait_ge(sc_copied, NT + 1)
                sp.dma_start(scratch_sc.rearrange("(b h) n -> b (h n)", h=HEADS),
                             scs[0:NB].rearrange("p h n -> p (h n)")).then_inc(smp_out, 16)
                sp.wait_ge(smp_out, 32)
                sp.dma_start(ssc[0:R2], scratch_sc.rearrange("r (c n) -> r c n", c=2)).then_inc(ss_here, 16)
                write_block(NT - 1)
                fetch_x1(NT)
                sp.wait_ge(sel2, 24 + 4)
                sp.dma_start(scratch_ids.rearrange("b (h k) -> (b h) k", h=HEADS), ids_s[0:R2]).then_inc(lists_out, 16)
                sp.dma_start(scratch_gate.rearrange("b (h k) -> (b h) k", h=HEADS), gate_s[0:R2])\
                  .then_inc(lists_out, 16)
                sp.wait_ge(lists_out, 32)
                with nc.allow_non_contiguous_dma("a list of 1024 words, turned"):
                    sp.dma_start(idcols, scratch_ids.rearrange("b s -> s b")).then_inc(lists_in, 16)
                    sp.dma_start(gatecols, scratch_gate.rearrange("b s -> s b")).then_inc(lists_in, 16)
                sp.wait_ge(dot_done, NT * SLOTS)
                for b in range(NB):
                    sp.dma_start(xbc[:, b, :], bass.AP(tensor=scratch_xb.tensor, offset=b * D, ap=[[0, P], [1, D]]))\
                      .then_inc(xbc_here, 16)
                sp.wait_ge(sy, 3)
                store(sp, y_sample, ys[0:NB, :])
                write_block(NT)
                sp.wait_ge(y_out, 16 * NT)

        with nc.Block() as block:
            @block.sync
            def _(sp):
                sp.wait_ge(stores, n_stores[0])


_NAMES = ["x_prompt", "x_sample", "xT", "memT", "w_chunks", "w_gates", "w_o", "w_q", "keysT", "bias_tab", "onehot",
          "sinks_bc", "sinks_s", "g1", "gm", "g2", "gf", "conv_w", "conv_b", "ln_g", "ln_b", "cacheT", "cache_conv",
          "cache_k", "cache_v", "cache_kT", "memkT", "cache_mv", "w_down", "w_up"]
_OUTS = [((SEQ, D), (1, SEQ, D)), ((NB, D), (NB, 1, D)), ((HALO, CH), (1, 1, HALO, CH)),
         ((WIN, P), (1, 1, WIN, 2, HD)), ((WIN, P), (1, 1, WIN, 2, HD)),
         ((MEM, CH), (1, 1, MEM, 4, P)), ((MEM, CH), (1, 1, MEM, 4, P)),
         ((NB, HALO, CH), (1, NB, HALO, CH)), ((NB, WIN, P), (1, NB, WIN, 2, HD)), ((NB, WIN, P), (1, NB, WIN, 2, HD))]


def bucket_rows():
    oh = np.zeros((33, LINE - 1), np.float32)
    for r in range(LINE - 1):
        dist = 2 * P - 1 - r
        if dist < 0 or dist > WIN:
            oh[32, r] = 1
        elif dist < 16:
            oh[dist, r] = 1
        else:
            oh[min(31, 16 + int(math.log(dist / 16) / math.log(128 / 16) * 16)), r] = 1
    return oh


def lay_out(x_prompt, x_sample, cache_conv, cache_swa_k, cache_swa_v, cache_mem_k, cache_mem_v, mem_prompt,
            rel_bias_table, norm1_g, w_in, conv_dw_w, conv_dw_b, conv_ln_g, conv_ln_b, w_conv_out, swa_sinks,
            w_swa_out, mem_norm_g, w_mem_kv, w_mem_out, w_out, norm2_g, peer_w_q, peer_keys, peer_w_down,
            peer_w_up, final_norm_g):
    xp, xs = x_prompt[0], x_sample[:, 0]

    def slices(w):
        return w.reshape(-1, P, w.shape[1]).transpose(1, 0, 2)

    w = w_in[0]
    q_cols = [np.r_[c * HD:(c + 1) * HD, (c + 4) * HD:(c + 5) * HD] for c in range(4)]
    q0, k0 = 2 * CH, 2 * CH + 512
    v0, m0, gate0 = k0 + P, k0 + 2 * P, k0 + 2 * P + 512
    start = {"a": 0, "b": CH, "k": k0, "v": v0, "qm": m0}
    chunks = []
    for kind, c in CHUNKS:
        if kind == "q":
            part = w[:, q0 + q_cols[c]]
        elif kind == "mem":
            part = w_mem_kv[0][:, c * P:(c + 1) * P]
        else:
            part = w[:, start[kind] + c * P:start[kind] + (c + 1) * P]
        chunks.append(slices(part))
    outs = [w_conv_out[0], w_swa_out[0][np.concatenate(q_cols)], w_mem_out[0]]
    gates = []
    for m in range(KD):
        for br in range(3):
            g = slices(w[:, gate0 + br * D + m * P:gate0 + br * D + (m + 1) * P])
            gates.append(np.concatenate([g, slices(outs[br][:, m * P:(m + 1) * P])], axis=1))
    order = [2 * hf + cc + 4 * j for hf in range(2) for j in range(2) for cc in range(2)]
    sinks = swa_sinks[0]
    return {
        "x_prompt": xp, "x_sample": xs,
        "xT": slices(np.concatenate([xp, xs]).T), "memT": slices(mem_prompt[0].T),
        "w_chunks": np.stack(chunks), "w_gates": np.stack(gates),
        "w_o": slices(w_out[0]), "w_q": slices(peer_w_q[0]),
        "keysT": peer_keys[0].transpose(1, 3, 0, 2).reshape(P, HEADS, NKEYS),
        "bias_tab": rel_bias_table[:, order], "onehot": bucket_rows(),
        "sinks_bc": np.broadcast_to(sinks[order], (P, 8)),
        "sinks_s": np.repeat(sinks.reshape(2, 4).T, NB, axis=0),
        "g1": norm1_g[0].reshape(KD, P).T, "gm": mem_norm_g[0].reshape(KD, P).T,
        "g2": norm2_g[0], "gf": final_norm_g,
        "conv_w": conv_dw_w[0].reshape(TAPS, NC, P).transpose(2, 1, 0),
        "conv_b": conv_dw_b[0].reshape(NC, P).T, "ln_g": conv_ln_g[0].reshape(NC, P).T,
        "ln_b": conv_ln_b[0].reshape(NC, P).T,
        "cacheT": cache_conv[0].transpose(2, 0, 1).reshape(NC, P, NB, HALO).transpose(1, 0, 2, 3),
        "cache_conv": cache_conv[0], "cache_k": cache_swa_k[0].reshape(NB, WIN, P),
        "cache_v": cache_swa_v[0].reshape(NB, WIN, P),
        "cache_kT": cache_swa_k[0].reshape(NB, WIN, P).transpose(2, 0, 1),
        "memkT": cache_mem_k[0].transpose(0, 3, 2, 1), "cache_mv": cache_mem_v[0].reshape(NB, MEM, CH),
        "w_down": peer_w_down[0], "w_up": peer_w_up[0],
    }


def kernel(**inputs):
    import concourse.bacc as bacc
    from concourse.bass_utils import run_bass_kernel_spmd

    laid = lay_out(**{k: np.asarray(v) for k, v in inputs.items()})
    nc = bacc.Bacc("TRN2", target_bir_lowering=False, num_devices=1)
    arrays, args = {}, []
    for name in _NAMES:
        a = np.ascontiguousarray(laid[name])
        arrays[f"in_{name}"] = a
        args.append(nc.dram_tensor(f"in_{name}", a.shape, mybir.dt.from_np(a.dtype), kind="ExternalInput").ap())
    for i, (shape, _) in enumerate(_OUTS):
        args.append(nc.dram_tensor(f"out_{i}", shape, F32, kind="ExternalOutput").ap())
    build_kernel(nc, *args)
    r = run_bass_kernel_spmd(nc, [arrays], core_ids=[0])
    return tuple(r.results[0][f"out_{i}"].reshape(full) for i, (_, full) in enumerate(_OUTS))
```
